# Optimizing a Trainium2 kernel written in Bass

```python
import math
import jax
import jax.numpy as jnp
from jax import lax
import numpy as np

D_MODEL = 1024
BATCH = 1
SEQ = 256
DEPTH = 2
DEC_BATCH = 8
DEC_SEQ = 1
PAST_LEN = 256
PAGE_SIZE = 128

NSA_HEADS = 8
NSA_GROUPS = 2
NSA_HPG = NSA_HEADS // NSA_GROUPS
HEAD_DIM = 64
SCALE = HEAD_DIM ** -0.5
CMP_LEN = 32
CMP_STRIDE = 16
CMP_HID = 2 * HEAD_DIM
SEL_LEN = 64
N_SEL = 16
WINDOW = 512
Q_BLOCK = 128
GLA_HEADS = 4
GLA_DK = D_MODEL // 4 // GLA_HEADS
GLA_DV = D_MODEL // 2 // GLA_HEADS
GLA_RANK = 16
GLA_TAU = 16.0
GLA_CHUNK = 64
D_FF = 4 * D_MODEL
N_KV_SLOTS = 4
ROPE_THETA = 10000.0
EPS = 1e-5
BIG = 1e6
DN_ALPHA = (2.0 * DEPTH) ** 0.25
DN_BETA = (8.0 * DEPTH) ** -0.25

SPLIT_SIZES = (NSA_HEADS * HEAD_DIM, 6 * NSA_GROUPS * HEAD_DIM, 3 * NSA_HEADS,
               GLA_HEADS * GLA_DK, GLA_HEADS * GLA_DK, GLA_HEADS * GLA_DV,
               GLA_RANK, GLA_HEADS * GLA_DV, 2 * D_MODEL)
SPLIT_POINTS = tuple(int(v) for v in np.cumsum(SPLIT_SIZES)[:-1])
D_IN = sum(SPLIT_SIZES)

kernel_name = 'nsa_gla_parallel_deepnorm_decode_step'

def layer_norm(x, g, b):
    xf = x.astype(jnp.float32)
    mu = jnp.mean(xf, -1, keepdims=True)
    var = jnp.mean(jnp.square(xf - mu), -1, keepdims=True)
    return ((xf - mu) * lax.rsqrt(var + EPS)).astype(x.dtype) * g + b

def rms_norm(x, g):
    xf = x.astype(jnp.float32)
    return (xf * lax.rsqrt(jnp.mean(jnp.square(xf), -1, keepdims=True) + EPS)).astype(x.dtype) * g

def rope(x, pos):
    half = x.shape[-1] // 2
    inv = ROPE_THETA ** (-jnp.arange(half, dtype=jnp.float32) / half)
    ang = pos.astype(jnp.float32)[:, None] * inv[None, :]
    cos = jnp.cos(ang)[:, None, :].astype(x.dtype)
    sin = jnp.sin(ang)[:, None, :].astype(x.dtype)
    x1, x2 = x[..., :half], x[..., half:]
    return jnp.concatenate([x1 * cos - x2 * sin, x2 * cos + x1 * sin], axis=-1)

def masked_softmax(s, mask):
    s = jnp.where(mask, s.astype(jnp.float32), -jnp.inf)
    m = jnp.max(s, axis=-1, keepdims=True)
    p = jnp.exp(s - jnp.where(jnp.isfinite(m), m, 0.0))
    return p / jnp.maximum(jnp.sum(p, axis=-1, keepdims=True), 1e-30)

def compress_blocks(rows, pe, w1, w2):
    B, T, G, dh = rows.shape
    nc = (T - CMP_LEN) // CMP_STRIDE + 1
    idx = jnp.arange(nc)[:, None] * CMP_STRIDE + jnp.arange(CMP_LEN)[None, :]
    blk = rows[:, idx] + pe[None, None, :, None, :]
    blk = blk.transpose(0, 1, 3, 2, 4).reshape(B, nc, G, CMP_LEN * dh)
    return jax.nn.gelu(blk @ w1) @ w2

def nsa_compressed(q, k_cmp, v_cmp, qpos):
    nc = k_cmp.shape[1]
    s = jnp.einsum('btghd,bcgd->bghtc', q, k_cmp) * SCALE
    valid = (jnp.arange(nc) * CMP_STRIDE + CMP_LEN - 1)[None, :] <= qpos[:, None]
    p = masked_softmax(s, valid)
    o = jnp.einsum('bghtc,bcgd->btghd', p.astype(v_cmp.dtype), v_cmp)
    return o, p

def select_blocks(p_cmp, qpos, n_blocks):
    nc = p_cmp.shape[-1]
    r, w = SEL_LEN // CMP_STRIDE, CMP_LEN // CMP_STRIDE
    off = (jnp.arange(r)[:, None] + jnp.arange(w)[None, :]).reshape(-1)
    blk = jnp.arange(n_blocks)
    overlap = jnp.sum(jnp.arange(nc)[:, None, None] == (r * blk[None, :, None] + off[None, None, :]),
                      axis=-1).astype(jnp.float32)
    imp = jnp.einsum('bghtc,cj->bgtj', p_cmp, overlap)
    cur = qpos[:, None] // SEL_LEN
    causal = blk[None, :] * SEL_LEN <= qpos[:, None]
    forced = (blk[None, :] == 0) | (blk[None, :] == cur) | (blk[None, :] == cur - 1)
    score = jnp.where(forced, BIG, jnp.where(causal, imp, -jnp.inf))
    top, idx = lax.top_k(score, min(N_SEL, n_blocks))
    return idx, jnp.isfinite(top)

def nsa_selected(q, k_rows, v_rows, idx, ok, qpos):
    B, Tk = k_rows.shape[:2]
    n_blocks = -(-Tk // SEL_LEN)
    pad = ((0, 0), (0, n_blocks * SEL_LEN - Tk), (0, 0), (0, 0))
    kb = jnp.pad(k_rows, pad).reshape(B, n_blocks, SEL_LEN, NSA_GROUPS, HEAD_DIM).transpose(0, 3, 1, 2, 4)
    vb = jnp.pad(v_rows, pad).reshape(B, n_blocks, SEL_LEN, NSA_GROUPS, HEAD_DIM).transpose(0, 3, 1, 2, 4)
    Tq, n = q.shape[1], idx.shape[-1]
    qb = math.gcd(Tq, Q_BLOCK)
    nqb = Tq // qb
    qs = q.reshape(B, nqb, qb, NSA_GROUPS, NSA_HPG, HEAD_DIM).transpose(1, 0, 2, 3, 4, 5)
    idxs = idx.reshape(B, NSA_GROUPS, nqb, qb, n).transpose(2, 0, 1, 3, 4)
    oks = ok.reshape(B, NSA_GROUPS, nqb, qb, n).transpose(2, 0, 1, 3, 4)
    poss = qpos.reshape(nqb, qb)
    bi = jnp.arange(B)[:, None, None, None]
    gi = jnp.arange(NSA_GROUPS)[None, :, None, None]

    def one_block(args):
        qc, ic, okc, pc = args
        kg = kb[bi, gi, ic]
        vg = vb[bi, gi, ic]
        s = jnp.einsum('bqghd,bgqnld->bghqnl', qc, kg) * SCALE
        kpos = ic[..., None] * SEL_LEN + jnp.arange(SEL_LEN)
        mask = okc[..., None] & (kpos <= pc[None, None, :, None, None])
        p = masked_softmax(s.reshape(B, NSA_GROUPS, NSA_HPG, qb, n * SEL_LEN),
                           mask.reshape(B, NSA_GROUPS, 1, qb, n * SEL_LEN))
        return jnp.einsum('bghqm,bgqmd->bqghd', p.astype(vg.dtype),
                          vg.reshape(B, NSA_GROUPS, qb, n * SEL_LEN, HEAD_DIM))

    out = lax.map(one_block, (qs, idxs, oks, poss))
    return out.transpose(1, 0, 2, 3, 4, 5).reshape(B, Tq, NSA_GROUPS, NSA_HPG, HEAD_DIM)

def window_prompt(q, k, v):
    B, T = q.shape[:2]
    qb = math.gcd(T, Q_BLOCK)
    nqb = T // qb
    span = WINDOW + qb
    pad = ((0, 0), (WINDOW, 0), (0, 0), (0, 0))
    idx = jnp.arange(nqb)[:, None] * qb + jnp.arange(span)[None, :]
    k_band = jnp.pad(k, pad)[:, idx]
    v_band = jnp.pad(v, pad)[:, idx]
    qpos = jnp.arange(T).reshape(nqb, qb)
    kpos = idx - WINDOW
    d = qpos[:, :, None] - kpos[:, None, :]
    mask = (kpos[:, None, :] >= 0) & (d >= 0) & (d <= WINDOW)
    s = jnp.einsum('bnqghd,bnkgd->bghnqk',
                   q.reshape(B, nqb, qb, NSA_GROUPS, NSA_HPG, HEAD_DIM), k_band) * SCALE
    p = masked_softmax(s, mask)
    o = jnp.einsum('bghnqk,bnkgd->bnqghd', p.astype(v_band.dtype), v_band)
    return o.reshape(B, T, NSA_GROUPS, NSA_HPG, HEAD_DIM)

def window_decode(q, buf, k_new, v_new, qpos):
    wb = buf.shape[1]
    k = jnp.concatenate([buf[:, :, 0], k_new], axis=1)
    v = jnp.concatenate([buf[:, :, 1], v_new], axis=1)
    kpos = qpos[0] - wb + jnp.arange(wb + q.shape[1])
    d = qpos[:, None] - kpos[None, :]
    mask = (d >= 0) & (d <= WINDOW)
    s = jnp.einsum('btghd,bkgd->bghtk', q, k) * SCALE
    p = masked_softmax(s, mask)
    o = jnp.einsum('bghtk,bkgd->btghd', p.astype(v.dtype), v)
    return o, jnp.stack([k[:, -wb:], v[:, -wb:]], axis=2)

def gla_chunked(q, k, v, log_a, s0):
    B, T = q.shape[:2]
    C = math.gcd(T, GLA_CHUNK)
    nch = T // C

    def to_chunks(a):
        return a.reshape(B, nch, C, a.shape[2], a.shape[3]).transpose(1, 0, 3, 2, 4)

    tri = jnp.tril(jnp.ones((C, C), dtype=bool))

    def step(S, inp):
        qc, kc, vc, lc = inp
        b = jnp.cumsum(lc, axis=2)
        o_inter = jnp.einsum('bhtk,bhkv->bhtv', qc * jnp.exp(b).astype(qc.dtype), S)
        diff = jnp.where(tri[:, :, None], b[:, :, :, None, :] - b[:, :, None, :, :], -jnp.inf)
        A = jnp.einsum('bhtk,bhsk,bhtsk->bhts', qc, kc, jnp.exp(diff).astype(qc.dtype))
        o = o_inter + jnp.einsum('bhts,bhsv->bhtv', A, vc)
        b_last = b[:, :, -1, :]
        k_dec = kc * jnp.exp(b_last[:, :, None, :] - b).astype(kc.dtype)
        S_new = jnp.exp(b_last)[..., None].astype(S.dtype) * S + jnp.einsum('bhsk,bhsv->bhkv', k_dec, vc)
        return S_new.astype(S.dtype), o

    S, o = lax.scan(step, s0, (to_chunks(q), to_chunks(k), to_chunks(v), to_chunks(log_a)))
    return o.transpose(1, 0, 3, 2, 4).reshape(B, T, q.shape[2], v.shape[3]), S

def token_mixer(x, pos, past_kv, win_buf, gla_s0, p):
    B, T, _ = x.shape
    z = x @ p['w_in']
    q, kv6, nsa_g, gq, gk, gv, g_lr, g_r, mg = jnp.split(z, SPLIT_POINTS, axis=-1)
    q = q.reshape(B, T, NSA_HEADS, HEAD_DIM)
    kv6 = kv6.reshape(B, T, 6, NSA_GROUPS, HEAD_DIM)
    k_win = rope(kv6[:, :, 4], pos)
    v_win = kv6[:, :, 5]
    kv_rows = jnp.stack([kv6[:, :, 0], kv6[:, :, 1], rope(kv6[:, :, 2], pos), kv6[:, :, 3]], axis=2)
    full = kv_rows if past_kv is None else jnp.concatenate([past_kv, kv_rows], axis=1)
    k_cmp = compress_blocks(full[:, :, 0], p['cmp_k_pe'], p['cmp_k_w1'], p['cmp_k_w2'])
    v_cmp = compress_blocks(full[:, :, 1], p['cmp_v_pe'], p['cmp_v_w1'], p['cmp_v_w2'])
    q_plain = q.reshape(B, T, NSA_GROUPS, NSA_HPG, HEAD_DIM)
    q_rot = rope(q, pos).reshape(B, T, NSA_GROUPS, NSA_HPG, HEAD_DIM)
    o_cmp, p_cmp = nsa_compressed(q_plain, k_cmp, v_cmp, pos)
    n_blocks = -(-full.shape[1] // SEL_LEN)
    sel_idx, sel_ok = select_blocks(p_cmp, pos, n_blocks)
    o_sel = nsa_selected(q_rot, full[:, :, 2], full[:, :, 3], sel_idx, sel_ok, pos)
    if win_buf is None:
        o_win = window_prompt(q_rot, k_win, v_win)
        wb = min(WINDOW, T)
        win_new = jnp.stack([k_win[:, T - wb:], v_win[:, T - wb:]], axis=2)
    else:
        o_win, win_new = window_decode(q_rot, win_buf, k_win, v_win, pos)
    g = jax.nn.sigmoid(nsa_g.reshape(B, T, NSA_GROUPS, NSA_HPG, 3))
    o_nsa = g[..., 0:1] * o_cmp + g[..., 1:2] * o_sel + g[..., 2:3] * o_win
    gq = gq.reshape(B, T, GLA_HEADS, GLA_DK) * (GLA_DK ** -0.5)
    gk = gk.reshape(B, T, GLA_HEADS, GLA_DK)
    gv = gv.reshape(B, T, GLA_HEADS, GLA_DV)
    log_a = jax.nn.log_sigmoid((g_lr @ p['gla_w_a2'] + p['gla_b_a']).astype(jnp.float32)) / GLA_TAU
    log_a = log_a.reshape(B, T, GLA_HEADS, GLA_DK)
    if gla_s0 is None:
        gla_s0 = jnp.zeros((B, GLA_HEADS, GLA_DK, GLA_DV), x.dtype)
    o_gla, gla_s = gla_chunked(gq, gk, gv, log_a, gla_s0)
    o_gla = rms_norm(o_gla, p['gla_norm_g']) * jax.nn.silu(g_r.reshape(B, T, GLA_HEADS, GLA_DV))
    a = o_nsa.reshape(B, T, NSA_HEADS * HEAD_DIM) @ p['w_nsa_up']
    c = o_gla.reshape(B, T, GLA_HEADS * GLA_DV) @ p['w_gla_up']
    m_a, m_c = jnp.split(mg, 2, axis=-1)
    y = (jax.nn.sigmoid(m_a) * a + jax.nn.sigmoid(m_c) * c) @ p['w_out']
    return y, kv_rows, win_new, gla_s

def trunk_layer(h, pos, past_kv, win_buf, gla_s0, p):
    y, kv_rows, win_new, gla_s = token_mixer(h, pos, past_kv, win_buf, gla_s0, p)
    h = layer_norm(DN_ALPHA * h + y, p['ln1_g'], p['ln1_b'])
    f = jnp.square(jax.nn.relu(h @ p['mlp_w1'])) @ p['mlp_w2']
    h = layer_norm(DN_ALPHA * h + f, p['ln2_g'], p['ln2_b'])
    return h, kv_rows, win_new, gla_s

def setup_inputs(seed: int = 0) -> dict:
    key = jax.random.key(seed)
    ks = iter(jax.random.split(key, 40))

    def nrm(shape, scale):
        return jax.random.normal(next(ks), shape, jnp.float32) * scale

    n_pages = PAST_LEN // PAGE_SIZE
    used = DEC_BATCH * n_pages
    n_phys = used + max(1, used // 4)
    win_buf = min(WINDOW, PAST_LEN)
    page_table = jax.random.permutation(next(ks), n_phys)[:used].reshape(DEC_BATCH, n_pages).astype(jnp.int32)
    qw = NSA_HEADS * HEAD_DIM
    vw = GLA_HEADS * GLA_DV
    return {
        'x_prompt': nrm((BATCH, SEQ, D_MODEL), 1.0),
        'x_sample': nrm((DEC_BATCH, DEC_SEQ, D_MODEL), 1.0),
        'cache_nsa_kv': nrm((n_phys, DEPTH, PAGE_SIZE, N_KV_SLOTS, NSA_GROUPS, HEAD_DIM), 1.0),
        'cache_win_kv': nrm((DEC_BATCH, DEPTH, win_buf, 2, NSA_GROUPS, HEAD_DIM), 1.0),
        'state_gla': nrm((DEC_BATCH, DEPTH, GLA_HEADS, GLA_DK, GLA_DV), 0.1),
        'page_table': page_table,
        'ln_in_g': 1.0 + nrm((D_MODEL,), 0.02),
        'ln_in_b': nrm((D_MODEL,), 0.02),
        'w_in': nrm((DEPTH, D_MODEL, D_IN), D_MODEL ** -0.5),
        'cmp_k_pe': nrm((DEPTH, CMP_LEN, HEAD_DIM), 0.02),
        'cmp_k_w1': nrm((DEPTH, CMP_LEN * HEAD_DIM, CMP_HID), (CMP_LEN * HEAD_DIM) ** -0.5),
        'cmp_k_w2': nrm((DEPTH, CMP_HID, HEAD_DIM), CMP_HID ** -0.5),
        'cmp_v_pe': nrm((DEPTH, CMP_LEN, HEAD_DIM), 0.02),
        'cmp_v_w1': nrm((DEPTH, CMP_LEN * HEAD_DIM, CMP_HID), (CMP_LEN * HEAD_DIM) ** -0.5),
        'cmp_v_w2': nrm((DEPTH, CMP_HID, HEAD_DIM), CMP_HID ** -0.5),
        'gla_w_a2': nrm((DEPTH, GLA_RANK, GLA_HEADS * GLA_DK), GLA_RANK ** -0.5),
        'gla_b_a': nrm((DEPTH, GLA_HEADS * GLA_DK), 0.5),
        'gla_norm_g': 1.0 + nrm((DEPTH, GLA_DV), 0.02),
        'w_nsa_up': nrm((DEPTH, qw, D_MODEL), qw ** -0.5 * DN_BETA),
        'w_gla_up': nrm((DEPTH, vw, D_MODEL), vw ** -0.5 * DN_BETA),
        'w_out': nrm((DEPTH, D_MODEL, D_MODEL), D_MODEL ** -0.5 * DN_BETA),
        'ln1_g': 1.0 + nrm((DEPTH, D_MODEL), 0.02),
        'ln1_b': nrm((DEPTH, D_MODEL), 0.02),
        'mlp_w1': nrm((DEPTH, D_MODEL, D_FF), D_MODEL ** -0.5),
        'mlp_w2': nrm((DEPTH, D_FF, D_MODEL), D_FF ** -0.5 * DN_BETA),
        'ln2_g': 1.0 + nrm((DEPTH, D_MODEL), 0.02),
        'ln2_b': nrm((DEPTH, D_MODEL), 0.02),
    }

def reference(x_prompt, x_sample, cache_nsa_kv, cache_win_kv, state_gla, page_table,
              ln_in_g, ln_in_b, w_in, cmp_k_pe, cmp_k_w1, cmp_k_w2, cmp_v_pe, cmp_v_w1, cmp_v_w2,
              gla_w_a2, gla_b_a, gla_norm_g, w_nsa_up, w_gla_up, w_out,
              ln1_g, ln1_b, mlp_w1, mlp_w2, ln2_g, ln2_b):
    dec_b, n_pages = page_table.shape
    pos_p = jnp.arange(x_prompt.shape[1])
    pos_s = PAST_LEN + jnp.arange(x_sample.shape[1])
    hp = layer_norm(x_prompt, ln_in_g, ln_in_b)
    hs = layer_norm(x_sample, ln_in_g, ln_in_b)
    kv_p, win_p, gla_p, kv_s, win_s, gla_s = [], [], [], [], [], []
    for l in range(DEPTH):
        p = dict(w_in=w_in[l], cmp_k_pe=cmp_k_pe[l], cmp_k_w1=cmp_k_w1[l], cmp_k_w2=cmp_k_w2[l],
                 cmp_v_pe=cmp_v_pe[l], cmp_v_w1=cmp_v_w1[l], cmp_v_w2=cmp_v_w2[l],
                 gla_w_a2=gla_w_a2[l], gla_b_a=gla_b_a[l], gla_norm_g=gla_norm_g[l],
                 w_nsa_up=w_nsa_up[l], w_gla_up=w_gla_up[l], w_out=w_out[l],
                 ln1_g=ln1_g[l], ln1_b=ln1_b[l], mlp_w1=mlp_w1[l], mlp_w2=mlp_w2[l],
                 ln2_g=ln2_g[l], ln2_b=ln2_b[l])
        hp, kv, win, st = trunk_layer(hp, pos_p, None, None, None, p)
        kv_p.append(kv); win_p.append(win); gla_p.append(st)
        past = cache_nsa_kv[page_table, l].reshape(dec_b, n_pages * PAGE_SIZE, N_KV_SLOTS, NSA_GROUPS, HEAD_DIM)
        hs, kv, win, st = trunk_layer(hs, pos_s, past, cache_win_kv[:, l], state_gla[:, l], p)
        kv_s.append(kv); win_s.append(win); gla_s.append(st)
    nsa_kv_prompt = jnp.stack(kv_p, axis=1)
    win_kv_prompt = jnp.stack(win_p, axis=1)
    gla_state_prompt = jnp.stack(gla_p, axis=1)
    nsa_kv_sample = jnp.stack(kv_s, axis=1)
    win_kv_sample = jnp.stack(win_s, axis=1)
    gla_state_sample = jnp.stack(gla_s, axis=1)
    return (hp, hs, nsa_kv_prompt, win_kv_prompt, gla_state_prompt, nsa_kv_sample, win_kv_sample, gla_state_sample)


_drawn_inputs = setup_inputs


def setup_inputs(seed=0):
    import zlib

    import numpy as np

    out = dict(_drawn_inputs(seed))
    spreads = {}
    factors = {'cache_nsa_kv': 3.784,
     'cmp_k_pe': 8.0,
     'cmp_k_w1': 7.261,
     'cmp_k_w2': 7.153,
     'cmp_v_pe': 28.251,
     'gla_norm_g': 31.193}
    for name, (base, spread) in spreads.items():
        noise = np.random.default_rng([zlib.crc32(name.encode()), seed]).standard_normal(out[name].shape)
        drawn = base * np.exp(spread * noise) if base else spread * noise
        out[name] = jnp.asarray(drawn.astype(out[name].dtype))
    for name, factor in factors.items():
        out[name] = (out[name] * factor).astype(out[name].dtype)
    return out
```

```python
from contextlib import ExitStack

import concourse.bass as bass
from concourse import mybir

F32 = mybir.dt.float32
I32 = mybir.dt.int32
ALU = mybir.AluOpType
ACT = mybir.ActivationFunctionType
AX = mybir.AxisListType.X

D = 1024
KD = D // 128
SEQ, NS = 256, 8
NT = SEQ + NS
LAYERS = 2
HEADS, GROUPS, HD = 8, 2, 64
HPG = HEADS // GROUPS
SLOTS = 6
SCALE = HD ** -0.5
NWIN = 15
CSTR, CLEN = 16, 32
PAST = 256
NKEY = PAST + 1
GH, DK, DV = 4, 64, 128
CH = 64
RANK = 16
TAU = 16.0
DFF = 4096
EPS = 1e-5
ALPHA = (2.0 * LAYERS) ** 0.25
NEG = -1e30
GELU_C = 0.7978845608028654
OFF_Q, OFF_KV, OFF_G = 0, 512, 1280
OFF_GQ, OFF_GK, OFF_GV, OFF_LR, OFF_GR, OFF_MG = 1304, 1560, 1816, 2328, 2344, 2856

C_ID, C_ONE, C_ROT, C_CAUS, C_TRI, C_MID, C_AFT, C_GM = (128 * i for i in range(8))
C_COS = 1024
C_SIN = C_COS + NT
C_CADD = C_SIN + NT
C_C01 = C_CADD + 2 * NWIN
C_M8 = C_C01 + 2 * NWIN
C_KD = C_M8 + 8
C_EPS = C_KD + 8
C_N = C_EPS + 1

V_L1G, V_L1B, V_L2G, V_L2B, V_GN, V_PEK, V_PEV, V_N = 0, 8, 16, 24, 32, 33, 49, 65


class Banks:

    def __init__(self, plan, ready, done, banks):
        self.plan, self.ready, self.done, self.banks = plan, ready, done, banks
        self.total = len(plan)
        self.at = {name: i for i, name in enumerate(plan)}
        assert len(self.at) == self.total

    def bank(self, name):
        return self.banks[self.at[name] % 2]

    def filled(self, l, name):
        return l * self.total + (self.at[name] + 1)

    def emptied(self, l, name):
        return l * self.total + (self.at[name] + 3)

    def free(self, l, name):
        return l * self.total + (2 + max(self.at[name] - 1, 0))


class Steps:

    def __init__(self, sem, per_layer):
        self.sem, self.per = sem, per_layer

    def at(self, l, n):
        return l * self.per + n


def unit_name(u):
    return f"unit{u}"


STORES = 12
LINKS = (258, 33)


def build(nc, A, O):
    RING = 4
    TILES = 61
    T_Q, T_KV, T_GLA, T_GR, T_CMP, T_MG, T_UP, T_OUT, T_M1, T_M2 = 0, 2, 5, 9, 11, 13, 21, 25, 29, 45

    acc_plan = ([f"q{i}" for i in range(4)] + [f"kv{i}" for i in range(6)] + [f"gla{i}" for i in range(4)] + ["small"] + [f"gla{i}" for i in range(4, 8)]
                + [f"gr{i}" for i in range(4)] + [f"mg{i}" for i in range(16)]
                + [f"up{i}" for i in range(16)] + [f"out{i}" for i in range(8)]
                + [f"m1_{i}" for i in range(32)] + [f"m2_{i}" for i in range(8)])
    t_plan = (["vec"] + [f"rope{i}" for i in range(6)] + [f"kvt{i}" for i in range(6)]
              + sum([[f"pairs{s}", f"keys{s}"] for s in range(NS)], []) + [f"glt{i}" for i in range(6)] + ["gate", "kcmp"] + [f"vcmp{i}" for i in range(3)]
              + ["pc00", "pc01"] + [f"pt{u}" for u in range(9)] + ["pc10", "pc11"] + [f"pt{u}" for u in range(9, 16)]
              + ["spt", "snew"]
              + ["la01", "la2", "elas"]
              + sum([[f"aft{t}", f"gA{t}0", f"gA{t}1", f"U{t}0", f"U{t}1"] for t in range(2)], [])
              + [f"SU{i}" for i in range(8)])
    sc_plan = (["ssc0", "ssc1", "hidk", "hidv", "csc00", "csc01", "csc10", "csc11", "ssc2"] + [f"sc{u}" for u in range(16)]
               + ["gB0", "gB1", "rms0", "rms1", "rms2"] + ["ln1m", "ln1v", "ln2m", "ln2v"])
    o_plan = [f"o{i}" for i in range(8)] + ["so", "go00", "go01", "go10", "go11", "gos0", "gos1"]

    with ExitStack() as ctx:
        def sb(name, shape, dt=F32):
            return ctx.enter_context(nc.sbuf_tensor(name, shape, dt))

        def pb(name):
            return ctx.enter_context(nc.psum_tensor(name, [128, 512], F32))

        def sem(name):
            return ctx.enter_context(nc.semaphore(name))

        cst = sb("cst", [128, C_N])
        ident, ones = cst[:, C_ID:C_ID + 128], cst[:, C_ONE:C_ONE + 128]
        epsc = cst[:, C_EPS:C_EPS + 1]
        ptab = sb("ptab", [1, 16], I32)
        hT = sb("hT", [128, KD, NT])
        wt = [sb(f"wt{i}", [128, 2048]) for i in range(RING)]
        wsm = sb("wsm", [128, KD, 56])
        small = sb("small", [32, NT])
        gateT = sb("gateT", [24, NT])
        AR = sb("AR", [128, 40 * NT])
        used = [0]

        def ar(n):
            a = AR[:, used[0]:used[0] + n]
            used[0] += n
            return a

        qT = ar(4 * NT).rearrange("p (c t) -> p c t", c=4)
        qR = ar(4 * NT).rearrange("p (c t) -> p c t", c=4)
        kvT = ar(6 * NT).rearrange("p (c t) -> p c t", c=6)
        glT = ar(8 * NT).rearrange("p (c t) -> p c t", c=8)
        cmpT = ar(2 * 2 * 9 * 128).rearrange("p (j g s i) -> p j g s i", j=2, g=2, s=9)
        assert used[0] <= 40 * NT
        gtmp = cmpT.rearrange("p j g s i -> p (j g s i)")
        tused = [0]

        def tmp(n, rows=128):
            a = gtmp[0:rows, tused[0]:tused[0] + n]
            tused[0] += n
            assert tused[0] <= 4608
            return a

        hid = AR[:, 0:32 * NT].rearrange("p (c t) -> p c t", c=32)
        sq = AR[:, 32 * NT:40 * NT].rearrange("p (c t) -> p c t", c=8)
        grT = sb("grT", [128, 4, NT])
        mgT = sb("mgT", [128, 16, NT])
        gre = mgT[:, 12:16, :]
        kTs = sb("kTs", [128, 2, 2, NKEY])
        kvtok = sb("kvtok", [128, 3, SLOTS * 128])
        gltok = sb("gltok", [128, 3, 768])
        stg = sb("stg", [128, 2, 2, 512])
        stw = sb("stw", [128, 2, 2, 128])
        Vs = sb("Vs", [128, 2, NS, 2, 128])
        Sst = sb("Sst", [128, NS, 2, 128])
        Sp = sb("Sp", [128, 2, 2, 128])
        vecr = sb("vecr", [V_N, 128])
        lv = sb("lv", [128, V_N])
        wa2 = sb("wa2", [RANK + 1, 256])
        w2 = sb("w2", [128, 2, 64])
        gates = sb("gates", [128, 3, 24])
        gate64 = sb("gate64", [64, 3])
        tmpA = cmpT.rearrange("p j g s i -> p (j g s i)")[:, 0:NT]
        hb = sb("hb", [128, 2])
        kc = sb("kc", [128, 9 * NWIN])
        cv = sb("cv", [NWIN, (9 + 8) * 128])
        vc = cv[:, 0:9 * 128].rearrange("p (s d) -> p s d", s=9)
        PS = sb("PS", [128, 2, 2, 256])
        pflat = PS[:, :, :, :].rearrange("p u r k -> p (u r k)")
        hx = pflat[:, 0:540].rearrange("p (j n) -> p j n", j=2)
        hy = pflat[:, 540:810]
        PT = sb("PT", [128, 2, 4, 128])
        st = sb("st", [128, 2, 8])
        CS = sb("CS", [128, 2, 8, NWIN])
        cst8 = sb("cst8", [128, 2, 3, 8])
        PTc = cv[:, 9 * 128:17 * 128].rearrange("p (h q) -> p h q", h=8)
        onT = sb("onT", [128, 4, NT])
        ogT = glT[:, 4:8, :]
        Qz = sb("Qz", [128, 2, NS, 64])
        P64 = sb("P64", [64, 2, NKEY])
        C64 = sb("C64", [64, NWIN])
        s64 = sb("s64", [64, 12])
        PTs = sb("PTs", [128, 4, 64])
        PTcs = sb("PTcs", [NWIN, 64])
        An = sb("An", [64, 2, 8])
        Pn = sb("Pn", [8, 2, 64])
        xla = sb("xla", [128, 3, 256])
        lla = tmp(768).rearrange("p (g n) -> p g n", g=3)
        ela = sb("ela", [128, 2, 8])
        qs = sb("qs", [128, 2, 8])
        kz = cv[0:NS, 0:NS * 256].rearrange("p (s n) -> p s n", s=NS)
        EB = tmp(768).rearrange("p (a h n) -> p a h n", a=3, h=2)
        kd = tmp(256)
        qe, qm, km = (tmp(256).rearrange("p (h n) -> p h n", h=2) for _ in range(3))
        gAs = tmp(512).rearrange("p (h n) -> p h n", h=4)
        osq = tmp(512)
        rr = tmp(512)
        upb = qT[:, 0:2, :]
        yb, mu, rs = onT[:, 0:2, :], onT[:, 2, :], onT[:, 3, :]
        xin = mgT[:, 0:12, :].rearrange("p a b -> p (a b)")[:, 0:3072].rearrange("p (g f) -> p g f", g=3)

        acc = Banks(acc_plan, sem("acc_ready"), sem("acc_done"), [pb("acc0"), pb("acc1")])
        tb = Banks(t_plan, sem("tr_ready"), sem("tr_done"), [pb("tr0"), pb("tr1")])
        sc = Banks(sc_plan, sem("sc_ready"), sem("sc_done"), [pb("sc0"), pb("sc1")])
        ob = Banks(o_plan, sem("o_ready"), sem("o_done"), [pb("o0"), pb("o1")])

        w_landed = [sem(f"w_landed{i}") for i in range(RING)]
        m2_part = Steps(sem("m2_part"), 12)
        const_in = sem("const_in")
        x_in = sem("x_in")
        wsm_in = Steps(sem("wsm_in"), 32)
        vec_in = Steps(sem("vec_in"), 16 * 7)
        par_in = Steps(sem("par_in"), 16 * 4)
        cache_in = [Steps(sem(f"cache_in{i}"), 16 * 3 * 4) for i in range(2)]
        mixers_done = Steps(sem("mixers_done"), 1)
        val_in = Steps(sem("val_in"), 16 * NS)
        val_copied = Steps(sem("val_copied"), NS)
        state_in = Steps(sem("state_in"), 64)
        gate_in = Steps(sem("gate_in"), 32)
        stored = sem("stored")
        pe_passed, pool_passed, sp_passed = sem("pe_passed"), sem("pool_passed"), sem("sp_passed")

        ini = {n: sem("in_" + n) for n in ("tr", "trc", "sum", "mu", "cen", "sq", "var", "rs", "h", "zero")}
        dve_link = Steps(sem("dve_link"), 0)
        act_link = Steps(sem("act_link"), 0)
        DVE_LINKS, ACT_LINKS = LINKS
        dve_link.per, act_link.per = DVE_LINKS, ACT_LINKS
        h_ready = Steps(sem("h_ready"), 2)
        vec_cols = Steps(sem("vec_cols"), 1)
        q_rot = Steps(sem("q_rot"), 6)
        gla_silu = Steps(sem("gla_silu"), 1)
        pairs = Steps(sem("pairs"), 1)
        gate_exp = Steps(sem("gate_exp"), 1)
        gate_sig = Steps(sem("gate_sig"), 1)
        hid_x = Steps(sem("hid_x"), 2)
        hid_u = Steps(sem("hid_u"), 2)
        hid_e = Steps(sem("hid_e"), 2)
        hid_g = Steps(sem("hid_g"), 2)
        mg_exp = Steps(sem("mg_exp"), 16)
        mg_sig = Steps(sem("mg_sig"), 16)
        c_shift = Steps(sem("c_shift"), 2)
        c_exp = Steps(sem("c_exp"), 2)
        s_cmax = Steps(sem("s_cmax"), 1)
        u_half = Steps(sem("u_half"), 16)
        pv_done = Steps(sem("pv_done"), 8)
        c_prob = Steps(sem("c_prob"), 2)
        u_max = Steps(sem("u_max"), 16)
        u_exp = Steps(sem("u_exp"), 16)
        u_prob = Steps(sem("u_prob"), 16)
        s_qz = Steps(sem("s_qz"), 1)
        s_keys = Steps(sem("s_keys"), 7)
        s_max = Steps(sem("s_max"), 1)
        s_exp = Steps(sem("s_exp"), 1)
        s_prob = Steps(sem("s_prob"), 1)
        s_anew = Steps(sem("s_anew"), 1)
        la_e = Steps(sem("la_e"), 1)
        la_t = Steps(sem("la_t"), 1)
        ela_d = Steps(sem("ela_d"), 1)
        kz_d = Steps(sem("kz_d"), 1)
        g_eb = Steps(sem("g_eb"), 2)
        g_ea = Steps(sem("g_ea"), 2)
        g_q = Steps(sem("g_q"), 2)
        g_state = Steps(sem("g_state"), 4)
        s_state = Steps(sem("s_state"), 8)
        r_sq = Steps(sem("r_sq"), 3)
        r_rs = Steps(sem("r_rs"), 3)
        og_d = Steps(sem("og_d"), 3)
        up_m = Steps(sem("up_m"), 8)
        res1 = Steps(sem("res1"), 8)
        res2 = Steps(sem("res2"), 8)
        m1_sq = Steps(sem("m1_sq"), 32)
        ln_cen = Steps(sem("ln_cen"), 2)
        ln_sq = Steps(sem("ln_sq"), 2)
        ln_rs = Steps(sem("ln_rs"), 2)

        TG = [(0, 128), (128, 128), (256, NS)]
        block = ctx.enter_context(nc.Block())

        @block.sync
        def _(sp):
            sp.dma_start(cst[:, :], A["consts"]).then_inc(const_in, 16)
            sp.wait_ge(x_in, 80)
            with sp.Fori(0, LAYERS) as l:
                wl = lambda name: A[name][bass.ds(l, 1)].rearrange("a k n -> (a k) n")
                w_in = wl("w_in").rearrange("(k p) n -> p k n", p=128)
                w1 = wl("mlp_w1").rearrange("(k p) n -> p k n", p=128)
                w2m = wl("mlp_w2").rearrange("(kg k p) n -> kg p k n", p=128, k=KD)
                wo = wl("w_out").rearrange("(k p) n -> p k n", p=128)
                wn = wl("w_nsa_up").rearrange("(g c d) n -> g d c n", g=2, c=4)
                wg = wl("w_gla_up").rearrange("(c p) n -> p c n", p=128)

                def slot_free(t):
                    p = t - RING
                    if p < 0:
                        return acc.done, 2 + l * acc.total
                    if T_CMP <= p < T_CMP + 2:
                        return sc.ready, sc.filled(l, ("hidk", "hidv")[p - T_CMP])
                    if p >= T_M2:
                        cg, kg = (p - T_M2) // 4, (p - T_M2) % 4
                        if kg < 3:
                            return m2_part.sem, m2_part.at(l, 3 * cg + kg + 1)
                        return acc.ready, acc.filled(l, f"m2_{2 * cg + 1}")
                    name = (f"q{2 * (p - T_Q) + 1}" if p < T_KV else f"kv{2 * (p - T_KV) + 1}" if p < T_GLA
                            else f"gla{2 * (p - T_GLA) + 1}" if p < T_GR else f"gr{2 * (p - T_GR) + 1}" if p < T_CMP
                            else f"mg{2 * (p - T_MG) + 1}" if p < T_UP else f"up{4 * (p - T_UP) + 3}" if p < T_OUT
                            else f"out{2 * (p - T_OUT) + 1}" if p < T_M1 else f"m1_{2 * (p - T_M1) + 1}")
                    return acc.ready, acc.filled(l, name)

                def load(t, parts):
                    free, v = slot_free(t)
                    v = sp.snap(v)
                    sp.wait_ge(free, v)
                    for i, (dst, src) in enumerate(parts):
                        ins = sp.dma_start(dst, src)
                        ins.then_inc(w_landed[t % RING], 16)

                def t8(t):
                    return wt[t % RING][:, :].rearrange("p (k n) -> p k n", k=KD)

                def cols(t, w, c0):
                    load(t, [(t8(t), w[:, :, c0:c0 + 256])])

                def cached(s):
                    if s >= 2:
                        sp.wait_ge(val_copied.sem, val_copied.at(l, s - 1))
                        sp.sem_inc(sp_passed, 1)
                        sp.wait_ge(tb.done, tb.emptied(l, f"keys{s - 2}"))
                        sp.sem_inc(sp_passed, 1)
                    for pg in range(2):
                        page = sp.value_load(ptab[0:1, 2 * s + pg:2 * s + pg + 1], min_val=0, max_val=A["cache_nsa_kv"].shape[0] - 1)
                        src = A["cache_nsa_kv"][bass.ds(page, 1), bass.ds(l, 1)].rearrange("a b (i r) j g d -> (a b i) r (j g d)", r=2)
                        sp.dma_start(stg[64 * pg:64 * pg + 64, s % 2, :, :], src).then_inc(cache_in[s % 2].sem, 16)
                    win = A["cache_win_kv"][s, bass.ds(l, 1)].rearrange("a (i r) j g d -> (a i) r (j g d)", r=2)
                    sp.dma_start(stw[:, s % 2, :, :], win[:, :, 0:128]).then_inc(cache_in[s % 2].sem, 16)
                    sp.dma_start(Vs[:, 1, s, :, :], win[:, :, 128:256]).then_inc(val_in.sem, 16)

                for i in range(2):
                    dst = wt[(T_Q + i) % RING][:, :].rearrange("p (k c g n) -> p k c g n", k=KD, c=2, g=2)
                    load(T_Q + i, [(dst[:, :, c, g, :], w_in[:, :, OFF_Q + g * 256 + (2 * i + c) * 64:OFF_Q + g * 256 + (2 * i + c) * 64 + 64])
                                   for c in range(2) for g in range(2)])
                for i in range(3):
                    cols(T_KV + i, w_in, OFF_KV + i * 256)

                def cmp_w1(i):
                    dst = wt[(T_CMP + i) % RING][:, :].rearrange("p (k n) -> p k n", k=16)
                    src = wl(("cmp_k_w1", "cmp_v_w1")[i]).rearrange("(k p) n -> p k n", p=128)
                    load(T_CMP + i, [(dst[:, 8 * a:8 * a + 8, :], src[:, 8 * a:8 * a + 8, :]) for a in range(2)])

                v = sp.snap(mixers_done.at(l, 1))
                sp.wait_ge(mixers_done.sem, v)
                sp.sem_inc(sp_passed, 1)
                cached(0)
                cols(T_GLA, w_in, OFF_GQ)
                cached(1)
                for i in range(1, 4):
                    cols(T_GLA + i, w_in, OFF_GQ + i * 256)
                for i in range(2):
                    cols(T_GR + i, w_in, OFF_GR + i * 256)
                cached(2)
                cmp_w1(0)
                cached(3)
                cached(4)
                cmp_w1(1)
                cached(5)
                cached(6)
                cols(T_MG, w_in, OFF_MG)
                cached(7)
                for i in range(1, 8):
                    cols(T_MG + i, w_in, OFF_MG + i * 256)
                for i in range(4):
                    d = t8(T_UP + i)
                    load(T_UP + i, [(d[64 * g:64 * g + 64, 0:4, :], wn[g, :, :, i * 256:i * 256 + 256]) for g in range(2)]
                         + [(d[:, 4:8, :], wg[:, :, i * 256:i * 256 + 256])])
                for i in range(4):
                    cols(T_OUT + i, wo, i * 256)
                for i in range(16):
                    cols(T_M1 + i, w1, i * 256)
                for i in range(16):
                    load(T_M2 + i, [(t8(T_M2 + i), w2m[i % 4, :, :, (i // 4) * 256:(i // 4) * 256 + 256])])

        parts_of = {**{T_Q + i: 4 for i in range(2)}, **{T_CMP + i: 2 for i in range(2)}, **{T_UP + i: 3 for i in range(4)}}
        per_slot = [sum(16 * parts_of.get(t, 1) for t in range(TILES) if t % RING == s) for s in range(RING)]

        def landed(t):
            s = t % RING
            return w_landed[s], per_slot[s], sum(16 * parts_of.get(x, 1) for x in range(t + 1) if x % RING == s)

        @block.gpsimd
        def _(pool):
            pool.memset(small[:, :], 1.0).then_inc(ini["zero"], 1)
            pool.memset(Qz[:, :, :, :], 0.0).then_inc(ini["zero"], 1)
            pool.memset(wsm[:, :, :], 0.0).then_inc(ini["zero"], 1)
            pool.memset(xin[:, 2, :], 0.0).then_inc(ini["zero"], 1)
            pool.memset(vecr[:, :], 0.0).then_inc(ini["zero"], 1)
            pool.memset(xla[:, 2, :], 0.0).then_inc(ini["zero"], 1)
            pool.memset(gates[:, 2, :], 0.0).then_inc(ini["zero"], 1)
            pool.wait_ge(ini["zero"], 7)
            pool.dma_start(ptab[:, :], A["page_table"].rearrange("(a s) n -> a (s n)", a=1)).then_inc(x_in, 16)
            pool.dma_start(xin[:, 0:2, :], A["x_prompt"][0].rearrange("(g p) f -> p g f", p=128)).then_inc(x_in, 16)
            pool.dma_start(xin[0:NS, 2, :], A["x_sample"].rearrange("s t f -> (s t) f")).then_inc(x_in, 16)
            pool.dma_start(vecr[0:8, :], A["ln_in_g"].rearrange("(c p) -> c p", p=128)).then_inc(x_in, 16)
            pool.dma_start(vecr[8:16, :], A["ln_in_b"].rearrange("(c p) -> c p", p=128)).then_inc(x_in, 16)
            pool.wait_ge(x_in, 80)
            pool.dma_start(O["win_kv_sample"].rearrange("s l t j g d -> s l (t j g d)")[:, :, 0:255 * 256],
                           A["cache_win_kv"].rearrange("s l t j g d -> s l (t j g d)")[:, :, 256:256 * 256]).then_inc(stored, 16)
            pool.wait_ge(ini["trc"], 7)
            with pool.Fori(0, LAYERS) as l:
                def row(name, pat, **kw):
                    return A[name][bass.ds(l, 1)].rearrange(pat, **kw)

                wv = A["w_in"][bass.ds(l, 1)].rearrange("a (k p) n -> p (a k) n", p=128)
                pool.wait_ge(mixers_done.sem, mixers_done.at(l, 1))
                pool.sem_inc(pool_passed, 1)
                pool.dma_start(wsm[:, :, 0:RANK], wv[:, :, OFF_LR:OFF_LR + RANK]).then_inc(wsm_in.sem, 16)
                pool.dma_start(wsm[:, :, 32:56], wv[:, :, OFF_G:OFF_G + 24]).then_inc(wsm_in.sem, 16)
                for k, name in ((V_L1G, "ln1_g"), (V_L1B, "ln1_b"), (V_L2G, "ln2_g"), (V_L2B, "ln2_b")):
                    pool.dma_start(vecr[k:k + 8, :], row(name, "a (c p) -> (a c) p", p=128)).then_inc(vec_in.sem, 16)
                pool.dma_start(vecr[V_GN:V_GN + 1, :], row("gla_norm_g", "a p -> a p")).then_inc(vec_in.sem, 16)
                pool.dma_start(vecr[V_PEK:V_PEK + 16, :], row("cmp_k_pe", "a (i b) d -> (a i) (b d)", b=2)).then_inc(vec_in.sem, 16)
                pool.dma_start(vecr[V_PEV:V_PEV + 16, :], row("cmp_v_pe", "a (i b) d -> (a i) (b d)", b=2)).then_inc(vec_in.sem, 16)
                pool.dma_start(wa2[0:RANK, :], row("gla_w_a2", "a r n -> (a r) n")).then_inc(par_in.sem, 16)
                pool.dma_start(wa2[RANK:RANK + 1, :], row("gla_b_a", "a n -> a n")).then_inc(par_in.sem, 16)
                pool.dma_start(w2[:, 0, :], row("cmp_k_w2", "a h n -> (a h) n")).then_inc(par_in.sem, 16)
                pool.dma_start(w2[:, 1, :], row("cmp_v_w2", "a h n -> (a h) n")).then_inc(par_in.sem, 16)
                for h2 in range(2):
                    for hp in range(2):
                        if h2 == 0 and hp == 0:
                            pool.wait_ge(stored, l * (16 * STORES) + 16)
                            pool.sem_inc(pool_passed, 1)
                        ins = pool.dma_start(Sst[64 * h2:64 * h2 + 64, :, hp, :],
                                             A["state_gla"][:, bass.ds(l, 1), 2 * hp + h2].rearrange("s a k v -> k (s a) v"))
                        ins.then_inc(state_in.sem, 16)
                pool.wait_ge(tb.done, tb.emptied(l, "kvt5"))
                pool.sem_inc(pool_passed, 1)
                for g in range(2):
                    pool.dma_start(O["nsa_kv_prompt"][0, bass.ds(l, 1), 128 * g:128 * g + 128].rearrange("a t j g d -> (a t) (j g d)"),
                                   kvtok[:, g, 0:512]).then_inc(stored, 16)
                    pool.dma_start(O["win_kv_prompt"][0, bass.ds(l, 1), 128 * g:128 * g + 128].rearrange("a t j g d -> (a t) (j g d)"),
                                   kvtok[:, g, 512:768]).then_inc(stored, 16)
                pool.dma_start(O["nsa_kv_sample"][:, bass.ds(l, 1), 0].rearrange("s a j g d -> (s a) (j g d)"),
                               kvtok[0:NS, 2, 0:512]).then_inc(stored, 16)
                pool.dma_start(O["win_kv_sample"][:, bass.ds(l, 1), PAST - 1].rearrange("s a j g d -> (s a) (j g d)"),
                               kvtok[0:NS, 2, 512:768]).then_inc(stored, 16)
                pool.wait_ge(gate_sig.sem, gate_sig.at(l, 1))
                pool.sem_inc(pool_passed, 1)
                for g in range(2):
                    pool.dma_start(gate64[32 * g:32 * g + 32, :],
                                   gates[0:NS, 2, 12 * g:12 * g + 12].rearrange("s (c b) -> s c b", c=4)).then_inc(gate_in.sem, 16)
                pool.wait_ge(g_state.sem, g_state.at(l, 4))
                pool.sem_inc(pool_passed, 1)
                for h2 in range(2):
                    pool.dma_start(O["gla_state_prompt"][0, bass.ds(l, 1), h2::2].rearrange("a h k v -> k (a h) v"),
                                   Sp[64 * h2:64 * h2 + 64, 1, :, :]).then_inc(stored, 16)
                pool.wait_ge(s_state.sem, s_state.at(l, 8))
                pool.sem_inc(pool_passed, 1)
                for h2 in range(2):
                    for hp in range(2):
                        pool.dma_start(O["gla_state_sample"][:, bass.ds(l, 1), 2 * hp + h2].rearrange("s a k v -> k (s a) v"),
                                       Sst[64 * h2:64 * h2 + 64, :, hp, :]).then_inc(stored, 16)
            pool.wait_ge(ini["trc"], 13)
            pool.dma_start(O["y_prompt"][0].rearrange("(g p) f -> p g f", p=128), xin[:, 0:2, :]).then_inc(stored, 16)
            pool.dma_start(O["y_sample"].rearrange("s t f -> (s t) f"), xin[0:NS, 2, :]).then_inc(stored, 16)
            pool.wait_ge(stored, 16 * (STORES * LAYERS + 3))

        @block.tensor
        def _(pe):
            mm = nc.tensor.matmul
            pe.wait_ge(const_in, 16)
            pe.wait_ge(x_in, 80)

            def tr(out, in_, p0, np_):
                return nc.tensor.transpose(out, in_, cst[p0:p0 + np_, C_ID + p0:C_ID + p0 + np_])

            for n in range(6):
                g, half = n // 2, n % 2
                if n >= 2:
                    pe.wait_ge(ini["trc"], n - 1)
                for c in range(4):
                    ins = tr(tb.banks[n % 2][:, 128 * c:128 * c + 128], xin[:, g, (4 * half + c) * 128:(4 * half + c) * 128 + 128], 0, 128)
                ins.then_inc(ini["tr"], 1)
            pe.wait_ge(ini["trc"], 5)
            tr(tb.banks[0][:, 0:V_N], vecr[:, :], 0, V_N).then_inc(ini["tr"], 1)
            pe.wait_ge(ini["trc"], 7)
            for c in range(KD):
                ins = mm(sc.banks[0][:, 0:NT], ones, hT[:, c, :], start=(c == 0), stop=(c == KD - 1))
            ins.then_inc(ini["sum"], 1)
            pe.wait_ge(ini["sq"], 1)
            for c in range(KD):
                ins = mm(sc.banks[1][:, 0:NT], ones, sq[:, c, :], start=(c == 0), stop=(c == KD - 1))
            ins.then_inc(ini["var"], 1)

            with pe.Fori(0, LAYERS) as l:
                def wait(sem_, value):
                    pe.wait_ge(sem_, value)
                    pe.sem_inc(pe_passed, 1)

                def take(bk, name):
                    wait(bk.done, bk.free(l, name))
                    return bk.bank(name)

                def chunk(name, w, n, mv, k0=0, kn=KD, free=True, first=True, last=True, m=128):
                    bank = acc.bank(name)
                    if free:
                        pe.wait_ge(acc.done, acc.free(l, name))
                    for k in range(kn):
                        ins = mm(bank[0:m, 0:NT], w(k, n), mv(k), start=(first and k == 0), stop=(last and k == kn - 1))
                    if last:
                        ins.then_inc(acc.ready, 1)
                    return ins

                def tile_in(t):
                    s, per, v = landed(t)
                    pe.wait_ge(s, l * per + v)
                    r = wt[t % RING][:, :].rearrange("p (k n) -> p k n", k=KD)
                    return lambda k, n: r[:, k, n * 128:n * 128 + 128]

                pe.wait_ge(h_ready.sem, h_ready.at(l, 1))
                hk = lambda k: hT[:, k, :]

                def project(names, t, mv=hk):
                    w = tile_in(t)
                    for n, name in enumerate(names):
                        chunk(name, w, n, mv)

                for i in range(2):
                    project([f"q{2 * i}", f"q{2 * i + 1}"], T_Q + i)
                for i in range(3):
                    project([f"kv{2 * i}", f"kv{2 * i + 1}"], T_KV + i)
                for i in range(2):
                    project([f"gla{2 * i}", f"gla{2 * i + 1}"], T_GLA + i)
                wait(wsm_in.sem, wsm_in.at(l, 32))
                chunk("small", lambda k, n: wsm[:, k, :], 0, hk, m=56)

                wait(vec_in.sem, vec_in.at(l, 112))
                b = take(tb, "vec")
                tr(b[:, 0:V_N], vecr[:, :], 0, V_N).then_inc(tb.ready, 1)
                for i in range(6):
                    src, name = (qT[:, i, :], f"q{i}") if i < 4 else (kvT[:, 2 * (i - 3), :], f"kv{2 * (i - 3)}")
                    wait(acc.done, acc.emptied(l, name))
                    b = take(tb, f"rope{i}")
                    mm(b[:, 0:NT], cst[:, C_ROT:C_ROT + 128], src, start=True, stop=True).then_inc(tb.ready, 1)

                wait(q_rot.sem, q_rot.at(l, 6))
                wait(acc.done, acc.emptied(l, "kv5"))
                for i in range(6):
                    c0, n = TG[i // 2]
                    b = take(tb, f"kvt{i}")
                    for j in range(4 if i % 2 == 0 else 2):
                        ins = tr(b[0:n, 128 * j:128 * j + 128], kvT[:, 4 * (i % 2) + j, c0:c0 + n], 0, 128)
                    ins.then_inc(tb.ready, 1)
                wait(s_qz.sem, s_qz.at(l, 1))
                for s in range(NS):
                    wait(cache_in[s % 2].sem, cache_in[s % 2].at(l, 48 * (s // 2 + 1)))
                    b = take(tb, f"pairs{s}")
                    for n in range(4):
                        for r in range(2):
                            ins = mm(b[64 * r:64 * r + 64, 128 * n:128 * n + 128], stg[:, s % 2, r, 64 * n:64 * n + 64], ident,
                                     start=True, stop=True)
                    ins.then_inc(tb.ready, 1)
                    b = take(tb, f"keys{s}")
                    for n in range(4):
                        src = stg[:, s % 2, n, 256:384] if n < 2 else stw[:, s % 2, n - 2, :]
                        ins = tr(b[:, 128 * n:128 * n + 128], src, 0, 128)
                    ins.then_inc(tb.ready, 1)
                    if s == 0:
                        take(sc, "ssc0")
                        take(sc, "ssc1")
                    wait(tb.done, tb.emptied(l, f"keys{s}"))
                    for br in range(2):
                        ins = mm(sc.bank(f"ssc{br}")[0:64, 0:NKEY], Qz[:, 1, s, :], kTs[:, s % 2, br, :], start=(s == 0), stop=(s == NS - 1))
                        if s == NS - 1:
                            ins.then_inc(sc.ready, 1)
                        elif br == 1:
                            ins.then_inc(s_keys.sem, 1)
                    if s % 2 == 0:
                        w = tile_in((T_GLA + 2, T_GLA + 3, T_GR, T_GR + 1)[s // 2])
                    chunk(f"gla{4 + s}" if s < 4 else f"gr{s - 4}", w, s % 2, hk)
                wait(acc.done, acc.emptied(l, "gla7"))
                for i in range(6):
                    c0, n = TG[i // 2]
                    b = take(tb, f"glt{i}")
                    for j in range(4 if i % 2 == 0 else 2):
                        ins = tr(b[0:n, 128 * j:128 * j + 128], glT[:, 2 + 4 * (i % 2) + j, c0:c0 + n], 0, 128)
                    ins.then_inc(tb.ready, 1)
                b = take(tb, "gate")
                for g, (c0, n) in enumerate(TG):
                    ins = tr(b[0:n, 24 * g:24 * g + 24], gateT[:, c0:c0 + n], 0, 24)
                ins.then_inc(tb.ready, 1)
                wait(pairs.sem, pairs.at(l, 1))
                for j, name in enumerate(("hidk", "hidv")):
                    s, per, v = landed(T_CMP + j)
                    wait(s, l * per + v)
                    b = take(sc, name)
                    w = wt[(T_CMP + j) % RING]
                    for lp in range(16):
                        wk = w[:, 128 * lp:128 * lp + 128]
                        rows = cmpT[:, j].rearrange("p g s i -> p (g s) i")[:, :, lp:lp + 8 * 14 + 1:8]
                        mm(b[:, 0:270], wk, rows, start=(lp == 0), stop=(lp == 15))
                    for lp in range(16):
                        ins = mm(b[:, 272:273], w[:, 128 * lp:128 * lp + 128],
                                 lv[:, V_PEK + 16 * j + lp:V_PEK + 16 * j + lp + 1], start=(lp == 0), stop=(lp == 15))
                    ins.then_inc(sc.ready, 1)

                def gate_chunk(i):
                    chunk(f"mg{i}", tile_in(T_MG + i // 2), i % 2, hk)

                gate_chunk(0)
                gate_chunk(1)
                wait(par_in.sem, par_in.at(l, 64))
                wait(hid_g.sem, hid_g.at(l, 1))
                b = take(tb, "kcmp")
                for g in range(2):
                    ins = mm(b[64 * g:64 * g + 64, 0:135], w2[:, 0, :], hx[:, 0, 135 * g:135 * g + 135], start=True, stop=True)
                ins.then_inc(tb.ready, 1)
                wait(hid_g.sem, hid_g.at(l, 2))
                for i in range(3):
                    b = take(tb, f"vcmp{i}")
                    for s in range(4 * i, min(4 * i + 4, 9)):
                        for g in range(2):
                            o0 = (s - 4 * i) * 128 + 64 * g
                            ins = mm(b[0:NWIN, o0:o0 + 64], hx[:, 1, 135 * g + 15 * s:135 * g + 15 * s + 15], w2[:, 1, :],
                                     start=True, stop=True)
                    ins.then_inc(tb.ready, 1)

                for t in range(2):
                    wait(tb.done, tb.emptied(l, "kcmp"))
                    for g in range(GROUPS):
                        b = take(sc, f"csc{t}{g}")
                        for c in range(4):
                            ins = mm(b[:, 15 * c:15 * c + 15], qT[64 * g:64 * g + 64, c, 128 * t:128 * t + 128],
                                     kc[64 * g:64 * g + 64, 120:135], start=True, stop=True)
                        ins.then_inc(sc.ready, 1)
                b = take(sc, "ssc2")
                for s in range(NS):
                    ins = mm(b[0:64, 0:NWIN], Qz[:, 0, s, :], kc[:, 15 * s:15 * s + 15], start=(s == 0), stop=(s == NS - 1))
                ins.then_inc(sc.ready, 1)

                def scores(u):
                    t, c, g = u // 8, (u % 8) // 2, u % 2
                    b = take(sc, f"sc{u}")
                    for br in range(2):
                        ins = mm(b[:, 256 * br:256 * br + 128 * (t + 1)], qR[64 * g:64 * g + 64, c, 128 * t:128 * t + 128],
                                 kvT[64 * g:64 * g + 64, 2 + 2 * br, 0:128 * (t + 1)], start=True, stop=True)
                    ins.then_inc(sc.ready, 1)

                def prob_tr(u):
                    t = u // 8
                    wait(u_prob.sem, u_prob.at(l, u + 1))
                    b = take(tb, f"pt{u}")
                    for br in range(2):
                        for kb in range(t + 1):
                            n = br * (t + 1) + kb
                            ins = tr(b[:, 128 * n:128 * n + 128], PS[:, u % 2, br, 128 * kb:128 * kb + 128], 0, 128)
                    ins.then_inc(tb.ready, 1)

                def values(u):
                    t, c, g = u // 8, (u % 8) // 2, u % 2
                    name = f"o{u // 2}"
                    b = take(ob, name) if g == 0 else ob.bank(name)
                    wait(tb.done, tb.emptied(l, f"pt{u}"))
                    o = b[64 * g:64 * g + 64, 0:128]
                    mm(o, vc[:, 8, 64 * g:64 * g + 64], PTc[:, 4 * g + c, :], start=True, stop=False)
                    for br in range(2):
                        for kb in range(t + 1):
                            c0 = (3 + 2 * br) * 128 + 64 * g
                            end = br == 1 and kb == t
                            ins = mm(o, kvtok[:, kb, c0:c0 + 64], PT[:, u % 2, br * (t + 1) + kb, :], start=False, stop=end)
                    ins.then_inc(ob.ready if g == 1 else pv_done.sem, 1)

                def compressed_tr(t):
                    wait(c_prob.sem, c_prob.at(l, t + 1))
                    for a in range(2):
                        b = take(tb, f"pc{t}{a}")
                        for i in range(4):
                            ins = tr(b[0:NWIN, 128 * i:128 * i + 128], CS[:, t, 4 * a + i, :], 0, 128)
                        ins.then_inc(tb.ready, 1)

                for k in range(18):
                    if k < 16:
                        scores(k)
                    if k < 14:
                        gate_chunk(k + 2)
                    if k == 1:
                        compressed_tr(0)
                    if 1 <= k <= 16:
                        prob_tr(k - 1)
                    if k >= 2:
                        values(k - 2)
                    if k == 9:
                        compressed_tr(1)

                wait(s_prob.sem, s_prob.at(l, 1))
                b = take(tb, "spt")
                for n in range(4):
                    tr(b[:, 64 * n:64 * n + 64], P64[:, n // 2, 128 * (n % 2):128 * (n % 2) + 128], 0, 64)
                tr(b[0:NWIN, 256:320], C64[:, :], 0, 64).then_inc(tb.ready, 1)
                b = take(tb, "snew")
                wait(s_anew.sem, s_anew.at(l, 1))
                for br in range(2):
                    ins = mm(b[0:8, 64 * br:64 * br + 64], An[:, br, :], cst[0:64, C_ID:C_ID + 64], start=True, stop=True)
                ins.then_inc(tb.ready, 1)
                wait(val_in.sem, val_in.at(l, 16 * NS))
                wait(val_copied.sem, val_copied.at(l, NS))
                wait(tb.done, tb.emptied(l, "snew"))
                b = take(ob, "so")
                for br in range(2):
                    c0 = (3 + 2 * br) * 128
                    mm(b[:, 0:64], kvtok[0:8, 2, c0:c0 + 128], Pn[:, br, :], start=(br == 0), stop=False, skip_group_check=True)
                for s in range(NS):
                    o = b[:, 0:64].rearrange("p (g s c) -> p g s c", g=2, s=NS)[:, :, s, :]
                    for n in range(4):
                        mv = PTs[:, n, :].rearrange("p (g s c) -> p g s c", g=2, s=NS)[:, :, s, :]
                        mm(o, Vs[:, n // 2, s, n % 2, :], mv, start=False, stop=False, skip_group_check=True)
                    mv = PTcs[:, :].rearrange("p (g s c) -> p g s c", g=2, s=NS)[:, :, s, :]
                    ins = mm(o, vc[:, s, :], mv, start=False, stop=(s == NS - 1), skip_group_check=True)
                ins.then_inc(ob.ready, 1)

                b = take(tb, "la01")
                wait(acc.done, acc.emptied(l, "small"))
                for g in range(2):
                    ins = mm(b[:, 256 * g:256 * g + 256], small[0:RANK + 1, 128 * g:128 * g + 128], wa2[:, :], start=True, stop=True)
                ins.then_inc(tb.ready, 1)
                b = take(tb, "la2")
                mm(b[0:NS, 0:256], small[0:RANK + 1, SEQ:NT], wa2[:, :], start=True, stop=True).then_inc(tb.ready, 1)
                wait(la_t.sem, la_t.at(l, 1))
                b = take(tb, "elas")
                for hp in range(2):
                    ins = tr(b[:, 8 * hp:8 * hp + 8], xla[0:NS, 2, 128 * hp:128 * hp + 128], 0, NS)
                ins.then_inc(tb.ready, 1)
                def head_squares(i):
                    wait(r_sq.sem, r_sq.at(l, i + 1))
                    n = 512 if i < 2 else 32
                    b = take(sc, f"rms{i}")
                    mm(b[:, 0:n], ones, osq[:, 0:n], start=True, stop=True).then_inc(sc.ready, 1)

                for t in range(2):
                    b = take(sc, f"gB{t}")
                    for hp in range(2):
                        ins = mm(b[:, 256 * hp:256 * hp + 256], xla[:, t, 128 * hp:128 * hp + 128], cst[:, C_TRI:C_TRI + 256], start=True, stop=True)
                    ins.then_inc(sc.ready, 1)
                    b = take(tb, f"aft{t}")
                    mm(b[:, 0:256], cst[:, C_AFT:C_AFT + 128], xla[:, t, :], start=True, stop=True).then_inc(tb.ready, 1)
                    if t == 1:
                        head_squares(0)
                    wait(g_q.sem, g_q.at(l, t + 1))
                    for h2 in range(2):
                        b = take(tb, f"gA{t}{h2}")
                        for hp in range(2):
                            ins = mm(b[:, 128 * hp:128 * hp + 128], km[64 * h2:64 * h2 + 64, hp, :], qm[64 * h2:64 * h2 + 64, hp, :], start=True, stop=True)
                        ins.then_inc(tb.ready, 1)
                    for ch in range(2):
                        b = take(tb, f"U{t}{ch}")
                        for hp in range(2):
                            ins = mm(b[:, 256 * hp:256 * hp + 256], kd[64 * ch:64 * ch + 64, 128 * hp:128 * hp + 128],
                                     gltok[64 * ch:64 * ch + 64, t, 256 + 256 * hp:512 + 256 * hp], start=True, stop=True)
                        ins.then_inc(tb.ready, 1)
                    bs = [take(ob, f"go{t}{h2}") for h2 in range(2)]
                    wait(tb.done, tb.emptied(l, f"gA{t}1"))
                    for h2 in range(2):
                        for hp in range(2):
                            h = 2 * hp + h2
                            mm(bs[h2][:, 128 * hp:128 * hp + 128], gltok[:, t, 256 + 128 * h:384 + 128 * h], gAs[:, h, :],
                               start=(hp == 0), stop=False, skip_group_check=True)
                    for ch in range(2):
                        k = 2 * t + ch
                        if k == 0:
                            continue
                        wait(g_state.sem, g_state.at(l, k))
                        for h2 in range(2):
                            for hp in range(2):
                                c0 = 128 * hp + 64 * ch
                                ins = mm(bs[h2][:, c0:c0 + 64], Sp[64 * h2:64 * h2 + 64, (k - 1) % 2, hp, :],
                                         qe[64 * h2:64 * h2 + 64, hp, 64 * ch:64 * ch + 64],
                                         start=False, stop=(ch == 1 and hp == 1), skip_group_check=True)
                            if ch == 1:
                                ins.then_inc(ob.ready, 1)
                wait(kz_d.sem, kz_d.at(l, 1))
                for s in range(NS):
                    b = take(tb, f"SU{s}")
                    for hp in range(2):
                        ins = mm(b[:, 256 * hp:256 * hp + 256], kz[:, s, 128 * hp:128 * hp + 128], gltok[0:NS, 2, 256 + 256 * hp:512 + 256 * hp], start=True, stop=True)
                    ins.then_inc(tb.ready, 1)
                head_squares(1)
                wait(s_state.sem, s_state.at(l, 8))
                for h2 in range(2):
                    b = take(ob, f"gos{h2}")
                    for hp in range(2):
                        for s in range(NS):
                            ins = mm(b[:, 8 * hp + s:8 * hp + s + 1], Sst[64 * h2:64 * h2 + 64, s, hp, :], qs[64 * h2:64 * h2 + 64, hp, s:s + 1], start=True, stop=True)
                    ins.then_inc(ob.ready, 1)
                head_squares(2)

                wait(ob.done, ob.emptied(l, "so"))
                wait(og_d.sem, og_d.at(l, 3))
                for i in range(4):
                    w = tile_in(T_UP + i)
                    for n in range(2):
                        chunk(f"up{4 * i + 2 * n}", w, n, lambda k: onT[:, k, :], kn=4)
                        chunk(f"up{4 * i + 2 * n + 1}", lambda k, n: w(4 + k, n), n, lambda k: ogT[:, k, :], kn=4)
                wait(up_m.sem, up_m.at(l, 8))
                for i in range(4):
                    project([f"out{2 * i}", f"out{2 * i + 1}"], T_OUT + i, mv=lambda k: mgT[:, k, :])

                def norm(i, res):
                    wait(res.sem, res.at(l, 8))
                    b = take(sc, f"ln{i + 1}m")
                    for c in range(KD):
                        ins = mm(b[:, 0:NT], ones, hT[:, c, :], start=(c == 0), stop=(c == KD - 1))
                    ins.then_inc(sc.ready, 1)
                    wait(ln_sq.sem, ln_sq.at(l, i + 1))
                    b = take(sc, f"ln{i + 1}v")
                    for c in range(KD):
                        ins = mm(b[:, 0:NT], ones, sq[:, c, :], start=(c == 0), stop=(c == KD - 1))
                    ins.then_inc(sc.ready, 1)

                norm(0, res1)
                wait(h_ready.sem, h_ready.at(l, 2))
                for i in range(16):
                    project([f"m1_{2 * i}", f"m1_{2 * i + 1}"], T_M1 + i)
                wait(m1_sq.sem, m1_sq.at(l, 32))
                for cg in range(4):
                    for kg in range(4):
                        w = tile_in(T_M2 + 4 * cg + kg)
                        for n in range(2):
                            ins = chunk(f"m2_{2 * cg + n}", w, n, lambda k: hid[:, 8 * kg + k, :], free=(kg == 0), first=(kg == 0), last=(kg == 3))
                        if kg < 3:
                            ins.then_inc(m2_part.sem, 1)
                norm(1, res2)

            pe.wait_ge(h_ready.sem, LAYERS * 2 + 1)
            for n in range(6):
                g, half = n // 2, n % 2
                c0, m = TG[g]
                if n >= 2:
                    pe.wait_ge(ini["trc"], 6 + n)
                for c in range(4):
                    ins = tr(tb.banks[n % 2][0:m, 128 * c:128 * c + 128], hT[:, 4 * half + c, c0:c0 + m], 0, 128)
                ins.then_inc(ini["tr"], 1)

        @block.scalar
        def _(act):
            A_ = nc.scalar.activation
            act.preload_act_table_set("natural_log_exp_and_others")
            act.sem_inc(acc.done, 2)
            act.sem_inc(sc.done, 2)
            act.sem_inc(ob.done, 2)
            act.wait_ge(ini["sum"], 1)
            A_(mu, sc.banks[0][:, 0:NT], ACT.Copy, scale=1.0 / D).then_inc(ini["mu"], 1)
            act.wait_ge(ini["cen"], 1)
            A_(sq[:, :, :], hT[:, :, :], ACT.Square).then_inc(ini["sq"], 1)
            act.wait_ge(ini["var"], 1)
            A_(rs, sc.banks[1][:, 0:NT], ACT.Ln, scale=1.0 / D, bias=epsc).then_inc(ini["rs"], 1)
            act.wait_ge(ini["rs"], 1)
            A_(rs, rs, ACT.Exp, scale=-0.5).then_inc(ini["rs"], 1)

            with act.Fori(0, LAYERS) as l:
                links = [0]

                def link(ins):
                    links[0] += 1
                    ins.then_inc(act_link.sem, 1)
                    act.wait_ge(act_link.sem, act_link.at(l, links[0]))

                def evac(name, dst, func=ACT.Copy, m=128, **kw):
                    act.wait_ge(acc.ready, acc.filled(l, name))
                    A_(dst, acc.bank(name)[0:m, 0:NT], func, **kw).then_inc(acc.done, 1)

                for i in range(4):
                    evac(f"q{i}", qT[:, i, :])
                for i in range(6):
                    evac(f"kv{i}", kvT[:, i, :])
                for i in range(4):
                    evac(f"gla{i}", glT[:, i, :])
                act.wait_ge(ini["zero"], 7)
                act.wait_ge(acc.ready, acc.filled(l, "small"))
                link(A_(small[0:RANK, :], acc.bank("small")[0:RANK, 0:NT], ACT.Copy))
                A_(gateT[:, :], acc.bank("small")[32:56, 0:NT], ACT.Copy).then_inc(acc.done, 1)
                for s in range(NS):
                    act.wait_ge(cache_in[s % 2].sem, cache_in[s % 2].at(l, 48 * (s // 2 + 1)))
                    A_(Vs[:, 0, s, :, :], stg[:, s % 2, :, 384:512], ACT.Copy).then_inc(val_copied.sem, 1)
                    if s < 4:
                        evac(f"gla{4 + s}", glT[:, 4 + s, :])
                    else:
                        i = s - 4
                        act.wait_ge(acc.ready, acc.filled(l, f"gr{i}"))
                        link(A_(gre[:, i, :], acc.bank(f"gr{i}")[:, 0:NT], ACT.Exp, scale=-1.0))
                        A_(grT[:, i, :], acc.bank(f"gr{i}")[:, 0:NT], ACT.Copy).then_inc(acc.done, 1)
                act.wait_ge(s_max.sem, s_max.at(l, 1))
                for br in range(2):
                    A_(P64[:, br, :], sc.bank(f"ssc{br}")[0:64, 0:NKEY], ACT.Exp, scale=SCALE, bias=s64[:, 3 + br:4 + br],
                       accum_out=s64[:, 6 + br:7 + br]).then_inc(sc.done, 1)
                act.wait_ge(tb.done, tb.emptied(l, "gate"))
                A_(gates[:, :, :], gates[:, :, :], ACT.Exp, scale=-1.0).then_inc(gate_exp.sem, 1)
                for j, name in enumerate(("hidk", "hidv")):
                    act.wait_ge(sc.ready, sc.filled(l, name))
                    b = sc.bank(name)
                    link(A_(hb[:, j:j + 1], b[:, 272:273], ACT.Copy))
                    A_(hx[:, j, :], b[:, 0:270], ACT.Identity, bias=hb[:, j:j + 1]).then_inc(sc.done, 1)
                    act.wait_ge(hid_u.sem, hid_u.at(l, j + 1))
                    A_(hy, hy, ACT.Exp, scale=-2.0 * GELU_C).then_inc(hid_e.sem, 1)

                def gate_sigmoid(i):
                    m = mgT[:, i, :]
                    evac(f"mg{i}", m, ACT.Exp, scale=-1.0)
                    act.wait_ge(acc.done, acc.emptied(l, f"mg{i}"))
                    link(A_(m, m, ACT.Ln, bias=1.0))
                    A_(m, m, ACT.Exp, scale=-1.0).then_inc(mg_sig.sem, 1)

                gate_sigmoid(0)
                gate_sigmoid(1)
                for t in range(2):
                    for g in range(GROUPS):
                        act.wait_ge(sc.ready, sc.filled(l, f"csc{t}{g}"))
                        A_(CS[:, t, 4 * g:4 * g + 4, :], sc.bank(f"csc{t}{g}")[:, 0:60].rearrange("p (h k) -> p h k", h=4), ACT.Copy).then_inc(sc.done, 1)
                for t in range(2):
                    act.wait_ge(c_shift.sem, c_shift.at(l, t + 1))
                    A_(CS[:, t, :, :], CS[:, t, :, :], ACT.Exp, scale=SCALE).then_inc(c_exp.sem, 1)
                act.wait_ge(s_cmax.sem, s_cmax.at(l, 1))
                A_(C64[:, :], sc.bank("ssc2")[0:64, 0:NWIN], ACT.Exp, scale=SCALE, bias=s64[:, 5:6],
                   accum_out=s64[:, 8:9]).then_inc(sc.done, 1)
                def unit_exp(u):
                    n = 128 * (u // 8 + 1)
                    act.wait_ge(u_max.sem, u_max.at(l, u + 1))
                    if u >= 2:
                        act.wait_ge(tb.ready, tb.filled(l, f"pt{u - 2}"))
                    b = sc.bank(f"sc{u}")
                    A_(PS[:, u % 2, 0, 0:n], b[:, 0:n], ACT.Exp, scale=SCALE, bias=st[:, u % 2, 2:3],
                       accum_out=st[:, u % 2, 4:5]).then_inc(u_half.sem, 1)
                    A_(PS[:, u % 2, 1, 0:n], b[:, 256:256 + n], ACT.Exp, scale=SCALE, bias=st[:, u % 2, 3:4],
                       accum_out=st[:, u % 2, 5:6]).then_inc(sc.done, 1)

                for k in range(18):
                    if k < 16:
                        unit_exp(k)
                    if k >= 3 and k % 2 == 1:
                        n = (k - 3) // 2
                        act.wait_ge(ob.ready, ob.filled(l, f"o{n}"))
                        A_(onT[:, n % 4, 128 * (n // 4):128 * (n // 4) + 128], ob.bank(f"o{n}")[:, 0:128], ACT.Copy).then_inc(ob.done, 1)
                    if k < 14:
                        if k == 10:
                            act.wait_ge(gla_silu.sem, gla_silu.at(l, 1))
                        gate_sigmoid(k + 2)
                act.wait_ge(ob.ready, ob.filled(l, "so"))
                for g in range(2):
                    ins = A_(onT[64 * g:64 * g + 64, :, SEQ:NT].rearrange("p c s -> p s c"),
                             ob.bank("so")[64 * g:64 * g + 64, 32 * g:32 * g + 32].rearrange("p (s c) -> p s c", s=NS), ACT.Copy)
                    if g == 0:
                        link(ins)
                    else:
                        ins.then_inc(ob.done, 1)
                act.wait_ge(tb.done, tb.emptied(l, "la2"))
                link(A_(lla[:, :, :], xla[:, :, :], ACT.Abs))
                link(A_(lla[:, :, :], lla[:, :, :], ACT.Exp, scale=-1.0))
                A_(lla[:, :, :], lla[:, :, :], ACT.Ln, bias=1.0).then_inc(la_e.sem, 1)
                act.wait_ge(tb.done, tb.emptied(l, "elas"))
                A_(ela[:, :, :], ela[:, :, :], ACT.Exp, scale=1.0 / TAU).then_inc(ela_d.sem, 1)

                def rms_squares(i):
                    n = 512 if i < 2 else 32
                    c0, m = TG[i]
                    if i > 0:
                        act.wait_ge(sc.ready, sc.filled(l, f"rms{i - 1}"))
                    for h2 in range(2):
                        name = f"go{i}{h2}" if i < 2 else f"gos{h2}"
                        act.wait_ge(ob.ready, ob.filled(l, name))
                        o = ob.bank(name)[:, 0:n // 2].rearrange("p (h t) -> p h t", h=2)
                        ins = A_(osq[:, 0:n].rearrange("p (h t) -> p h t", h=4)[:, h2:4:2, :], o, ACT.Square)
                        if h2 == 0:
                            link(ins)
                        else:
                            ins.then_inc(r_sq.sem, 1)
                        A_(ogT[:, h2:4:2, c0:c0 + m], o, ACT.Copy).then_inc(ob.done, 1)

                def rms_scale(i):
                    n = 512 if i < 2 else 32
                    act.wait_ge(sc.ready, sc.filled(l, f"rms{i}"))
                    if i > 0:
                        act.wait_ge(og_d.sem, og_d.at(l, i))
                    A_(rr[:, 0:n], sc.bank(f"rms{i}")[:, 0:n], ACT.Ln, scale=1.0 / DV, bias=epsc).then_inc(sc.done, 1)
                    act.wait_ge(sc.done, sc.emptied(l, f"rms{i}"))
                    A_(rr[:, 0:n], rr[:, 0:n], ACT.Exp, scale=-0.5).then_inc(r_rs.sem, 1)

                for t in range(2):
                    act.wait_ge(sc.ready, sc.filled(l, f"gB{t}"))
                    if t == 1:
                        rms_squares(0)
                        act.wait_ge(g_q.sem, g_q.at(l, 1))
                        act.wait_ge(g_state.sem, g_state.at(l, 2))
                    B = sc.bank(f"gB{t}")[:, :].rearrange("p (h m n) -> p h m n", h=2, m=2)
                    link(A_(EB[:, 0, :, :], B[:, :, 0, :], ACT.Exp))
                    link(A_(EB[:, 1, :, :], B[:, :, 1, :], ACT.Exp))
                    A_(EB[:, 2, :, :], B[:, :, 1, :], ACT.Exp, scale=-1.0).then_inc(sc.done, 1)
                    act.wait_ge(tb.done, tb.emptied(l, f"aft{t}"))
                    A_(kd, kd, ACT.Exp).then_inc(g_ea.sem, 1)
                rms_scale(0)
                rms_squares(1)
                rms_scale(1)
                rms_squares(2)
                rms_scale(2)
                for i in range(16):
                    if i >= 2:
                        act.wait_ge(up_m.sem, up_m.at(l, i // 2))
                    evac(f"up{i}", upb[:, i % 2, :])
                for i in range(8):
                    if i >= 2:
                        act.wait_ge(res1.sem, res1.at(l, i - 1))
                    evac(f"out{i}", yb[:, i % 2, :])

                def norm(i):
                    act.wait_ge(sc.ready, sc.filled(l, f"ln{i + 1}m"))
                    A_(mu, sc.bank(f"ln{i + 1}m")[:, 0:NT], ACT.Copy, scale=1.0 / D).then_inc(sc.done, 1)
                    act.wait_ge(ln_cen.sem, ln_cen.at(l, i + 1))
                    A_(sq[:, :, :], hT[:, :, :], ACT.Square).then_inc(ln_sq.sem, 1)
                    act.wait_ge(sc.ready, sc.filled(l, f"ln{i + 1}v"))
                    A_(rs, sc.bank(f"ln{i + 1}v")[:, 0:NT], ACT.Ln, scale=1.0 / D, bias=epsc).then_inc(sc.done, 1)
                    act.wait_ge(sc.done, sc.emptied(l, f"ln{i + 1}v"))
                    A_(rs, rs, ACT.Exp, scale=-0.5).then_inc(ln_rs.sem, 1)

                norm(0)
                for i in range(32):
                    if i >= 2:
                        act.wait_ge(m1_sq.sem, m1_sq.at(l, i - 1))
                    evac(f"m1_{i}", yb[:, i % 2, :], ACT.Relu)
                for i in range(8):
                    if i >= 2:
                        act.wait_ge(res2.sem, res2.at(l, i - 1))
                    else:
                        act.wait_ge(m1_sq.sem, m1_sq.at(l, 31 + i))
                    evac(f"m2_{i}", yb[:, i % 2, :])
                norm(1)
                assert links[0] == act_link.per, links[0]

        @block.vector
        def _(dve):
            V = nc.vector
            dve.sem_inc(tb.done, 2)
            dve.sem_inc(mixers_done.sem, 1)
            for n in range(6):
                g, half = n // 2, n % 2
                c0, m = TG[g]
                dve.wait_ge(ini["tr"], n + 1)
                V.tensor_copy(hT[:, 4 * half:4 * half + 4, c0:c0 + m],
                              tb.banks[n % 2][:, :].rearrange("p (c t) -> p c t", c=4)[:, :, 0:m]).then_inc(ini["trc"], 1)
            dve.wait_ge(ini["tr"], 7)
            V.tensor_copy(lv[:, :], tb.banks[0][:, 0:V_N]).then_inc(ini["trc"], 1)

            def bc(a, n):
                return a[:, None, :].to_broadcast([128, n, NT])

            dve.wait_ge(ini["mu"], 1)
            V.tensor_tensor(hT[:, :, :], hT[:, :, :], bc(mu, KD), ALU.subtract).then_inc(ini["cen"], 1)
            dve.wait_ge(ini["rs"], 2)
            dve.wait_ge(ini["sq"], 1)
            V.tensor_tensor(hT[:, :, :], hT[:, :, :], bc(rs, KD), ALU.mult).then_inc(ini["cen"], 1)
            dve.wait_ge(ini["cen"], 2)
            for c in range(KD):
                ins = V.tensor_scalar(hT[:, c, :], hT[:, c, :], lv[:, c:c + 1], lv[:, 8 + c:9 + c], ALU.mult, ALU.add)
                ins.then_inc(h_ready.sem if c == KD - 1 else ini["cen"], 1)

            with dve.Fori(0, LAYERS) as l:
                links = [0]

                def link(ins):
                    links[0] += 1
                    ins.then_inc(dve_link.sem, 1)
                    dve.wait_ge(dve_link.sem, dve_link.at(l, links[0]))

                def tr_in(name):
                    dve.wait_ge(tb.ready, tb.filled(l, name))
                    return tb.bank(name)

                b = tr_in("vec")
                dve.wait_ge(h_ready.sem, h_ready.at(l, 1))
                V.tensor_copy(lv[:, :], b[:, 0:V_N]).then_inc(tb.done, 1)
                cos, sin = cst[:, C_COS:C_COS + NT], cst[:, C_SIN:C_SIN + NT]
                for i in range(6):
                    b = tr_in(f"rope{i}")
                    src, dst = (qT[:, i, :], qR[:, i, :]) if i < 4 else (kvT[:, 2 * (i - 3), :],) * 2
                    link(V.tensor_tensor(tmpA[:, :], b[:, 0:NT], sin, ALU.mult))
                    V.tensor_tensor(dst, src, cos, ALU.mult).then_inc(tb.done, 1)
                    dve.wait_ge(tb.done, tb.emptied(l, f"rope{i}"))
                    V.tensor_tensor(dst, dst, tmpA[:, :], ALU.add).then_inc(q_rot.sem, 1)
                    dve.wait_ge(q_rot.sem, q_rot.at(l, i + 1))
                dve.wait_ge(ini["zero"], 7)
                for r, q in enumerate((qT, qR)):
                    for g in range(2):
                        dst = Qz[64 * g:64 * g + 64, r, :, :].rearrange("p s x -> p (s x)")[:, 32 * g:32 * g + 7 * 68 + 4]
                        base = Qz[64 * g:64 * g + 64, r, :, :].rearrange("p s x -> p (s x)")
                        for s in range(NS):
                            o0 = 64 * s + 32 * g + 4 * s
                            ins = V.tensor_copy(base[:, o0:o0 + 4], q[64 * g:64 * g + 64, :, SEQ + s])
                            if (r, g, s) == (1, 1, NS - 1):
                                ins.then_inc(s_qz.sem, 1)
                            else:
                                links[0] += 1
                                ins.then_inc(dve_link.sem, 1)
                dve.wait_ge(stored, l * (16 * STORES) + 16)
                def token_major(kind, dst):
                    for i in range(6):
                        b = tr_in(f"{kind}{i}")
                        g, a = i // 2, i % 2
                        m, n = TG[g][1], (256 if a else 512)
                        V.tensor_copy(dst[0:m, g, 512 * a:512 * a + n], b[0:m, 0:n]).then_inc(tb.done, 1)

                token_major("kvt", kvtok)
                for j in range(2):
                    for g in range(2):
                        for r in range(2):
                            ins = V.tensor_copy(cmpT[64 * r:64 * r + 64, j, g, NS, :], kvT[64 * g:64 * g + 64, j, r:SEQ:2])
                            if (j, g, r) == (1, 1, 1):
                                ins.then_inc(pairs.sem, 1)
                            else:
                                links[0] += 1
                                ins.then_inc(dve_link.sem, 1)
                for s in range(NS):
                    b = tr_in(f"pairs{s}")
                    V.tensor_copy(cmpT[:, :, :, s, :], b[:, :].rearrange("p (j g i) -> p j g i", j=2, g=2)).then_inc(tb.done, 1)
                    b = tr_in(f"keys{s}")
                    if s >= 2:
                        dve.wait_ge(s_keys.sem, s_keys.at(l, s - 1))
                    link(V.tensor_copy(kTs[:, s % 2, :, PAST:NKEY], kvT[:, 2:6:2, SEQ + s:SEQ + s + 1]))
                    V.tensor_copy(kTs[:, s % 2, :, 0:PAST], b[:, :].rearrange("p (r k) -> p r k", r=2)).then_inc(tb.done, 1)
                token_major("glt", gltok)
                for br in range(2):
                    dve.wait_ge(sc.ready, sc.filled(l, f"ssc{br}"))
                    link(V.tensor_reduce(s64[:, br:br + 1], sc.bank(f"ssc{br}")[0:64, 0:NKEY], AX, ALU.max))
                V.tensor_scalar(s64[:, 3:5], s64[:, 0:2], -SCALE, None, ALU.mult).then_inc(s_max.sem, 1)
                b = tr_in("gate")
                for g, (c0, m) in enumerate(TG):
                    ins = V.tensor_copy(gates[0:m, g, :], b[0:m, 24 * g:24 * g + 24])
                    if g < 2:
                        link(ins)
                    else:
                        ins.then_inc(tb.done, 1)
                dve.wait_ge(gate_exp.sem, gate_exp.at(l, 1))
                link(V.tensor_scalar(gates[:, :, :], gates[:, :, :], 1.0, None, ALU.add))
                V.reciprocal(gates[:, :, :], gates[:, :, :]).then_inc(gate_sig.sem, 1)
                dve.wait_ge(acc.done, acc.emptied(l, "gr3"))
                link(V.tensor_scalar(gre, gre, 1.0, None, ALU.add))
                link(V.reciprocal(gre, gre))
                V.tensor_tensor(grT[:, :, :], grT[:, :, :], gre, ALU.mult).then_inc(gla_silu.sem, 1)
                for j in range(2):
                    dve.wait_ge(sc.done, sc.emptied(l, ("hidk", "hidv")[j]))
                    x = hx[:, j, :]
                    if j == 1:
                        dve.wait_ge(hid_g.sem, hid_g.at(l, 1))
                    link(V.tensor_tensor(hy, x, x, ALU.mult))
                    link(V.tensor_scalar(hy, hy, 0.044715, 1.0, ALU.mult, ALU.add))
                    link(V.tensor_tensor(hy, hy, x, ALU.mult))
                    V.tensor_scalar(hy, hy, -50.0, None, ALU.max).then_inc(hid_u.sem, 1)
                    dve.wait_ge(hid_e.sem, hid_e.at(l, j + 1))
                    link(V.tensor_scalar(hy, hy, 1.0, None, ALU.add))
                    link(V.reciprocal(hy, hy))
                    V.tensor_tensor(x, x, hy, ALU.mult).then_inc(hid_g.sem, 1)
                b = tr_in("kcmp")
                V.tensor_copy(kc[:, :], b[:, 0:135]).then_inc(tb.done, 1)
                for i in range(3):
                    b = tr_in(f"vcmp{i}")
                    n = min(4, 9 - 4 * i)
                    V.tensor_copy(vc[:, 4 * i:4 * i + n, :], b[0:NWIN, 0:128 * n].rearrange("p (s d) -> p s d", d=128)).then_inc(tb.done, 1)
                def heads(a, w):
                    return a[:, :, None].to_broadcast([128, 8, w])

                for t in range(2):
                    S = CS[:, t, :, :]
                    add = cst[:, C_CADD + 15 * t:C_CADD + 15 * t + 15][:, None, :].to_broadcast([128, 4, NWIN])
                    for g in range(GROUPS):
                        dve.wait_ge(sc.done, sc.emptied(l, f"csc{t}{g}"))
                        ins = V.tensor_tensor(S[:, 4 * g:4 * g + 4, :], S[:, 4 * g:4 * g + 4, :], add, ALU.add)
                        links[0] += 1
                        ins.then_inc(dve_link.sem, 1)
                    dve.wait_ge(dve_link.sem, dve_link.at(l, links[0]))
                    link(V.tensor_reduce(cst8[:, t, 0, :], S, AX, ALU.max))
                    V.tensor_tensor(S, S, heads(cst8[:, t, 0, :], NWIN), ALU.subtract).then_inc(c_shift.sem, 1)
                for t in range(2):
                    S = CS[:, t, :, :]
                    dve.wait_ge(c_exp.sem, c_exp.at(l, t + 1))
                    live = cst[:, C_C01 + 15 * t:C_C01 + 15 * t + 15][:, None, :].to_broadcast([128, 8, NWIN])
                    link(V.tensor_tensor(S, S, live, ALU.mult))
                    link(V.tensor_reduce(cst8[:, t, 1, :], S, AX, ALU.add))
                    link(V.tensor_scalar(cst8[:, t, 1, :], cst8[:, t, 1, :], 1e-30, None, ALU.max))
                    link(V.reciprocal(cst8[:, t, 1, :], cst8[:, t, 1, :]))
                    link(V.tensor_tensor(cst8[:, t, 2, :], cst8[:, t, 1, :], gates[:, t, 0:24:3], ALU.mult))
                    V.tensor_tensor(S, S, heads(cst8[:, t, 2, :], NWIN), ALU.mult).then_inc(c_prob.sem, 1)
                dve.wait_ge(sc.ready, sc.filled(l, "ssc2"))
                link(V.tensor_reduce(s64[:, 2:3], sc.bank("ssc2")[0:64, 0:NWIN], AX, ALU.max))
                V.tensor_scalar(s64[:, 5:6], s64[:, 2:3], -SCALE, None, ALU.mult).then_inc(s_cmax.sem, 1)

                def unit_max(u):
                    t = u // 8
                    dve.wait_ge(sc.ready, sc.filled(l, f"sc{u}"))
                    b = sc.bank(f"sc{u}")[:, :].rearrange("p (r k) -> p r k", r=2)
                    diag = b[:, :, 128 * t:128 * t + 128]
                    mask = cst[:, C_CAUS:C_CAUS + 128][:, None, :].to_broadcast([128, 2, 128])
                    link(V.tensor_tensor(diag, diag, mask, ALU.add))
                    link(V.tensor_reduce(st[:, u % 2, 0:2], b[:, :, 0:128 * (t + 1)], AX, ALU.max))
                    V.tensor_scalar(st[:, u % 2, 2:4], st[:, u % 2, 0:2], -SCALE, None, ALU.mult).then_inc(u_max.sem, 1)

                def unit_prob(u):
                    t, c, g = u // 8, (u % 8) // 2, u % 2
                    n, h = 128 * (t + 1), 4 * g + c
                    dve.wait_ge(u_half.sem, u_half.at(l, u + 1))
                    dve.wait_ge(sc.done, sc.emptied(l, f"sc{u}"))
                    link(V.reciprocal(st[:, u % 2, 4:6], st[:, u % 2, 4:6]))
                    link(V.tensor_tensor(st[:, u % 2, 6:8], st[:, u % 2, 4:6], gates[:, t, 3 * h + 1:3 * h + 3], ALU.mult))
                    link(V.tensor_scalar(PS[:, u % 2, 0, 0:n], PS[:, u % 2, 0, 0:n], st[:, u % 2, 6:7], None, ALU.mult))
                    V.tensor_scalar(PS[:, u % 2, 1, 0:n], PS[:, u % 2, 1, 0:n], st[:, u % 2, 7:8], None, ALU.mult).then_inc(u_prob.sem, 1)

                def compressed_in(t):
                    if t == 1:
                        dve.wait_ge(ob.ready, ob.filled(l, "o3"))
                    for a in range(2):
                        b = tr_in(f"pc{t}{a}")
                        V.tensor_copy(PTc[:, 4 * a:4 * a + 4, :], b[0:NWIN, :].rearrange("p (h q) -> p h q", h=4)).then_inc(tb.done, 1)

                def prob_in(u):
                    b = tr_in(f"pt{u}")
                    n = 256 * (u // 8 + 1)
                    if u >= 2 and u % 2 == 0:
                        dve.wait_ge(pv_done.sem, pv_done.at(l, u // 2))
                    elif u >= 3:
                        dve.wait_ge(ob.ready, ob.filled(l, f"o{(u - 2) // 2}"))
                    V.tensor_copy(PT[:, u % 2, 0:n // 128, :], b[:, 0:n].rearrange("p (a q) -> p a q", q=128)).then_inc(tb.done, 1)

                for k in range(18):
                    if k == 2:
                        compressed_in(0)
                    if k >= 2:
                        prob_in(k - 2)
                    if k == 10:
                        compressed_in(1)
                    if 1 <= k <= 16:
                        unit_prob(k - 1)
                    if k < 16:
                        unit_max(k)

                dve.wait_ge(sc.done, sc.emptied(l, "ssc2"))
                dve.wait_ge(gate_in.sem, gate_in.at(l, 32))
                link(V.reciprocal(s64[:, 6:9], s64[:, 6:9]))
                link(V.tensor_tensor(s64[:, 9:10], s64[:, 8:9], gate64[:, 0:1], ALU.mult))
                link(V.tensor_tensor(s64[:, 10:12], s64[:, 6:8], gate64[:, 1:3], ALU.mult))
                link(V.tensor_scalar(C64[:, :], C64[:, :], s64[:, 9:10], None, ALU.mult))
                link(V.tensor_scalar(P64[:, 0, :], P64[:, 0, :], s64[:, 10:11], None, ALU.mult))
                V.tensor_scalar(P64[:, 1, :], P64[:, 1, :], s64[:, 11:12], None, ALU.mult).then_inc(s_prob.sem, 1)
                dve.wait_ge(s_prob.sem, s_prob.at(l, 1))
                link(V.tensor_scalar(An[:, 0, :], cst[0:64, C_M8:C_M8 + 8], P64[:, 0, PAST:NKEY], None, ALU.mult))
                V.tensor_scalar(An[:, 1, :], cst[0:64, C_M8:C_M8 + 8], P64[:, 1, PAST:NKEY], None, ALU.mult).then_inc(s_anew.sem, 1)
                b = tr_in("spt")
                link(V.tensor_copy(PTs[:, :, :], b[:, 0:256].rearrange("p (n r) -> p n r", n=4)))
                V.tensor_copy(PTcs[:, :], b[0:NWIN, 256:320]).then_inc(tb.done, 1)
                b = tr_in("snew")
                V.tensor_copy(Pn[:, :, :], b[0:8, 0:128].rearrange("p (r n) -> p r n", r=2)).then_inc(tb.done, 1)

                b = tr_in("la01")
                V.tensor_copy(xla[:, 0:2, :], b[:, :].rearrange("p (g n) -> p g n", g=2)).then_inc(tb.done, 1)
                b = tr_in("la2")
                V.tensor_copy(xla[0:NS, 2, :], b[0:NS, 0:256]).then_inc(tb.done, 1)
                dve.wait_ge(ob.ready, ob.filled(l, "so"))
                for s in range(NS):
                    links[0] += 1
                    V.tensor_scalar(kz[:, s, :], gltok[0:NS, 2, 0:256], cst[0:NS, C_KD + s:C_KD + s + 1], None, ALU.mult).then_inc(dve_link.sem, 1)
                V.tensor_scalar(qs[:, :, :], glT[:, 0:2, SEQ:NT], DK ** -0.5, None, ALU.mult).then_inc(kz_d.sem, 1)
                dve.wait_ge(la_e.sem, la_e.at(l, 1))
                V.scalar_tensor_tensor(xla[:, :, :], xla[:, :, :], 0.0, lla, ALU.min, ALU.subtract).then_inc(la_t.sem, 1)
                b = tr_in("elas")
                V.tensor_copy(ela[:, :, :], b[:, 0:16].rearrange("p (h s) -> p h s", h=2)).then_inc(tb.done, 1)

                def state(t, ch):
                    k = 2 * t + ch
                    b = tr_in(f"U{t}{ch}")
                    if k >= 2:
                        dve.wait_ge(ob.ready, ob.filled(l, f"go{(k - 1) // 2}1"))
                    for hp in range(2):
                        for h2 in range(2):
                            new = Sp[64 * h2:64 * h2 + 64, k % 2, hp, :]
                            upd = b[64 * h2:64 * h2 + 64, 256 * hp + 128 * h2:256 * hp + 128 * h2 + 128]
                            if k == 0:
                                ins = V.tensor_copy(new, upd)
                            else:
                                ins = V.scalar_tensor_tensor(new, Sp[64 * h2:64 * h2 + 64, (k - 1) % 2, hp, :],
                                                             EB[64 * h2:64 * h2 + 64, 0, hp, 64 * ch + 63:64 * ch + 64], upd, ALU.mult, ALU.add)
                            if hp + h2 < 2:
                                link(ins)
                            else:
                                ins.then_inc(tb.done, 1)
                    dve.wait_ge(tb.done, tb.emptied(l, f"U{t}{ch}"))
                    V.tensor_copy(st[:, 0, 0:1], Sp[:, k % 2, 0, 0:1]).then_inc(g_state.sem, 1)

                for t in range(2):
                    dve.wait_ge(sc.done, sc.emptied(l, f"gB{t}"))
                    q, k = glT[:, 0:2, 128 * t:128 * t + 128], glT[:, 2:4, 128 * t:128 * t + 128]
                    b = tr_in(f"aft{t}")
                    V.tensor_copy(kd, b[:, 0:256]).then_inc(tb.done, 1)
                    if t == 1:
                        dve.wait_ge(ob.ready, ob.filled(l, "go01"))
                    link(V.scalar_tensor_tensor(qe, q, DK ** -0.5, EB[:, 0, :, :], ALU.mult, ALU.mult))
                    link(V.scalar_tensor_tensor(qm, q, DK ** -0.5, EB[:, 1, :, :], ALU.mult, ALU.mult))
                    link(V.tensor_tensor(km, k, EB[:, 2, :, :], ALU.mult))
                    dve.wait_ge(g_ea.sem, g_ea.at(l, t + 1))
                    V.tensor_tensor(kd, kd, gltok[:, t, 0:256], ALU.mult).then_inc(g_q.sem, 1)
                    for h2 in range(2):
                        b = tr_in(f"gA{t}{h2}")
                        V.tensor_tensor(gAs[:, h2:4:2, :], b[:, 0:256].rearrange("p (h t) -> p h t", h=2),
                                        cst[:, C_GM:C_GM + 128][:, None, :].to_broadcast([128, 2, 128]), ALU.mult).then_inc(tb.done, 1)
                    state(t, 0)
                    state(t, 1)
                dve.wait_ge(state_in.sem, state_in.at(l, 64))
                dve.wait_ge(ela_d.sem, ela_d.at(l, 1))
                for s in range(NS):
                    b = tr_in(f"SU{s}")
                    for hp in range(2):
                        for h2 in range(2):
                            S = Sst[64 * h2:64 * h2 + 64, s, hp, :]
                            upd = b[64 * h2:64 * h2 + 64, 256 * hp + 128 * h2:256 * hp + 128 * h2 + 128]
                            ins = V.scalar_tensor_tensor(S, S, ela[64 * h2:64 * h2 + 64, hp, s:s + 1], upd, ALU.mult, ALU.add)
                            if hp + h2 < 2:
                                links[0] += 1
                                ins.then_inc(dve_link.sem, 1)
                            else:
                                ins.then_inc(tb.done, 1)
                    dve.wait_ge(tb.done, tb.emptied(l, f"SU{s}"))
                    V.tensor_copy(st[:, 0, 0:1], Sst[:, s, 0, 0:1]).then_inc(s_state.sem, 1)
                for i in range(3):
                    c0, m = TG[i]
                    dve.wait_ge(ob.done, ob.emptied(l, f"go{i}1" if i < 2 else "gos1"))
                    dve.wait_ge(r_rs.sem, r_rs.at(l, i + 1))
                    o = ogT[:, :, c0:c0 + m]
                    r = rr[:, 0:4 * m].rearrange("p (h t) -> p h t", h=4)
                    link(V.tensor_tensor(o, o, r, ALU.mult))
                    V.scalar_tensor_tensor(o, o, lv[:, V_GN:V_GN + 1], grT[:, :, c0:c0 + m], ALU.mult, ALU.mult).then_inc(og_d.sem, 1)
                dve.wait_ge(og_d.sem, og_d.at(l, 3))
                V.tensor_copy(st[:, 0, 0:1], ogT[:, 0, 0:1]).then_inc(mixers_done.sem, 1)
                dve.wait_ge(mg_sig.sem, mg_sig.at(l, 16))
                for i in range(8):
                    for a in range(2):
                        dve.wait_ge(acc.done, acc.emptied(l, f"up{2 * i + a}"))
                        m = mgT[:, 8 * a + i, :]
                        link(V.tensor_tensor(m, m, upb[:, a, :], ALU.mult))
                    V.tensor_tensor(mgT[:, i, :], mgT[:, i, :], mgT[:, 8 + i, :], ALU.add).then_inc(up_m.sem, 1)

                def residual(name, res):
                    for i in range(8):
                        dve.wait_ge(acc.done, acc.emptied(l, f"{name}{i}"))
                        V.scalar_tensor_tensor(hT[:, i, :], hT[:, i, :], ALPHA, yb[:, i % 2, :], ALU.mult, ALU.add).then_inc(res.sem, 1)
                    dve.wait_ge(res.sem, res.at(l, 8))

                def norm(i, vg, vb):
                    dve.wait_ge(sc.done, sc.emptied(l, f"ln{i + 1}m"))
                    V.tensor_tensor(hT[:, :, :], hT[:, :, :], bc(mu, KD), ALU.subtract).then_inc(ln_cen.sem, 1)
                    dve.wait_ge(ln_rs.sem, ln_rs.at(l, i + 1))
                    link(V.tensor_tensor(hT[:, :, :], hT[:, :, :], bc(rs, KD), ALU.mult))
                    for c in range(KD):
                        ins = V.tensor_scalar(hT[:, c, :], hT[:, c, :], lv[:, vg + c:vg + c + 1], lv[:, vb + c:vb + c + 1], ALU.mult, ALU.add)
                        if c < KD - 1:
                            links[0] += 1
                            ins.then_inc(dve_link.sem, 1)
                        else:
                            ins.then_inc(h_ready.sem, 1)

                residual("out", res1)
                norm(0, V_L1G, V_L1B)
                for i in range(32):
                    dve.wait_ge(acc.done, acc.emptied(l, f"m1_{i}"))
                    V.tensor_tensor(hid[:, i, :], yb[:, i % 2, :], yb[:, i % 2, :], ALU.mult).then_inc(m1_sq.sem, 1)
                residual("m2_", res2)
                norm(1, V_L2G, V_L2B)
                assert links[0] == dve_link.per, links[0]

            for n in range(6):
                g, half = n // 2, n % 2
                m = TG[g][1]
                dve.wait_ge(ini["tr"], 8 + n)
                V.tensor_copy(xin[0:m, g, 512 * half:512 * half + 512], tb.banks[n % 2][0:m, :]).then_inc(ini["trc"], 1)


INS = ["x_prompt", "x_sample", "cache_nsa_kv", "cache_win_kv", "state_gla", "page_table", "ln_in_g", "ln_in_b", "w_in",
       "cmp_k_pe", "cmp_k_w1", "cmp_k_w2", "cmp_v_pe", "cmp_v_w1", "cmp_v_w2", "gla_w_a2", "gla_b_a", "gla_norm_g",
       "w_nsa_up", "w_gla_up", "w_out", "ln1_g", "ln1_b", "mlp_w1", "mlp_w2", "ln2_g", "ln2_b"]
OUTS = [("y_prompt", (1, SEQ, D)), ("y_sample", (NS, 1, D)), ("nsa_kv_prompt", (1, LAYERS, SEQ, 4, GROUPS, HD)),
        ("win_kv_prompt", (1, LAYERS, SEQ, 2, GROUPS, HD)), ("gla_state_prompt", (1, LAYERS, GH, DK, DV)),
        ("nsa_kv_sample", (NS, LAYERS, 1, 4, GROUPS, HD)), ("win_kv_sample", (NS, LAYERS, PAST, 2, GROUPS, HD)),
        ("gla_state_sample", (NS, LAYERS, GH, DK, DV))]


def constants(np):
    c = np.zeros((128, C_N), np.float32)
    i = np.arange(128)
    c[:, C_ID:C_ID + 128] = np.eye(128)
    c[:, C_ONE:C_ONE + 128] = 1.0
    for m in range(128):
        c[m + 32 if m % 64 < 32 else m - 32, C_ROT + m] = -1.0 if m % 64 < 32 else 1.0
    c[:, C_CAUS:C_CAUS + 128] = np.where(i[None, :] <= i[:, None], 0.0, NEG)
    same = i[:, None] // CH == i[None, :] // CH
    u, t = i[:, None], i[None, :]
    mid = t // CH * CH + CH // 2 - 1
    c[:, C_TRI:C_TRI + 128] = same * (u <= t) / TAU
    c[:, C_MID:C_MID + 128] = same * ((u <= t).astype(np.float32) - (u <= mid)) / TAU
    c[:, C_AFT:C_AFT + 128] = same * (u > t) / TAU
    c[:, C_GM:C_GM + 128] = same * (u <= t)
    half = HD // 2
    inv = np.float32(10000.0) ** (-np.arange(half, dtype=np.float32) / np.float32(half))
    pos = np.concatenate([np.arange(SEQ), np.full(NS, PAST)]).astype(np.float32)
    ang = (pos[None, :] * inv[i % half][:, None]).astype(np.float32)
    c[:, C_COS:C_COS + NT] = np.cos(ang)
    c[:, C_SIN:C_SIN + NT] = np.sin(ang)
    for tile in range(2):
        live = (np.arange(NWIN) * CSTR + CLEN - 1)[None, :] <= (tile * 128 + i)[:, None]
        c[:, C_CADD + 15 * tile:C_CADD + 15 * tile + 15] = np.where(live, 0.0, NEG)
        c[:, C_C01 + 15 * tile:C_C01 + 15 * tile + 15] = live
    for r in range(64):
        c[r, C_M8 + (r % 32) // 4] = 1.0
    for s in range(NS):
        c[s, C_KD + s] = 1.0
    c[:, C_EPS] = EPS
    return c


def kernel(**inputs):
    import numpy as np
    import concourse.bacc as bacc
    from concourse.bass_utils import run_bass_kernel_spmd

    nc = bacc.Bacc("TRN2", target_bir_lowering=False, num_devices=1)
    arrays = {f"in_{n}": np.ascontiguousarray(inputs[n]) for n in INS}
    arrays["in_consts"] = constants(np)
    A = {n[3:]: nc.dram_tensor(n, a.shape, mybir.dt.from_np(a.dtype), kind="ExternalInput").ap() for n, a in arrays.items()}
    O = {n: nc.dram_tensor(f"out_{n}", s, F32, kind="ExternalOutput").ap() for n, s in OUTS}
    build(nc, A, O)
    r = run_bass_kernel_spmd(nc, [arrays], core_ids=[0])
    return tuple(r.results[0][f"out_{n}"] for n, _ in OUTS)
```

```python
from contextlib import ExitStack

import concourse.bass as bass
from concourse import mybir

F32 = mybir.dt.float32
F32R = mybir.dt.float32r
I32 = mybir.dt.int32
ALU = mybir.AluOpType
ACT = mybir.ActivationFunctionType
AX = mybir.AxisListType.X

D = 1024
KD = D // 128
SEQ, NS = 256, 8
NT = SEQ + NS
LAYERS = 2
HEADS, GROUPS, HD = 8, 2, 64
HPG = HEADS // GROUPS
SLOTS = 6
SCALE = HD ** -0.5
NWIN = 15
CSTR, CLEN = 16, 32
PAST = 256
NKEY = PAST + 1
GH, DK, DV = 4, 64, 128
CH = 64
RANK = 16
TAU = 16.0
DFF = 4096
EPS = 1e-5
ALPHA = (2.0 * LAYERS) ** 0.25
NEG = -1e30
GELU_C = 0.7978845608028654
OFF_Q, OFF_KV, OFF_G = 0, 512, 1280
OFF_GQ, OFF_GK, OFF_GV, OFF_LR, OFF_GR, OFF_MG = 1304, 1560, 1816, 2328, 2344, 2856

C_ID, C_ONE, C_ROT, C_CAUS, C_TRI, C_MID, C_AFT, C_GM = (128 * i for i in range(8))
C_COS = 1024
C_SIN = C_COS + NT
C_CADD = C_SIN + NT
C_C01 = C_CADD + 2 * NWIN
C_M8 = C_C01 + 2 * NWIN
C_KD = C_M8 + 8
C_EPS = C_KD + 8
C_N = C_EPS + 1

V_L1G, V_L1B, V_L2G, V_L2B, V_GN, V_PEK, V_PEV, V_N = 0, 8, 16, 24, 32, 33, 49, 65


class Banks:

    def __init__(self, plan, ready, done, banks):
        self.plan, self.ready, self.done, self.banks = plan, ready, done, banks
        self.total = len(plan)
        self.at = {name: i for i, name in enumerate(plan)}
        assert len(self.at) == self.total

    def bank(self, name):
        return self.banks[self.at[name] % 2]

    def filled(self, l, name):
        return l * self.total + (self.at[name] + 1)

    def emptied(self, l, name):
        return l * self.total + (self.at[name] + 3)

    def free(self, l, name):
        return l * self.total + (2 + max(self.at[name] - 1, 0))


class Steps:

    def __init__(self, sem, per_layer):
        self.sem, self.per = sem, per_layer

    def at(self, l, n):
        return l * self.per + n


def unit_name(u):
    return f"unit{u}"


STORES = 12
LINKS = (274, 35)


def build(nc, A, O):
    RING = 4
    TILES = 61
    T_Q, T_KV, T_GLA, T_GR, T_CMP, T_MG, T_UP, T_OUT, T_M1, T_M2 = 0, 2, 5, 9, 11, 13, 21, 25, 29, 45

    acc_plan = ([f"q{i}" for i in range(4)] + [f"kv{i}" for i in range(6)] + [f"gla{i}" for i in range(4)] + ["small"] + [f"gla{i}" for i in range(4, 8)]
                + [f"gr{i}" for i in range(4)] + [f"mg{i}" for i in range(16)]
                + [f"up{i}" for i in range(16)] + [f"out{i}" for i in range(8)]
                + [f"m1_{i}" for i in range(32)] + [f"m2_{i}" for i in range(8)])
    t_plan = (["vec"] + [f"rope{i}" for i in range(6)] + [f"kvt{i}" for i in range(6)]
              + sum([[f"pairs{s}", f"keys{s}"] for s in range(NS)], []) + [f"glt{i}" for i in range(6)] + ["gate", "kcmp"] + [f"vcmp{i}" for i in range(3)]
              + ["la01", "la2", "pc00", "pc01", "pt0", "spt", "snew", "pt1", "elas", "aft0", "pt2", "pt3", "gA00", "gA01",
                 "pt4", "U00", "U01", "pt5", "pt6", "pt7", "aft1", "pt8", "pc10", "pc11", "pt9", "gA10", "gA11", "pt10", "U10",
                 "pt11", "SU0", "SU1", "pt12", "U11", "pt13", "SU2", "SU3", "pt14", "SU4", "SU5", "pt15", "SU6", "SU7"])
    sc_plan = (["ssc0", "ssc1", "hidk", "hidv", "csc00", "csc01", "csc10", "csc11", "ssc2"] + [f"sc{u}" for u in range(3)] + ["gB0"] + [f"sc{u}" for u in range(3, 9)]
               + ["gB1", "sc9", "rms0"] + [f"sc{u}" for u in range(10, 16)] + ["rms1", "rms2"] + ["ln1m", "ln1v", "ln2m", "ln2v"])
    o_plan = ["o0", "so", "o1", "o2", "go00", "go01", "o3", "o4", "o5", "go10", "go11", "o6", "o7", "gos0", "gos1"]

    with ExitStack() as ctx:
        def sb(name, shape, dt=F32):
            return ctx.enter_context(nc.sbuf_tensor(name, shape, dt))

        def pb(name):
            return ctx.enter_context(nc.psum_tensor(name, [128, 512], F32))

        def sem(name):
            return ctx.enter_context(nc.semaphore(name))

        with ExitStack() as shared:
            def part(name, shape):
                return shared.enter_context(nc.sbuf_tensor(name, shape, F32R))

            wlo = [part(f"wlo{i}", [128, KD, 256]) for i in range(RING)]
            whi = [part(f"whi{i}", [128, KD, 256]) for i in range(2)]
            h_parts = part("h_parts", [128, 2, KD, NT])
            hid_parts = part("hid_parts", [128, 2, 32, NT])
        wt = [sb(f"wt{i}", [128, 2048]) for i in range(RING)]
        Vs = sb("Vs", [128, 2, NS, 2, 128])
        mgT = sb("mgT", [128, 16, NT])
        BIG = sb("BIG", [128, 40 * NT + 3 * SLOTS * 128 + 3 * 768 + 2 * 1024])
        assert 64 * NT <= BIG.shape[1]
        h_hi, h_lo = h_parts[:, 0], h_parts[:, 1]
        hid_hi, hid_lo = hid_parts[:, 0], hid_parts[:, 1]
        cst = sb("cst", [128, C_N])
        ident, ones = cst[:, C_ID:C_ID + 128], cst[:, C_ONE:C_ONE + 128]
        epsc = cst[:, C_EPS:C_EPS + 1]
        ptab = sb("ptab", [1, 16], I32)
        hT = sb("hT", [128, KD, NT])
        wsm = sb("wsm", [128, KD, 56])
        small = sb("small", [32, NT])
        gateT = sb("gateT", [24, NT])
        AR = BIG[:, 0:40 * NT]
        used = [0]

        def ar(n):
            a = AR[:, used[0]:used[0] + n]
            used[0] += n
            return a

        qT = ar(4 * NT).rearrange("p (c t) -> p c t", c=4)
        qR = ar(4 * NT).rearrange("p (c t) -> p c t", c=4)
        kvT = ar(6 * NT).rearrange("p (c t) -> p c t", c=6)
        glT = ar(8 * NT).rearrange("p (c t) -> p c t", c=8)
        cmpT = ar(2 * 2 * 9 * 128).rearrange("p (j g s i) -> p j g s i", j=2, g=2, s=9)
        assert used[0] <= 40 * NT
        gtmp = cmpT.rearrange("p j g s i -> p (j g s i)")
        tused = [0]

        def tmp(n, rows=128):
            a = gtmp[0:rows, tused[0]:tused[0] + n]
            tused[0] += n
            assert tused[0] <= 4608
            return a

        grT = sb("grT", [128, 4, NT])
        sq = mgT[:, 8:16, :]
        gre = mgT[:, 12:16, :]
        kTs = sb("kTs", [128, 2, 2, NKEY])
        u0 = 40 * NT
        kvtok = BIG[:, u0:u0 + 3 * SLOTS * 128].rearrange("p (g n) -> p g n", g=3)
        u0 += 3 * SLOTS * 128
        gltok = BIG[:, u0:u0 + 3 * 768].rearrange("p (g n) -> p g n", g=3)
        u0 += 3 * 768
        stg = BIG[:, u0:u0 + 2048].rearrange("p (s r n) -> p s r n", s=2, r=2)
        stw = sb("stw", [128, 2, 2, 128])
        Sst = sb("Sst", [128, NS, 2, 128])
        Sp = sb("Sp", [128, 2, 2, 128])
        vecr = sb("vecr", [V_N, 128])
        lv = sb("lv", [128, V_N])
        wa2 = sb("wa2", [RANK + 1, 256])
        w2 = sb("w2", [128, 2, 64])
        gates = sb("gates", [128, 3, 24])
        gate64 = sb("gate64", [64, 3])
        tmpA = cmpT.rearrange("p j g s i -> p (j g s i)")[:, 0:NT]
        hb = sb("hb", [128, 2])
        kc = sb("kc", [128, 9 * NWIN])
        cv = sb("cv", [NWIN, (9 + 8) * 128])
        vc = cv[:, 0:9 * 128].rearrange("p (s d) -> p s d", s=9)
        PS = sb("PS", [128, 2, 2, 256])
        pflat = PS[:, :, :, :].rearrange("p u r k -> p (u r k)")
        hx = pflat[:, 0:540].rearrange("p (j n) -> p j n", j=2)
        hy = pflat[:, 540:810]
        PT = sb("PT", [128, 2, 4, 128])
        st = sb("st", [128, 2, 8])
        CS = sb("CS", [128, 2, 8, NWIN])
        cst8 = sb("cst8", [128, 2, 3, 8])
        PTc = cv[:, 9 * 128:17 * 128].rearrange("p (h q) -> p h q", h=8)
        onT = sb("onT", [128, 4, NT])
        ogT = glT[:, 4:8, :]
        Qz = sb("Qz", [128, 2, NS, 64])
        P64 = sb("P64", [64, 2, NKEY])
        C64 = sb("C64", [64, NWIN])
        s64 = sb("s64", [64, 12])
        PTs = sb("PTs", [128, 4, 64])
        PTcs = sb("PTcs", [NWIN, 64])
        An = sb("An", [64, 2, 8])
        Pn = sb("Pn", [8, 2, 64])
        xla = sb("xla", [128, 3, 256])
        lla = tmp(768).rearrange("p (g n) -> p g n", g=3)
        ela = sb("ela", [128, 2, 8])
        qs = sb("qs", [128, 2, 8])
        EB = tmp(768).rearrange("p (a h n) -> p a h n", a=3, h=2)
        kd = tmp(256)
        qe, qm, km = (tmp(256).rearrange("p (h n) -> p h n", h=2) for _ in range(3))
        gAs = tmp(512).rearrange("p (h n) -> p h n", h=4)
        osq = tmp(512)
        rr = tmp(512)
        kz = tmp(512, NS).rearrange("p (s n) -> p s n", s=2)
        upb = qT[:, 0:2, :]
        yb, mu, rs, musq = onT[:, 0:2, :], onT[:, 2, :], onT[:, 3, :], onT[:, 0, :]
        xin = mgT[:, 0:12, :].rearrange("p a b -> p (a b)")[:, 0:3072].rearrange("p (g f) -> p g f", g=3)

        acc = Banks(acc_plan, sem("acc_ready"), sem("acc_done"), [pb("acc0"), pb("acc1")])
        tb = Banks(t_plan, sem("tr_ready"), sem("tr_done"), [pb("tr0"), pb("tr1")])
        sc = Banks(sc_plan, sem("sc_ready"), sem("sc_done"), [pb("sc0"), pb("sc1")])
        ob = Banks(o_plan, sem("o_ready"), sem("o_done"), [pb("o0"), pb("o1")])

        w_landed = [sem(f"w_landed{i}") for i in range(RING)]
        m2_part = Steps(sem("m2_part"), 12)
        const_in = sem("const_in")
        x_in = sem("x_in")
        wsm_in = Steps(sem("wsm_in"), 32)
        vec_in = Steps(sem("vec_in"), 16 * 7)
        par_in = Steps(sem("par_in"), 16 * 4)
        cache_in = [Steps(sem(f"cache_in{i}"), 16 * 3 * 4) for i in range(2)]
        mixers_done = Steps(sem("mixers_done"), 1)
        val_in = Steps(sem("val_in"), 16 * NS)
        val_copied = Steps(sem("val_copied"), NS)
        state_in = Steps(sem("state_in"), 64)
        gate_in = Steps(sem("gate_in"), 32)
        stored = sem("stored")
        pe_passed, pool_passed, sp_passed = sem("pe_passed"), sem("pool_passed"), sem("sp_passed")

        ini = {n: sem("in_" + n) for n in ("tr", "trc", "sum", "mu", "cen", "sq", "var", "rs", "h", "zero")}
        dve_link = Steps(sem("dve_link"), 0)
        act_link = Steps(sem("act_link"), 0)
        DVE_LINKS, ACT_LINKS = LINKS
        dve_link.per, act_link.per = DVE_LINKS, ACT_LINKS
        h_ready = Steps(sem("h_ready"), 16)
        h_hi_d, h_lo_d = Steps(sem("h_hi_d"), 8), Steps(sem("h_lo_d"), 8)
        w_hi, w_lo = Steps(sem("w_hi"), TILES - T_M1), Steps(sem("w_lo"), TILES - T_M1)
        hid_hi_d = Steps(sem("hid_hi_d"), 32)
        vec_cols = Steps(sem("vec_cols"), 1)
        q_rot = Steps(sem("q_rot"), 6)
        gla_silu = Steps(sem("gla_silu"), 1)
        pairs = Steps(sem("pairs"), 1)
        gate_exp = Steps(sem("gate_exp"), 1)
        gate_sig = Steps(sem("gate_sig"), 1)
        hid_x = Steps(sem("hid_x"), 2)
        hid_u = Steps(sem("hid_u"), 2)
        hid_e = Steps(sem("hid_e"), 2)
        hid_g = Steps(sem("hid_g"), 2)
        mg_sig = Steps(sem("mg_sig"), 16)
        c_shift = Steps(sem("c_shift"), 2)
        c_exp = Steps(sem("c_exp"), 2)
        s_cmax = Steps(sem("s_cmax"), 1)
        u_half = Steps(sem("u_half"), 16)
        pv_done = Steps(sem("pv_done"), 8)
        c_prob = Steps(sem("c_prob"), 2)
        u_max = Steps(sem("u_max"), 16)
        u_exp = Steps(sem("u_exp"), 16)
        u_prob = Steps(sem("u_prob"), 16)
        s_qz = Steps(sem("s_qz"), 1)
        s_keys = Steps(sem("s_keys"), 7)
        s_max = Steps(sem("s_max"), 1)
        s_exp = Steps(sem("s_exp"), 1)
        s_prob = Steps(sem("s_prob"), 1)
        s_anew = Steps(sem("s_anew"), 1)
        la_e = Steps(sem("la_e"), 1)
        la_t = Steps(sem("la_t"), 1)
        ela_d = Steps(sem("ela_d"), 1)
        kz_d = Steps(sem("kz_d"), NS)
        qs_d = Steps(sem("qs_d"), 1)
        g_eb = Steps(sem("g_eb"), 2)
        g_ea = Steps(sem("g_ea"), 2)
        g_q = Steps(sem("g_q"), 2)
        g_state = Steps(sem("g_state"), 4)
        s_state = Steps(sem("s_state"), 8)
        r_sq = Steps(sem("r_sq"), 3)
        r_rs = Steps(sem("r_rs"), 3)
        og_d = Steps(sem("og_d"), 3)
        up_m = Steps(sem("up_m"), 8)
        res1 = Steps(sem("res1"), 8)
        res2 = Steps(sem("res2"), 8)
        hid_lo_d = Steps(sem("hid_lo_d"), 32)
        ln_var = Steps(sem("ln_var"), 2)
        ln_sq = Steps(sem("ln_sq"), 16)
        ln_sc = Steps(sem("ln_sc"), 16)
        ln_rs = Steps(sem("ln_rs"), 2)

        TG = [(0, 128), (128, 128), (256, NS)]
        block = ctx.enter_context(nc.Block())

        def tile_used(l, p):
            if T_CMP <= p < T_CMP + 2:
                return sc.ready, sc.filled(l, ("hidk", "hidv")[p - T_CMP])
            if p >= T_M2:
                cg, kg = (p - T_M2) // 4, (p - T_M2) % 4
                if kg < 3:
                    return m2_part.sem, m2_part.at(l, 3 * cg + kg + 1)
                return acc.ready, acc.filled(l, f"m2_{2 * cg + 1}")
            name = (f"q{2 * (p - T_Q) + 1}" if p < T_KV else f"kv{2 * (p - T_KV) + 1}" if p < T_GLA
                    else f"gla{2 * (p - T_GLA) + 1}" if p < T_GR else f"gr{2 * (p - T_GR) + 1}" if p < T_CMP
                    else f"mg{2 * (p - T_MG) + 1}" if p < T_UP else f"up{4 * (p - T_UP) + 3}" if p < T_OUT
                    else f"out{2 * (p - T_OUT) + 1}" if p < T_M1 else f"m1_{2 * (p - T_M1) + 1}")
            return acc.ready, acc.filled(l, name)

        @block.sync
        def _(sp):
            sp.dma_start(cst[:, :], A["consts"]).then_inc(const_in, 16)
            sp.wait_ge(x_in, 80)
            with sp.Fori(0, LAYERS) as l:
                wl = lambda name: A[name][bass.ds(l, 1)].rearrange("a k n -> (a k) n")
                w_in = wl("w_in").rearrange("(k p) n -> p k n", p=128)
                w1 = wl("mlp_w1").rearrange("(k p) n -> p k n", p=128)
                w2m = wl("mlp_w2").rearrange("(kg k p) n -> kg p k n", p=128, k=KD)
                wo = wl("w_out").rearrange("(k p) n -> p k n", p=128)
                wn = wl("w_nsa_up").rearrange("(g c d) n -> g d c n", g=2, c=4)
                wg = wl("w_gla_up").rearrange("(c p) n -> p c n", p=128)

                def slot_free(t):
                    if t < RING:
                        return acc.done, 2 + l * acc.total
                    return tile_used(l, t - RING)

                def load(t, parts):
                    free, v = slot_free(t)
                    v = sp.snap(v)
                    sp.wait_ge(free, v)
                    for i, (dst, src) in enumerate(parts):
                        ins = sp.dma_start(dst, src)
                        ins.then_inc(w_landed[t % RING], 16)

                def t8(t):
                    return wt[t % RING][:, :].rearrange("p (k n) -> p k n", k=KD)

                def cols(t, w, c0):
                    load(t, [(t8(t), w[:, :, c0:c0 + 256])])

                def cached(s):
                    if s >= 2:
                        sp.wait_ge(val_copied.sem, val_copied.at(l, s - 1))
                        sp.sem_inc(sp_passed, 1)
                        sp.wait_ge(tb.done, tb.emptied(l, f"keys{s - 2}"))
                        sp.sem_inc(sp_passed, 1)
                    for pg in range(2):
                        page = sp.value_load(ptab[0:1, 2 * s + pg:2 * s + pg + 1], min_val=0, max_val=A["cache_nsa_kv"].shape[0] - 1)
                        src = A["cache_nsa_kv"][bass.ds(page, 1), bass.ds(l, 1)].rearrange("a b (i r) j g d -> (a b i) r (j g d)", r=2)
                        sp.dma_start(stg[64 * pg:64 * pg + 64, s % 2, :, :], src).then_inc(cache_in[s % 2].sem, 16)
                    win = A["cache_win_kv"][s, bass.ds(l, 1)].rearrange("a (i r) j g d -> (a i) r (j g d)", r=2)
                    sp.dma_start(stw[:, s % 2, :, :], win[:, :, 0:128]).then_inc(cache_in[s % 2].sem, 16)
                    sp.dma_start(Vs[:, 1, s, :, :], win[:, :, 128:256]).then_inc(val_in.sem, 16)

                for i in range(2):
                    dst = wt[(T_Q + i) % RING][:, :].rearrange("p (k c g n) -> p k c g n", k=KD, c=2, g=2)
                    load(T_Q + i, [(dst[:, :, c, g, :], w_in[:, :, OFF_Q + g * 256 + (2 * i + c) * 64:OFF_Q + g * 256 + (2 * i + c) * 64 + 64])
                                   for c in range(2) for g in range(2)])
                for i in range(3):
                    cols(T_KV + i, w_in, OFF_KV + i * 256)

                def cmp_w1(i):
                    dst = wt[(T_CMP + i) % RING][:, :].rearrange("p (k n) -> p k n", k=16)
                    src = wl(("cmp_k_w1", "cmp_v_w1")[i]).rearrange("(k p) n -> p k n", p=128)
                    load(T_CMP + i, [(dst[:, 8 * a:8 * a + 8, :], src[:, 8 * a:8 * a + 8, :]) for a in range(2)])

                sp.wait_ge(h_ready.sem, h_ready.at(l, 8))
                sp.sem_inc(sp_passed, 1)
                cached(0)
                cols(T_GLA, w_in, OFF_GQ)
                cached(1)
                for i in range(1, 4):
                    cols(T_GLA + i, w_in, OFF_GQ + i * 256)
                for i in range(2):
                    cols(T_GR + i, w_in, OFF_GR + i * 256)
                cached(2)
                cmp_w1(0)
                cached(3)
                cached(4)
                cmp_w1(1)
                cached(5)
                cached(6)
                cols(T_MG, w_in, OFF_MG)
                cached(7)
                for i in range(1, 8):
                    cols(T_MG + i, w_in, OFF_MG + i * 256)
                for i in range(4):
                    d = t8(T_UP + i)
                    load(T_UP + i, [(d[64 * g:64 * g + 64, 0:4, :], wn[g, :, :, i * 256:i * 256 + 256]) for g in range(2)]
                         + [(d[:, 4:8, :], wg[:, :, i * 256:i * 256 + 256])])
                for i in range(4):
                    cols(T_OUT + i, wo, i * 256)
                for i in range(16):
                    cols(T_M1 + i, w1, i * 256)
                for i in range(16):
                    load(T_M2 + i, [(t8(T_M2 + i), w2m[i % 4, :, :, (i // 4) * 256:(i // 4) * 256 + 256])])

        parts_of = {**{T_Q + i: 4 for i in range(2)}, **{T_CMP + i: 2 for i in range(2)}, **{T_UP + i: 3 for i in range(4)}}
        per_slot = [sum(16 * parts_of.get(t, 1) for t in range(TILES) if t % RING == s) for s in range(RING)]

        def landed(t):
            s = t % RING
            return w_landed[s], per_slot[s], sum(16 * parts_of.get(x, 1) for x in range(t + 1) if x % RING == s)

        @block.gpsimd
        def _(pool):
            pool.memset(small[:, :], 1.0).then_inc(ini["zero"], 1)
            pool.memset(Qz[:, :, :, :], 0.0).then_inc(ini["zero"], 1)
            pool.memset(wsm[:, :, :], 0.0).then_inc(ini["zero"], 1)
            pool.memset(xin[:, 2, :], 0.0).then_inc(ini["zero"], 1)
            pool.memset(vecr[:, :], 0.0).then_inc(ini["zero"], 1)
            pool.memset(xla[:, 2, :], 0.0).then_inc(ini["zero"], 1)
            pool.memset(gates[:, 2, :], 0.0).then_inc(ini["zero"], 1)
            pool.wait_ge(ini["zero"], 7)
            pool.dma_start(ptab[:, :], A["page_table"].rearrange("(a s) n -> a (s n)", a=1)).then_inc(x_in, 16)
            pool.dma_start(xin[:, 0:2, :], A["x_prompt"][0].rearrange("(g p) f -> p g f", p=128)).then_inc(x_in, 16)
            pool.dma_start(xin[0:NS, 2, :], A["x_sample"].rearrange("s t f -> (s t) f")).then_inc(x_in, 16)
            pool.dma_start(vecr[0:8, :], A["ln_in_g"].rearrange("(c p) -> c p", p=128)).then_inc(x_in, 16)
            pool.dma_start(vecr[8:16, :], A["ln_in_b"].rearrange("(c p) -> c p", p=128)).then_inc(x_in, 16)
            pool.wait_ge(x_in, 80)
            pool.dma_start(O["win_kv_sample"].rearrange("s l t j g d -> s l (t j g d)")[:, :, 0:255 * 256],
                           A["cache_win_kv"].rearrange("s l t j g d -> s l (t j g d)")[:, :, 256:256 * 256]).then_inc(stored, 16)
            pool.wait_ge(ini["trc"], 7)
            with pool.Fori(0, LAYERS) as l:
                def row(name, pat, **kw):
                    return A[name][bass.ds(l, 1)].rearrange(pat, **kw)

                wv = A["w_in"][bass.ds(l, 1)].rearrange("a (k p) n -> p (a k) n", p=128)
                pool.wait_ge(mixers_done.sem, mixers_done.at(l, 1))
                pool.sem_inc(pool_passed, 1)
                pool.dma_start(wsm[:, :, 0:RANK], wv[:, :, OFF_LR:OFF_LR + RANK]).then_inc(wsm_in.sem, 16)
                pool.dma_start(wsm[:, :, 32:56], wv[:, :, OFF_G:OFF_G + 24]).then_inc(wsm_in.sem, 16)
                for k, name in ((V_L1G, "ln1_g"), (V_L1B, "ln1_b"), (V_L2G, "ln2_g"), (V_L2B, "ln2_b")):
                    pool.dma_start(vecr[k:k + 8, :], row(name, "a (c p) -> (a c) p", p=128)).then_inc(vec_in.sem, 16)
                pool.dma_start(vecr[V_GN:V_GN + 1, :], row("gla_norm_g", "a p -> a p")).then_inc(vec_in.sem, 16)
                pool.dma_start(vecr[V_PEK:V_PEK + 16, :], row("cmp_k_pe", "a (i b) d -> (a i) (b d)", b=2)).then_inc(vec_in.sem, 16)
                pool.dma_start(vecr[V_PEV:V_PEV + 16, :], row("cmp_v_pe", "a (i b) d -> (a i) (b d)", b=2)).then_inc(vec_in.sem, 16)
                pool.dma_start(wa2[0:RANK, :], row("gla_w_a2", "a r n -> (a r) n")).then_inc(par_in.sem, 16)
                pool.dma_start(wa2[RANK:RANK + 1, :], row("gla_b_a", "a n -> a n")).then_inc(par_in.sem, 16)
                pool.dma_start(w2[:, 0, :], row("cmp_k_w2", "a h n -> (a h) n")).then_inc(par_in.sem, 16)
                pool.dma_start(w2[:, 1, :], row("cmp_v_w2", "a h n -> (a h) n")).then_inc(par_in.sem, 16)
                for h2 in range(2):
                    for hp in range(2):
                        if h2 == 0 and hp == 0:
                            pool.wait_ge(stored, l * (16 * STORES) + 16)
                            pool.sem_inc(pool_passed, 1)
                        ins = pool.dma_start(Sst[64 * h2:64 * h2 + 64, :, hp, :],
                                             A["state_gla"][:, bass.ds(l, 1), 2 * hp + h2].rearrange("s a k v -> k (s a) v"))
                        ins.then_inc(state_in.sem, 16)
                pool.wait_ge(tb.done, tb.emptied(l, "kvt5"))
                pool.sem_inc(pool_passed, 1)
                for g in range(2):
                    pool.dma_start(O["nsa_kv_prompt"][0, bass.ds(l, 1), 128 * g:128 * g + 128].rearrange("a t j g d -> (a t) (j g d)"),
                                   kvtok[:, g, 0:512]).then_inc(stored, 16)
                    pool.dma_start(O["win_kv_prompt"][0, bass.ds(l, 1), 128 * g:128 * g + 128].rearrange("a t j g d -> (a t) (j g d)"),
                                   kvtok[:, g, 512:768]).then_inc(stored, 16)
                pool.dma_start(O["nsa_kv_sample"][:, bass.ds(l, 1), 0].rearrange("s a j g d -> (s a) (j g d)"),
                               kvtok[0:NS, 2, 0:512]).then_inc(stored, 16)
                pool.dma_start(O["win_kv_sample"][:, bass.ds(l, 1), PAST - 1].rearrange("s a j g d -> (s a) (j g d)"),
                               kvtok[0:NS, 2, 512:768]).then_inc(stored, 16)
                pool.wait_ge(gate_sig.sem, gate_sig.at(l, 1))
                pool.sem_inc(pool_passed, 1)
                for g in range(2):
                    pool.dma_start(gate64[32 * g:32 * g + 32, :],
                                   gates[0:NS, 2, 12 * g:12 * g + 12].rearrange("s (c b) -> s c b", c=4)).then_inc(gate_in.sem, 16)
                pool.wait_ge(g_state.sem, g_state.at(l, 4))
                pool.sem_inc(pool_passed, 1)
                for h2 in range(2):
                    pool.dma_start(O["gla_state_prompt"][0, bass.ds(l, 1), h2::2].rearrange("a h k v -> k (a h) v"),
                                   Sp[64 * h2:64 * h2 + 64, 1, :, :]).then_inc(stored, 16)
                pool.wait_ge(s_state.sem, s_state.at(l, 8))
                pool.sem_inc(pool_passed, 1)
                for h2 in range(2):
                    for hp in range(2):
                        pool.dma_start(O["gla_state_sample"][:, bass.ds(l, 1), 2 * hp + h2].rearrange("s a k v -> k (s a) v"),
                                       Sst[64 * h2:64 * h2 + 64, :, hp, :]).then_inc(stored, 16)
            pool.wait_ge(ini["trc"], 13)
            pool.dma_start(O["y_prompt"][0].rearrange("(g p) f -> p g f", p=128), xin[:, 0:2, :]).then_inc(stored, 16)
            pool.dma_start(O["y_sample"].rearrange("s t f -> (s t) f"), xin[0:NS, 2, :]).then_inc(stored, 16)
            pool.wait_ge(stored, 16 * (STORES * LAYERS + 3))

        @block.tensor
        def _(pe):
            mm = nc.tensor.matmul
            pe.wait_ge(const_in, 16)
            pe.wait_ge(x_in, 80)

            def tr(out, in_, p0, np_):
                return nc.tensor.transpose(out, in_, cst[p0:p0 + np_, C_ID + p0:C_ID + p0 + np_])

            for n in range(6):
                g, half = n // 2, n % 2
                if n >= 2:
                    pe.wait_ge(ini["trc"], n - 1)
                for c in range(4):
                    ins = tr(tb.banks[n % 2][:, 128 * c:128 * c + 128], xin[:, g, (4 * half + c) * 128:(4 * half + c) * 128 + 128], 0, 128)
                ins.then_inc(ini["tr"], 1)
            pe.wait_ge(ini["trc"], 5)
            tr(tb.banks[0][:, 0:V_N], vecr[:, :], 0, V_N).then_inc(ini["tr"], 1)
            pe.wait_ge(ini["trc"], 7)
            for c in range(KD):
                ins = mm(sc.banks[0][:, 0:NT], ones, hT[:, c, :], start=(c == 0), stop=(c == KD - 1))
            ins.then_inc(ini["sum"], 1)
            pe.wait_ge(ini["sq"], 1)
            for c in range(KD):
                ins = mm(sc.banks[1][:, 0:NT], ones, sq[:, c, :], start=(c == 0), stop=(c == KD - 1))
            ins.then_inc(ini["var"], 1)

            with pe.Fori(0, LAYERS) as l:
                def wait(sem_, value):
                    pe.wait_ge(sem_, value)
                    pe.sem_inc(pe_passed, 1)

                def take(bk, name):
                    wait(bk.done, bk.free(l, name))
                    return bk.bank(name)

                def chunk(name, w, n, mv, k0=0, kn=KD, free=True, first=True, last=True, m=128):
                    bank = acc.bank(name)
                    if free:
                        pe.wait_ge(acc.done, acc.free(l, name))
                    for k in range(kn):
                        ins = mm(bank[0:m, 0:NT], w(k, n), mv(k), start=(first and k == 0), stop=(last and k == kn - 1))
                    if last:
                        ins.then_inc(acc.ready, 1)
                    return ins

                def tile_in(t):
                    s, per, v = landed(t)
                    pe.wait_ge(s, l * per + v)
                    r = wt[t % RING][:, :].rearrange("p (k n) -> p k n", k=KD)
                    return lambda k, n: r[:, k, n * 128:n * 128 + 128]

                hk = lambda k: hT[:, k, :]
                w = tile_in(T_Q)
                for k in range(KD):
                    pe.wait_ge(h_ready.sem, h_ready.at(l, k + 1))
                    if k == 0:
                        pe.wait_ge(acc.done, acc.free(l, "q0"))
                    ins = mm(acc.bank("q0")[:, 0:NT], w(k, 0), hk(k), start=(k == 0), stop=(k == KD - 1))
                ins.then_inc(acc.ready, 1)
                chunk("q1", w, 1, hk)

                def project(names, t, mv=hk):
                    w = tile_in(t)
                    for n, name in enumerate(names):
                        chunk(name, w, n, mv)

                project(["q2", "q3"], T_Q + 1)
                for i in range(3):
                    project([f"kv{2 * i}", f"kv{2 * i + 1}"], T_KV + i)
                for i in range(2):
                    project([f"gla{2 * i}", f"gla{2 * i + 1}"], T_GLA + i)
                wait(wsm_in.sem, wsm_in.at(l, 32))
                chunk("small", lambda k, n: wsm[:, k, :], 0, hk, m=56)

                wait(vec_in.sem, vec_in.at(l, 112))
                b = take(tb, "vec")
                tr(b[:, 0:V_N], vecr[:, :], 0, V_N).then_inc(tb.ready, 1)
                for i in range(6):
                    src, name = (qT[:, i, :], f"q{i}") if i < 4 else (kvT[:, 2 * (i - 3), :], f"kv{2 * (i - 3)}")
                    wait(acc.done, acc.emptied(l, name))
                    b = take(tb, f"rope{i}")
                    mm(b[:, 0:NT], cst[:, C_ROT:C_ROT + 128], src, start=True, stop=True).then_inc(tb.ready, 1)

                wait(q_rot.sem, q_rot.at(l, 6))
                wait(acc.done, acc.emptied(l, "kv5"))
                for i in range(6):
                    c0, n = TG[i // 2]
                    b = take(tb, f"kvt{i}")
                    for j in range(4 if i % 2 == 0 else 2):
                        ins = tr(b[0:n, 128 * j:128 * j + 128], kvT[:, 4 * (i % 2) + j, c0:c0 + n], 0, 128)
                    ins.then_inc(tb.ready, 1)
                wait(s_qz.sem, s_qz.at(l, 1))
                for s in range(NS):
                    wait(cache_in[s % 2].sem, cache_in[s % 2].at(l, 48 * (s // 2 + 1)))
                    b = take(tb, f"pairs{s}")
                    for n in range(4):
                        for r in range(2):
                            ins = mm(b[64 * r:64 * r + 64, 128 * n:128 * n + 128], stg[:, s % 2, r, 64 * n:64 * n + 64], ident,
                                     start=True, stop=True)
                    ins.then_inc(tb.ready, 1)
                    b = take(tb, f"keys{s}")
                    for n in range(4):
                        src = stg[:, s % 2, n, 256:384] if n < 2 else stw[:, s % 2, n - 2, :]
                        ins = tr(b[:, 128 * n:128 * n + 128], src, 0, 128)
                    ins.then_inc(tb.ready, 1)
                    if s == 0:
                        take(sc, "ssc0")
                        take(sc, "ssc1")
                    wait(tb.done, tb.emptied(l, f"keys{s}"))
                    for br in range(2):
                        ins = mm(sc.bank(f"ssc{br}")[0:64, 0:NKEY], Qz[:, 1, s, :], kTs[:, s % 2, br, :], start=(s == 0), stop=(s == NS - 1))
                        if s == NS - 1:
                            ins.then_inc(sc.ready, 1)
                        elif br == 1:
                            ins.then_inc(s_keys.sem, 1)
                    if s % 2 == 0:
                        w = tile_in((T_GLA + 2, T_GLA + 3, T_GR, T_GR + 1)[s // 2])
                    chunk(f"gla{4 + s}" if s < 4 else f"gr{s - 4}", w, s % 2, hk)
                wait(acc.done, acc.emptied(l, "gla7"))
                for i in range(6):
                    c0, n = TG[i // 2]
                    b = take(tb, f"glt{i}")
                    for j in range(4 if i % 2 == 0 else 2):
                        ins = tr(b[0:n, 128 * j:128 * j + 128], glT[:, 2 + 4 * (i % 2) + j, c0:c0 + n], 0, 128)
                    ins.then_inc(tb.ready, 1)
                b = take(tb, "gate")
                for g, (c0, n) in enumerate(TG):
                    ins = tr(b[0:n, 24 * g:24 * g + 24], gateT[:, c0:c0 + n], 0, 24)
                ins.then_inc(tb.ready, 1)
                wait(pairs.sem, pairs.at(l, 1))
                for j, name in enumerate(("hidk", "hidv")):
                    s, per, v = landed(T_CMP + j)
                    wait(s, l * per + v)
                    b = take(sc, name)
                    w = wt[(T_CMP + j) % RING]
                    for lp in range(16):
                        wk = w[:, 128 * lp:128 * lp + 128]
                        rows = cmpT[:, j].rearrange("p g s i -> p (g s) i")[:, :, lp:lp + 8 * 14 + 1:8]
                        mm(b[:, 0:270], wk, rows, start=(lp == 0), stop=(lp == 15))
                    for lp in range(16):
                        ins = mm(b[:, 272:273], w[:, 128 * lp:128 * lp + 128],
                                 lv[:, V_PEK + 16 * j + lp:V_PEK + 16 * j + lp + 1], start=(lp == 0), stop=(lp == 15))
                    ins.then_inc(sc.ready, 1)

                def gate_chunk(i):
                    chunk(f"mg{i}", tile_in(T_MG + i // 2), i % 2, hk)

                gate_chunk(0)
                gate_chunk(1)
                wait(par_in.sem, par_in.at(l, 64))
                wait(hid_g.sem, hid_g.at(l, 1))
                b = take(tb, "kcmp")
                for g in range(2):
                    ins = mm(b[64 * g:64 * g + 64, 0:135], w2[:, 0, :], hx[:, 0, 135 * g:135 * g + 135], start=True, stop=True)
                ins.then_inc(tb.ready, 1)
                wait(hid_g.sem, hid_g.at(l, 2))
                for i in range(3):
                    b = take(tb, f"vcmp{i}")
                    for s in range(4 * i, min(4 * i + 4, 9)):
                        for g in range(2):
                            o0 = (s - 4 * i) * 128 + 64 * g
                            ins = mm(b[0:NWIN, o0:o0 + 64], hx[:, 1, 135 * g + 15 * s:135 * g + 15 * s + 15], w2[:, 1, :],
                                     start=True, stop=True)
                    ins.then_inc(tb.ready, 1)

                for t in range(2):
                    wait(tb.done, tb.emptied(l, "kcmp"))
                    for g in range(GROUPS):
                        b = take(sc, f"csc{t}{g}")
                        for c in range(4):
                            ins = mm(b[:, 15 * c:15 * c + 15], qT[64 * g:64 * g + 64, c, 128 * t:128 * t + 128],
                                     kc[64 * g:64 * g + 64, 120:135], start=True, stop=True)
                        ins.then_inc(sc.ready, 1)
                b = take(sc, "ssc2")
                for s in range(NS):
                    ins = mm(b[0:64, 0:NWIN], Qz[:, 0, s, :], kc[:, 15 * s:15 * s + 15], start=(s == 0), stop=(s == NS - 1))
                ins.then_inc(sc.ready, 1)

                def scores(u):
                    t, c, g = u // 8, (u % 8) // 2, u % 2
                    b = take(sc, f"sc{u}")
                    for br in range(2):
                        ins = mm(b[:, 256 * br:256 * br + 128 * (t + 1)], qR[64 * g:64 * g + 64, c, 128 * t:128 * t + 128],
                                 kvT[64 * g:64 * g + 64, 2 + 2 * br, 0:128 * (t + 1)], start=True, stop=True)
                    ins.then_inc(sc.ready, 1)

                def prob_tr(u):
                    t = u // 8
                    wait(u_prob.sem, u_prob.at(l, u + 1))
                    b = take(tb, f"pt{u}")
                    for br in range(2):
                        for kb in range(t + 1):
                            n = br * (t + 1) + kb
                            ins = tr(b[:, 128 * n:128 * n + 128], PS[:, u % 2, br, 128 * kb:128 * kb + 128], 0, 128)
                    ins.then_inc(tb.ready, 1)

                def values(u):
                    t, c, g = u // 8, (u % 8) // 2, u % 2
                    name = f"o{u // 2}"
                    b = take(ob, name) if g == 0 else ob.bank(name)
                    wait(tb.done, tb.emptied(l, f"pt{u}"))
                    o = b[64 * g:64 * g + 64, 0:128]
                    mm(o, vc[:, 8, 64 * g:64 * g + 64], PTc[:, 4 * g + c, :], start=True, stop=False)
                    for br in range(2):
                        for kb in range(t + 1):
                            c0 = (3 + 2 * br) * 128 + 64 * g
                            end = br == 1 and kb == t
                            ins = mm(o, kvtok[:, kb, c0:c0 + 64], PT[:, u % 2, br * (t + 1) + kb, :], start=False, stop=end)
                    ins.then_inc(ob.ready if g == 1 else pv_done.sem, 1)

                def compressed_tr(t):
                    wait(c_prob.sem, c_prob.at(l, t + 1))
                    for a in range(2):
                        b = take(tb, f"pc{t}{a}")
                        for i in range(4):
                            ins = tr(b[0:NWIN, 128 * i:128 * i + 128], CS[:, t, 4 * a + i, :], 0, 128)
                        ins.then_inc(tb.ready, 1)

                def sample_probs():
                    wait(s_prob.sem, s_prob.at(l, 1))
                    b = take(tb, "spt")
                    for n in range(4):
                        tr(b[:, 64 * n:64 * n + 64], P64[:, n // 2, 128 * (n % 2):128 * (n % 2) + 128], 0, 64)
                    tr(b[0:NWIN, 256:320], C64[:, :], 0, 64).then_inc(tb.ready, 1)
                    b = take(tb, "snew")
                    wait(s_anew.sem, s_anew.at(l, 1))
                    for br in range(2):
                        ins = mm(b[0:8, 64 * br:64 * br + 64], An[:, br, :], cst[0:64, C_ID:C_ID + 64], start=True, stop=True)
                    ins.then_inc(tb.ready, 1)

                def sample_values():
                    wait(val_in.sem, val_in.at(l, 16 * NS))
                    wait(val_copied.sem, val_copied.at(l, NS))
                    wait(tb.done, tb.emptied(l, "snew"))
                    b = take(ob, "so")
                    for br in range(2):
                        c0 = (3 + 2 * br) * 128
                        mm(b[:, 0:64], kvtok[0:8, 2, c0:c0 + 128], Pn[:, br, :], start=(br == 0), stop=False, skip_group_check=True)
                    for s in range(NS):
                        o = b[:, 0:64].rearrange("p (g s c) -> p g s c", g=2, s=NS)[:, :, s, :]
                        for n in range(4):
                            mv = PTs[:, n, :].rearrange("p (g s c) -> p g s c", g=2, s=NS)[:, :, s, :]
                            mm(o, Vs[:, n // 2, s, n % 2, :], mv, start=False, stop=False, skip_group_check=True)
                        mv = PTcs[:, :].rearrange("p (g s c) -> p g s c", g=2, s=NS)[:, :, s, :]
                        ins = mm(o, vc[:, s, :], mv, start=False, stop=(s == NS - 1), skip_group_check=True)
                    ins.then_inc(ob.ready, 1)

                def log_decays():
                    b = take(tb, "la01")
                    wait(acc.done, acc.emptied(l, "small"))
                    for g in range(2):
                        ins = mm(b[:, 256 * g:256 * g + 256], small[0:RANK + 1, 128 * g:128 * g + 128], wa2[:, :], start=True, stop=True)
                    ins.then_inc(tb.ready, 1)
                    b = take(tb, "la2")
                    mm(b[0:NS, 0:256], small[0:RANK + 1, SEQ:NT], wa2[:, :], start=True, stop=True).then_inc(tb.ready, 1)

                def sample_decays():
                    wait(la_t.sem, la_t.at(l, 1))
                    b = take(tb, "elas")
                    for hp in range(2):
                        ins = tr(b[:, 8 * hp:8 * hp + 8], xla[0:NS, 2, 128 * hp:128 * hp + 128], 0, NS)
                    ins.then_inc(tb.ready, 1)

                def head_squares(i):
                    wait(r_sq.sem, r_sq.at(l, i + 1))
                    n = 512 if i < 2 else 32
                    b = take(sc, f"rms{i}")
                    mm(b[:, 0:n], ones, osq[:, 0:n], start=True, stop=True).then_inc(sc.ready, 1)

                def decays(t):
                    b = take(sc, f"gB{t}")
                    for hp in range(2):
                        ins = mm(b[:, 256 * hp:256 * hp + 256], xla[:, t, 128 * hp:128 * hp + 128], cst[:, C_TRI:C_TRI + 256], start=True, stop=True)
                    ins.then_inc(sc.ready, 1)
                    b = take(tb, f"aft{t}")
                    mm(b[:, 0:256], cst[:, C_AFT:C_AFT + 128], xla[:, t, :], start=True, stop=True).then_inc(tb.ready, 1)

                def gla_scores(t):
                    wait(g_q.sem, g_q.at(l, t + 1))
                    for h2 in range(2):
                        b = take(tb, f"gA{t}{h2}")
                        for hp in range(2):
                            ins = mm(b[:, 128 * hp:128 * hp + 128], km[64 * h2:64 * h2 + 64, hp, :], qm[64 * h2:64 * h2 + 64, hp, :], start=True, stop=True)
                        ins.then_inc(tb.ready, 1)

                def gla_update(t, ch):
                    b = take(tb, f"U{t}{ch}")
                    for hp in range(2):
                        ins = mm(b[:, 256 * hp:256 * hp + 256], kd[64 * ch:64 * ch + 64, 128 * hp:128 * hp + 128],
                                 gltok[64 * ch:64 * ch + 64, t, 256 + 256 * hp:512 + 256 * hp], start=True, stop=True)
                    ins.then_inc(tb.ready, 1)

                def gla_values(t):
                    bs = [take(ob, f"go{t}{h2}") for h2 in range(2)]
                    wait(tb.done, tb.emptied(l, f"gA{t}1"))
                    for h2 in range(2):
                        for hp in range(2):
                            h = 2 * hp + h2
                            mm(bs[h2][:, 128 * hp:128 * hp + 128], gltok[:, t, 256 + 128 * h:384 + 128 * h], gAs[:, h, :],
                               start=(hp == 0), stop=False, skip_group_check=True)
                    for ch in range(2):
                        k = 2 * t + ch
                        if k == 0:
                            continue
                        wait(g_state.sem, g_state.at(l, k))
                        for h2 in range(2):
                            for hp in range(2):
                                c0 = 128 * hp + 64 * ch
                                ins = mm(bs[h2][:, c0:c0 + 64], Sp[64 * h2:64 * h2 + 64, (k - 1) % 2, hp, :],
                                         qe[64 * h2:64 * h2 + 64, hp, 64 * ch:64 * ch + 64],
                                         start=False, stop=(ch == 1 and hp == 1), skip_group_check=True)
                            if ch == 1:
                                ins.then_inc(ob.ready, 1)

                def sample_update(s):
                    wait(kz_d.sem, kz_d.at(l, s + 1))
                    b = take(tb, f"SU{s}")
                    for hp in range(2):
                        ins = mm(b[:, 256 * hp:256 * hp + 256], kz[:, s % 2, 128 * hp:128 * hp + 128], gltok[0:NS, 2, 256 + 256 * hp:512 + 256 * hp], start=True, stop=True)
                    ins.then_inc(tb.ready, 1)

                def sample_outputs():
                    wait(qs_d.sem, qs_d.at(l, 1))
                    wait(s_state.sem, s_state.at(l, 8))
                    for h2 in range(2):
                        b = take(ob, f"gos{h2}")
                        for hp in range(2):
                            for s in range(NS):
                                ins = mm(b[:, 8 * hp + s:8 * hp + s + 1], Sst[64 * h2:64 * h2 + 64, s, hp, :], qs[64 * h2:64 * h2 + 64, hp, s:s + 1], start=True, stop=True)
                        ins.then_inc(ob.ready, 1)

                for k in range(18):
                    if k < 16:
                        scores(k)
                    if k < 14:
                        gate_chunk(k + 2)
                    if k == 1:
                        compressed_tr(0)
                    if 1 <= k <= 16:
                        prob_tr(k - 1)
                    if k >= 2:
                        values(k - 2)
                    if k == 9:
                        compressed_tr(1)
                    if k == 0:
                        log_decays()
                    elif k == 1:
                        sample_probs()
                    elif k == 2:
                        sample_decays()
                        decays(0)
                    elif k == 3:
                        sample_values()
                    elif k == 4:
                        gla_scores(0)
                    elif k == 5:
                        gla_update(0, 0)
                        gla_update(0, 1)
                    elif k == 7:
                        gla_values(0)
                    elif k == 8:
                        decays(1)
                    elif k == 9:
                        head_squares(0)
                    elif k == 10:
                        gla_scores(1)
                    elif k == 11:
                        gla_update(1, 0)
                    elif k == 13:
                        gla_values(1)
                        gla_update(1, 1)
                    elif k == 15:
                        head_squares(1)
                    elif k == 17:
                        sample_outputs()
                    if k in (12, 14, 15, 16):
                        for s in range(2 * max(0, k - 13), 2 * max(0, k - 13) + 2):
                            sample_update(s)
                head_squares(2)

                wait(ob.done, ob.emptied(l, "so"))
                wait(og_d.sem, og_d.at(l, 3))
                for i in range(4):
                    w = tile_in(T_UP + i)
                    for n in range(2):
                        chunk(f"up{4 * i + 2 * n}", w, n, lambda k: onT[:, k, :], kn=4)
                        chunk(f"up{4 * i + 2 * n + 1}", lambda k, n: w(4 + k, n), n, lambda k: ogT[:, k, :], kn=4)
                wait(up_m.sem, up_m.at(l, 8))

                def stats(i, res, c):
                    if c == 0:
                        take(sc, f"ln{i + 1}m")
                        take(sc, f"ln{i + 1}v")
                    wait(res.sem, res.at(l, c + 1))
                    ins = mm(sc.bank(f"ln{i + 1}m")[:, 0:NT], ones, hT[:, c, :], start=(c == 0), stop=(c == KD - 1))
                    if c == KD - 1:
                        ins.then_inc(sc.ready, 1)
                    wait(ln_sq.sem, ln_sq.at(l, 8 * i + c + 1))
                    ins = mm(sc.bank(f"ln{i + 1}v")[:, 0:NT], ones, sq[:, c, :], start=(c == 0), stop=(c == KD - 1))
                    if c == KD - 1:
                        ins.then_inc(sc.ready, 1)

                for i in range(4):
                    w = tile_in(T_OUT + i)
                    for n in range(2):
                        chunk(f"out{2 * i + n}", w, n, lambda k: mgT[:, k, :])
                        if i >= 1:
                            stats(0, res1, 2 * i + n - 2)
                for c in range(6, 8):
                    stats(0, res1, c)

                def split_in(t):
                    wait(w_lo.sem, w_lo.at(l, t - T_M1 + 1))
                    hi = whi[(t - T_M1) % 2]
                    lo = wlo[t % RING]
                    return (lambda k, n: hi[:, k, n * 128:n * 128 + 128]), (lambda k, n: lo[:, k, n * 128:n * 128 + 128])

                def split_chunk(name, w, n, hi, lo, first=True, last=True, wait_k=None):
                    bank = acc.bank(name)
                    if first:
                        wait(acc.done, acc.free(l, name))
                    for k in range(KD):
                        if wait_k:
                            wait_k(k)
                        mm(bank[:, 0:NT], w[0](k, n), hi(k), start=(first and k == 0), stop=False)
                        mm(bank[:, 0:NT], w[0](k, n), lo(k), start=False, stop=False)
                        ins = mm(bank[:, 0:NT], w[1](k, n), hi(k), start=False, stop=(last and k == KD - 1))
                    if last:
                        ins.then_inc(acc.ready, 1)
                    return ins

                for i in range(16):
                    w = split_in(T_M1 + i)
                    for n in range(2):
                        split_chunk(f"m1_{2 * i + n}", w, n, lambda k: h_hi[:, k, :], lambda k: h_lo[:, k, :],
                                    wait_k=(lambda k: wait(h_lo_d.sem, h_lo_d.at(l, k + 1))) if i + n == 0 else None)
                for cg in range(4):
                    for kg in range(4):
                        w = split_in(T_M2 + 4 * cg + kg)
                        if cg == 0:
                            wait(hid_lo_d.sem, hid_lo_d.at(l, 8 * kg + 8))
                        for n in range(2):
                            ins = split_chunk(f"m2_{2 * cg + n}", w, n, lambda k: hid_hi[:, 8 * kg + k, :], lambda k: hid_lo[:, 8 * kg + k, :],
                                              first=(kg == 0), last=(kg == 3))
                        if kg < 3:
                            ins.then_inc(m2_part.sem, 1)
                        if kg == 0 and cg > 0:
                            stats(1, res2, 2 * cg - 2)
                            stats(1, res2, 2 * cg - 1)
                for c in range(6, 8):
                    stats(1, res2, c)

            pe.wait_ge(h_ready.sem, LAYERS * 16 + 8)
            for n in range(6):
                g, half = n // 2, n % 2
                c0, m = TG[g]
                if n >= 2:
                    pe.wait_ge(ini["trc"], 6 + n)
                for c in range(4):
                    ins = tr(tb.banks[n % 2][0:m, 128 * c:128 * c + 128], hT[:, 4 * half + c, c0:c0 + m], 0, 128)
                ins.then_inc(ini["tr"], 1)

        @block.scalar
        def _(act):
            A_ = nc.scalar.activation
            act.preload_act_table_set("natural_log_exp_and_others")
            act.sem_inc(acc.done, 2)
            act.sem_inc(sc.done, 2)
            act.sem_inc(ob.done, 2)
            act.wait_ge(ini["sum"], 1)
            A_(mu, sc.banks[0][:, 0:NT], ACT.Copy, scale=1.0 / D).then_inc(ini["mu"], 1)
            act.wait_ge(ini["cen"], 1)
            A_(sq[:, :, :], hT[:, :, :], ACT.Square).then_inc(ini["sq"], 1)
            act.wait_ge(ini["var"], 1)
            A_(rs, sc.banks[1][:, 0:NT], ACT.Ln, scale=1.0 / D, bias=epsc).then_inc(ini["rs"], 1)
            act.wait_ge(ini["rs"], 1)
            A_(rs, rs, ACT.Exp, scale=-0.5).then_inc(ini["rs"], 1)
            for c in range(KD):
                act.wait_ge(ini["cen"], c + 2)
                A_(hT[:, c, :], hT[:, c, :], ACT.Identity, bias=lv[:, 8 + c:9 + c]).then_inc(h_ready.sem, 1)

            with act.Fori(0, LAYERS) as l:
                links = [0]

                def link(ins):
                    links[0] += 1
                    ins.then_inc(act_link.sem, 1)
                    act.wait_ge(act_link.sem, act_link.at(l, links[0]))

                def evac(name, dst, func=ACT.Copy, m=128, **kw):
                    act.wait_ge(acc.ready, acc.filled(l, name))
                    A_(dst, acc.bank(name)[0:m, 0:NT], func, **kw).then_inc(acc.done, 1)

                for i in range(4):
                    evac(f"q{i}", qT[:, i, :])
                for i in range(6):
                    evac(f"kv{i}", kvT[:, i, :])
                for i in range(4):
                    evac(f"gla{i}", glT[:, i, :])
                act.wait_ge(ini["zero"], 7)
                act.wait_ge(acc.ready, acc.filled(l, "small"))
                link(A_(small[0:RANK, :], acc.bank("small")[0:RANK, 0:NT], ACT.Copy))
                A_(gateT[:, :], acc.bank("small")[32:56, 0:NT], ACT.Copy).then_inc(acc.done, 1)
                for s in range(NS):
                    act.wait_ge(cache_in[s % 2].sem, cache_in[s % 2].at(l, 48 * (s // 2 + 1)))
                    A_(Vs[:, 0, s, :, :], stg[:, s % 2, :, 384:512], ACT.Copy).then_inc(val_copied.sem, 1)
                    if s < 4:
                        evac(f"gla{4 + s}", glT[:, 4 + s, :])
                    else:
                        i = s - 4
                        act.wait_ge(acc.ready, acc.filled(l, f"gr{i}"))
                        link(A_(gre[:, i, :], acc.bank(f"gr{i}")[:, 0:NT], ACT.Exp, scale=-1.0))
                        A_(grT[:, i, :], acc.bank(f"gr{i}")[:, 0:NT], ACT.Copy).then_inc(acc.done, 1)
                act.wait_ge(s_max.sem, s_max.at(l, 1))
                for br in range(2):
                    A_(P64[:, br, :], sc.bank(f"ssc{br}")[0:64, 0:NKEY], ACT.Exp, scale=SCALE, bias=s64[:, 3 + br:4 + br],
                       accum_out=s64[:, 6 + br:7 + br]).then_inc(sc.done, 1)
                act.wait_ge(tb.done, tb.emptied(l, "gate"))
                A_(gates[:, :, :], gates[:, :, :], ACT.Exp, scale=-1.0).then_inc(gate_exp.sem, 1)
                for j, name in enumerate(("hidk", "hidv")):
                    act.wait_ge(sc.ready, sc.filled(l, name))
                    b = sc.bank(name)
                    link(A_(hb[:, j:j + 1], b[:, 272:273], ACT.Copy))
                    A_(hx[:, j, :], b[:, 0:270], ACT.Identity, bias=hb[:, j:j + 1]).then_inc(sc.done, 1)
                    act.wait_ge(hid_u.sem, hid_u.at(l, j + 1))
                    A_(hy, hy, ACT.Exp, scale=-2.0 * GELU_C).then_inc(hid_e.sem, 1)

                def gate_sigmoid(i):
                    m = mgT[:, i, :]
                    evac(f"mg{i}", m, ACT.Exp, scale=-1.0)
                    act.wait_ge(acc.done, acc.emptied(l, f"mg{i}"))
                    link(A_(m, m, ACT.Ln, bias=1.0))
                    A_(m, m, ACT.Exp, scale=-1.0).then_inc(mg_sig.sem, 1)

                gate_sigmoid(0)
                gate_sigmoid(1)
                for t in range(2):
                    for g in range(GROUPS):
                        act.wait_ge(sc.ready, sc.filled(l, f"csc{t}{g}"))
                        A_(CS[:, t, 4 * g:4 * g + 4, :], sc.bank(f"csc{t}{g}")[:, 0:60].rearrange("p (h k) -> p h k", h=4), ACT.Copy).then_inc(sc.done, 1)
                for t in range(2):
                    act.wait_ge(c_shift.sem, c_shift.at(l, t + 1))
                    A_(CS[:, t, :, :], CS[:, t, :, :], ACT.Exp, scale=SCALE).then_inc(c_exp.sem, 1)
                act.wait_ge(s_cmax.sem, s_cmax.at(l, 1))
                A_(C64[:, :], sc.bank("ssc2")[0:64, 0:NWIN], ACT.Exp, scale=SCALE, bias=s64[:, 5:6],
                   accum_out=s64[:, 8:9]).then_inc(sc.done, 1)
                def unit_exp(u):
                    n = 128 * (u // 8 + 1)
                    act.wait_ge(u_max.sem, u_max.at(l, u + 1))
                    if u >= 2:
                        act.wait_ge(tb.ready, tb.filled(l, f"pt{u - 2}"))
                    b = sc.bank(f"sc{u}")
                    A_(PS[:, u % 2, 0, 0:n], b[:, 0:n], ACT.Exp, scale=SCALE, bias=st[:, u % 2, 2:3],
                       accum_out=st[:, u % 2, 4:5]).then_inc(u_half.sem, 1)
                    A_(PS[:, u % 2, 1, 0:n], b[:, 256:256 + n], ACT.Exp, scale=SCALE, bias=st[:, u % 2, 3:4],
                       accum_out=st[:, u % 2, 5:6]).then_inc(sc.done, 1)

                def sample_values():
                    act.wait_ge(ob.ready, ob.filled(l, "so"))
                    for g in range(2):
                        ins = A_(onT[64 * g:64 * g + 64, :, SEQ:NT].rearrange("p c s -> p s c"),
                                 ob.bank("so")[64 * g:64 * g + 64, 32 * g:32 * g + 32].rearrange("p (s c) -> p s c", s=NS), ACT.Copy)
                        if g == 0:
                            link(ins)
                        else:
                            ins.then_inc(ob.done, 1)

                def log_decays():
                    act.wait_ge(tb.done, tb.emptied(l, "la2"))
                    link(A_(lla[:, :, :], xla[:, :, :], ACT.Abs))
                    link(A_(lla[:, :, :], lla[:, :, :], ACT.Exp, scale=-1.0))
                    A_(lla[:, :, :], lla[:, :, :], ACT.Ln, bias=1.0).then_inc(la_e.sem, 1)

                def decays(t):
                    if t == 1:
                        act.wait_ge(g_q.sem, g_q.at(l, 1))
                        act.wait_ge(g_state.sem, g_state.at(l, 2))
                    act.wait_ge(sc.ready, sc.filled(l, f"gB{t}"))
                    B = sc.bank(f"gB{t}")[:, :].rearrange("p (h m n) -> p h m n", h=2, m=2)
                    link(A_(EB[:, 0, :, :], B[:, :, 0, :], ACT.Exp))
                    link(A_(EB[:, 1, :, :], B[:, :, 1, :], ACT.Exp))
                    A_(EB[:, 2, :, :], B[:, :, 1, :], ACT.Exp, scale=-1.0).then_inc(sc.done, 1)

                def decays_after(t):
                    act.wait_ge(tb.done, tb.emptied(l, f"aft{t}"))
                    A_(kd, kd, ACT.Exp).then_inc(g_ea.sem, 1)

                def rms_squares(i):
                    n = 512 if i < 2 else 32
                    c0, m = TG[i]
                    if i > 0:
                        act.wait_ge(sc.ready, sc.filled(l, f"rms{i - 1}"))
                    for h2 in range(2):
                        name = f"go{i}{h2}" if i < 2 else f"gos{h2}"
                        act.wait_ge(ob.ready, ob.filled(l, name))
                        o = ob.bank(name)[:, 0:n // 2].rearrange("p (h t) -> p h t", h=2)
                        ins = A_(osq[:, 0:n].rearrange("p (h t) -> p h t", h=4)[:, h2:4:2, :], o, ACT.Square)
                        if h2 == 0:
                            link(ins)
                        else:
                            ins.then_inc(r_sq.sem, 1)
                        A_(ogT[:, h2:4:2, c0:c0 + m], o, ACT.Copy).then_inc(ob.done, 1)

                def rms_scale(i):
                    n = 512 if i < 2 else 32
                    act.wait_ge(sc.ready, sc.filled(l, f"rms{i}"))
                    if i > 0:
                        act.wait_ge(og_d.sem, og_d.at(l, i))
                    A_(rr[:, 0:n], sc.bank(f"rms{i}")[:, 0:n], ACT.Ln, scale=1.0 / DV, bias=epsc).then_inc(sc.done, 1)
                    act.wait_ge(sc.done, sc.emptied(l, f"rms{i}"))
                    A_(rr[:, 0:n], rr[:, 0:n], ACT.Exp, scale=-0.5).then_inc(r_rs.sem, 1)

                for k in range(18):
                    if k < 16:
                        unit_exp(k)
                    if k >= 3 and k % 2 == 1:
                        n = (k - 3) // 2
                        act.wait_ge(ob.ready, ob.filled(l, f"o{n}"))
                        A_(onT[:, n % 4, 128 * (n // 4):128 * (n // 4) + 128], ob.bank(f"o{n}")[:, 0:128], ACT.Copy).then_inc(ob.done, 1)
                    if k < 14:
                        if k == 10:
                            act.wait_ge(gla_silu.sem, gla_silu.at(l, 1))
                        gate_sigmoid(k + 2)
                    if k == 1:
                        log_decays()
                    elif k == 2:
                        decays(0)
                    elif k == 3:
                        sample_values()
                        act.wait_ge(tb.done, tb.emptied(l, "elas"))
                        A_(ela[:, :, :], ela[:, :, :], ACT.Exp, scale=1.0 / TAU).then_inc(ela_d.sem, 1)
                        decays_after(0)
                    elif k == 7:
                        rms_squares(0)
                    elif k == 8:
                        decays(1)
                    elif k == 9:
                        decays_after(1)
                        rms_scale(0)
                    elif k == 13:
                        rms_squares(1)
                    elif k == 15:
                        rms_scale(1)
                    elif k == 17:
                        rms_squares(2)
                rms_scale(2)
                for i in range(16):
                    if i >= 2:
                        act.wait_ge(up_m.sem, up_m.at(l, i // 2))
                    evac(f"up{i}", upb[:, i % 2, :])

                def square(i, res, c):
                    act.wait_ge(res.sem, res.at(l, c + 1))
                    A_(sq[:, c, :], hT[:, c, :], ACT.Square).then_inc(ln_sq.sem, 1)

                def split_hi(t):
                    s, per, v = landed(t)
                    if t >= T_M1 + 2:
                        act.wait_ge(*tile_used(l, t - 2))
                    act.wait_ge(s, l * per + v)
                    A_(whi[(t - T_M1) % 2][:, :, :], wt[t % RING][:, :].rearrange("p (k n) -> p k n", k=KD), ACT.Copy).then_inc(w_hi.sem, 1)

                def norm(i, vb):
                    act.wait_ge(sc.ready, sc.filled(l, f"ln{i + 1}m"))
                    A_(mu, sc.bank(f"ln{i + 1}m")[:, 0:NT], ACT.Copy, scale=1.0 / D).then_inc(sc.done, 1)
                    act.wait_ge(sc.ready, sc.filled(l, f"ln{i + 1}v"))
                    A_(rs, sc.bank(f"ln{i + 1}v")[:, 0:NT], ACT.Copy, scale=1.0 / D).then_inc(sc.done, 1)
                    act.wait_ge(ln_var.sem, ln_var.at(l, i + 1))
                    link(A_(rs, rs, ACT.Ln, bias=epsc))
                    A_(rs, rs, ACT.Exp, scale=-0.5).then_inc(ln_rs.sem, 1)
                    for c in range(KD):
                        act.wait_ge(ln_sc.sem, ln_sc.at(l, 8 * i + c + 1))
                        A_(hT[:, c, :], hT[:, c, :], ACT.Identity, bias=lv[:, vb + c:vb + c + 1]).then_inc(h_ready.sem, 1)
                        if i == 0:
                            act.wait_ge(h_ready.sem, h_ready.at(l, 9 + c))
                            A_(h_hi[:, c, :], hT[:, c, :], ACT.Copy).then_inc(h_hi_d.sem, 1)

                for i in range(8):
                    if i >= 2:
                        act.wait_ge(res1.sem, res1.at(l, i - 1))
                    evac(f"out{i}", yb[:, i % 2, :])
                    if i >= 1:
                        square(0, res1, i - 1)
                    if i == 5:
                        split_hi(T_M1)
                square(0, res1, 7)
                norm(0, V_L1B)
                split_hi(T_M1 + 1)
                for i in range(32):
                    if i >= 2:
                        act.wait_ge(hid_lo_d.sem, hid_lo_d.at(l, i - 1))
                    evac(f"m1_{i}", yb[:, i % 2, :], ACT.Relu)
                    act.wait_ge(acc.done, acc.emptied(l, f"m1_{i}"))
                    A_(hid_hi[:, i, :], yb[:, i % 2, :], ACT.Square).then_inc(hid_hi_d.sem, 1)
                    if i % 2 == 1:
                        split_hi(T_M1 + i // 2 + 2)
                act.wait_ge(hid_lo_d.sem, hid_lo_d.at(l, 32))
                for t in range(16):
                    if t % 4 == 3:
                        for i in range(t // 2 - 1, t // 2 + 1):
                            if i >= 2:
                                act.wait_ge(res2.sem, res2.at(l, i - 1))
                            evac(f"m2_{i}", yb[:, i % 2, :])
                        square(1, res2, t // 2 - 1)
                        square(1, res2, t // 2)
                    if t < 14:
                        split_hi(T_M2 + t + 2)
                norm(1, V_L2B)
                assert links[0] == act_link.per, links[0]

        @block.vector
        def _(dve):
            V = nc.vector
            dve.sem_inc(tb.done, 2)
            dve.sem_inc(mixers_done.sem, 1)
            for n in range(6):
                g, half = n // 2, n % 2
                c0, m = TG[g]
                dve.wait_ge(ini["tr"], n + 1)
                V.tensor_copy(hT[:, 4 * half:4 * half + 4, c0:c0 + m],
                              tb.banks[n % 2][:, :].rearrange("p (c t) -> p c t", c=4)[:, :, 0:m]).then_inc(ini["trc"], 1)
            dve.wait_ge(ini["tr"], 7)
            V.tensor_copy(lv[:, :], tb.banks[0][:, 0:V_N]).then_inc(ini["trc"], 1)

            def bc(a, n):
                return a[:, None, :].to_broadcast([128, n, NT])

            dve.wait_ge(ini["mu"], 1)
            V.tensor_tensor(hT[:, :, :], hT[:, :, :], bc(mu, KD), ALU.subtract).then_inc(ini["cen"], 1)
            dve.wait_ge(ini["rs"], 2)
            dve.wait_ge(ini["sq"], 1)
            for c in range(KD):
                V.scalar_tensor_tensor(hT[:, c, :], hT[:, c, :], lv[:, c:c + 1], rs, ALU.mult, ALU.mult).then_inc(ini["cen"], 1)

            with dve.Fori(0, LAYERS) as l:
                links = [0]

                def link(ins):
                    links[0] += 1
                    ins.then_inc(dve_link.sem, 1)
                    dve.wait_ge(dve_link.sem, dve_link.at(l, links[0]))

                def tr_in(name):
                    dve.wait_ge(tb.ready, tb.filled(l, name))
                    return tb.bank(name)

                b = tr_in("vec")
                dve.wait_ge(h_ready.sem, h_ready.at(l, 8))
                V.tensor_copy(lv[:, :], b[:, 0:V_N]).then_inc(tb.done, 1)
                cos, sin = cst[:, C_COS:C_COS + NT], cst[:, C_SIN:C_SIN + NT]
                for i in range(6):
                    b = tr_in(f"rope{i}")
                    src, dst = (qT[:, i, :], qR[:, i, :]) if i < 4 else (kvT[:, 2 * (i - 3), :],) * 2
                    link(V.tensor_tensor(tmpA[:, :], b[:, 0:NT], sin, ALU.mult))
                    V.tensor_tensor(dst, src, cos, ALU.mult).then_inc(tb.done, 1)
                    dve.wait_ge(tb.done, tb.emptied(l, f"rope{i}"))
                    V.tensor_tensor(dst, dst, tmpA[:, :], ALU.add).then_inc(q_rot.sem, 1)
                    dve.wait_ge(q_rot.sem, q_rot.at(l, i + 1))
                dve.wait_ge(ini["zero"], 7)
                for r, q in enumerate((qT, qR)):
                    for g in range(2):
                        dst = Qz[64 * g:64 * g + 64, r, :, :].rearrange("p s x -> p (s x)")[:, 32 * g:32 * g + 7 * 68 + 4]
                        base = Qz[64 * g:64 * g + 64, r, :, :].rearrange("p s x -> p (s x)")
                        for s in range(NS):
                            o0 = 64 * s + 32 * g + 4 * s
                            ins = V.tensor_copy(base[:, o0:o0 + 4], q[64 * g:64 * g + 64, :, SEQ + s])
                            if (r, g, s) == (1, 1, NS - 1):
                                ins.then_inc(s_qz.sem, 1)
                            else:
                                links[0] += 1
                                ins.then_inc(dve_link.sem, 1)
                dve.wait_ge(stored, l * (16 * STORES) + 16)
                def token_major(kind, dst):
                    for i in range(6):
                        b = tr_in(f"{kind}{i}")
                        g, a = i // 2, i % 2
                        m, n = TG[g][1], (256 if a else 512)
                        V.tensor_copy(dst[0:m, g, 512 * a:512 * a + n], b[0:m, 0:n]).then_inc(tb.done, 1)

                token_major("kvt", kvtok)
                for j in range(2):
                    for g in range(2):
                        for r in range(2):
                            ins = V.tensor_copy(cmpT[64 * r:64 * r + 64, j, g, NS, :], kvT[64 * g:64 * g + 64, j, r:SEQ:2])
                            if (j, g, r) == (1, 1, 1):
                                ins.then_inc(pairs.sem, 1)
                            else:
                                links[0] += 1
                                ins.then_inc(dve_link.sem, 1)
                for s in range(NS):
                    b = tr_in(f"pairs{s}")
                    V.tensor_copy(cmpT[:, :, :, s, :], b[:, :].rearrange("p (j g i) -> p j g i", j=2, g=2)).then_inc(tb.done, 1)
                    b = tr_in(f"keys{s}")
                    if s >= 2:
                        dve.wait_ge(s_keys.sem, s_keys.at(l, s - 1))
                    link(V.tensor_copy(kTs[:, s % 2, :, PAST:NKEY], kvT[:, 2:6:2, SEQ + s:SEQ + s + 1]))
                    V.tensor_copy(kTs[:, s % 2, :, 0:PAST], b[:, :].rearrange("p (r k) -> p r k", r=2)).then_inc(tb.done, 1)
                token_major("glt", gltok)
                for br in range(2):
                    dve.wait_ge(sc.ready, sc.filled(l, f"ssc{br}"))
                    link(V.tensor_reduce(s64[:, br:br + 1], sc.bank(f"ssc{br}")[0:64, 0:NKEY], AX, ALU.max))
                V.tensor_scalar(s64[:, 3:5], s64[:, 0:2], -SCALE, None, ALU.mult).then_inc(s_max.sem, 1)
                b = tr_in("gate")
                for g, (c0, m) in enumerate(TG):
                    ins = V.tensor_copy(gates[0:m, g, :], b[0:m, 24 * g:24 * g + 24])
                    if g < 2:
                        link(ins)
                    else:
                        ins.then_inc(tb.done, 1)
                dve.wait_ge(gate_exp.sem, gate_exp.at(l, 1))
                link(V.tensor_scalar(gates[:, :, :], gates[:, :, :], 1.0, None, ALU.add))
                V.reciprocal(gates[:, :, :], gates[:, :, :]).then_inc(gate_sig.sem, 1)
                dve.wait_ge(acc.done, acc.emptied(l, "gr3"))
                link(V.tensor_scalar(gre, gre, 1.0, None, ALU.add))
                link(V.reciprocal(gre, gre))
                V.tensor_tensor(grT[:, :, :], grT[:, :, :], gre, ALU.mult).then_inc(gla_silu.sem, 1)
                for j in range(2):
                    dve.wait_ge(sc.done, sc.emptied(l, ("hidk", "hidv")[j]))
                    x = hx[:, j, :]
                    if j == 1:
                        dve.wait_ge(hid_g.sem, hid_g.at(l, 1))
                    link(V.tensor_tensor(hy, x, x, ALU.mult))
                    link(V.tensor_scalar(hy, hy, 0.044715, 1.0, ALU.mult, ALU.add))
                    link(V.tensor_tensor(hy, hy, x, ALU.mult))
                    V.tensor_scalar(hy, hy, -50.0, None, ALU.max).then_inc(hid_u.sem, 1)
                    dve.wait_ge(hid_e.sem, hid_e.at(l, j + 1))
                    link(V.tensor_scalar(hy, hy, 1.0, None, ALU.add))
                    link(V.reciprocal(hy, hy))
                    V.tensor_tensor(x, x, hy, ALU.mult).then_inc(hid_g.sem, 1)
                b = tr_in("kcmp")
                V.tensor_copy(kc[:, :], b[:, 0:135]).then_inc(tb.done, 1)
                for i in range(3):
                    b = tr_in(f"vcmp{i}")
                    n = min(4, 9 - 4 * i)
                    V.tensor_copy(vc[:, 4 * i:4 * i + n, :], b[0:NWIN, 0:128 * n].rearrange("p (s d) -> p s d", d=128)).then_inc(tb.done, 1)
                def heads(a, w):
                    return a[:, :, None].to_broadcast([128, 8, w])

                for t in range(2):
                    S = CS[:, t, :, :]
                    add = cst[:, C_CADD + 15 * t:C_CADD + 15 * t + 15][:, None, :].to_broadcast([128, 4, NWIN])
                    for g in range(GROUPS):
                        dve.wait_ge(sc.done, sc.emptied(l, f"csc{t}{g}"))
                        ins = V.tensor_tensor(S[:, 4 * g:4 * g + 4, :], S[:, 4 * g:4 * g + 4, :], add, ALU.add)
                        links[0] += 1
                        ins.then_inc(dve_link.sem, 1)
                    dve.wait_ge(dve_link.sem, dve_link.at(l, links[0]))
                    link(V.tensor_reduce(cst8[:, t, 0, :], S, AX, ALU.max))
                    V.tensor_tensor(S, S, heads(cst8[:, t, 0, :], NWIN), ALU.subtract).then_inc(c_shift.sem, 1)
                for t in range(2):
                    S = CS[:, t, :, :]
                    dve.wait_ge(c_exp.sem, c_exp.at(l, t + 1))
                    live = cst[:, C_C01 + 15 * t:C_C01 + 15 * t + 15][:, None, :].to_broadcast([128, 8, NWIN])
                    link(V.tensor_tensor(S, S, live, ALU.mult))
                    link(V.tensor_reduce(cst8[:, t, 1, :], S, AX, ALU.add))
                    link(V.tensor_scalar(cst8[:, t, 1, :], cst8[:, t, 1, :], 1e-30, None, ALU.max))
                    link(V.reciprocal(cst8[:, t, 1, :], cst8[:, t, 1, :]))
                    link(V.tensor_tensor(cst8[:, t, 2, :], cst8[:, t, 1, :], gates[:, t, 0:24:3], ALU.mult))
                    V.tensor_tensor(S, S, heads(cst8[:, t, 2, :], NWIN), ALU.mult).then_inc(c_prob.sem, 1)
                dve.wait_ge(sc.ready, sc.filled(l, "ssc2"))
                link(V.tensor_reduce(s64[:, 2:3], sc.bank("ssc2")[0:64, 0:NWIN], AX, ALU.max))
                V.tensor_scalar(s64[:, 5:6], s64[:, 2:3], -SCALE, None, ALU.mult).then_inc(s_cmax.sem, 1)

                def unit_max(u):
                    t = u // 8
                    dve.wait_ge(sc.ready, sc.filled(l, f"sc{u}"))
                    b = sc.bank(f"sc{u}")[:, :].rearrange("p (r k) -> p r k", r=2)
                    diag = b[:, :, 128 * t:128 * t + 128]
                    mask = cst[:, C_CAUS:C_CAUS + 128][:, None, :].to_broadcast([128, 2, 128])
                    link(V.tensor_tensor(diag, diag, mask, ALU.add))
                    link(V.tensor_reduce(st[:, u % 2, 0:2], b[:, :, 0:128 * (t + 1)], AX, ALU.max))
                    V.tensor_scalar(st[:, u % 2, 2:4], st[:, u % 2, 0:2], -SCALE, None, ALU.mult).then_inc(u_max.sem, 1)

                def unit_prob(u):
                    t, c, g = u // 8, (u % 8) // 2, u % 2
                    n, h = 128 * (t + 1), 4 * g + c
                    dve.wait_ge(u_half.sem, u_half.at(l, u + 1))
                    dve.wait_ge(sc.done, sc.emptied(l, f"sc{u}"))
                    link(V.reciprocal(st[:, u % 2, 4:6], st[:, u % 2, 4:6]))
                    link(V.tensor_tensor(st[:, u % 2, 6:8], st[:, u % 2, 4:6], gates[:, t, 3 * h + 1:3 * h + 3], ALU.mult))
                    link(V.tensor_scalar(PS[:, u % 2, 0, 0:n], PS[:, u % 2, 0, 0:n], st[:, u % 2, 6:7], None, ALU.mult))
                    V.tensor_scalar(PS[:, u % 2, 1, 0:n], PS[:, u % 2, 1, 0:n], st[:, u % 2, 7:8], None, ALU.mult).then_inc(u_prob.sem, 1)

                def compressed_in(t):
                    if t == 1:
                        dve.wait_ge(ob.ready, ob.filled(l, "o3"))
                    for a in range(2):
                        b = tr_in(f"pc{t}{a}")
                        V.tensor_copy(PTc[:, 4 * a:4 * a + 4, :], b[0:NWIN, :].rearrange("p (h q) -> p h q", h=4)).then_inc(tb.done, 1)

                def prob_in(u):
                    b = tr_in(f"pt{u}")
                    n = 256 * (u // 8 + 1)
                    if u >= 2 and u % 2 == 0:
                        dve.wait_ge(pv_done.sem, pv_done.at(l, u // 2))
                    elif u >= 3:
                        dve.wait_ge(ob.ready, ob.filled(l, f"o{(u - 2) // 2}"))
                    V.tensor_copy(PT[:, u % 2, 0:n // 128, :], b[:, 0:n].rearrange("p (a q) -> p a q", q=128)).then_inc(tb.done, 1)

                def sample_probs():
                    dve.wait_ge(sc.done, sc.emptied(l, "ssc2"))
                    dve.wait_ge(gate_in.sem, gate_in.at(l, 32))
                    link(V.reciprocal(s64[:, 6:9], s64[:, 6:9]))
                    link(V.tensor_tensor(s64[:, 9:10], s64[:, 8:9], gate64[:, 0:1], ALU.mult))
                    link(V.tensor_tensor(s64[:, 10:12], s64[:, 6:8], gate64[:, 1:3], ALU.mult))
                    link(V.tensor_scalar(C64[:, :], C64[:, :], s64[:, 9:10], None, ALU.mult))
                    link(V.tensor_scalar(P64[:, 0, :], P64[:, 0, :], s64[:, 10:11], None, ALU.mult))
                    V.tensor_scalar(P64[:, 1, :], P64[:, 1, :], s64[:, 11:12], None, ALU.mult).then_inc(s_prob.sem, 1)
                    dve.wait_ge(s_prob.sem, s_prob.at(l, 1))
                    link(V.tensor_scalar(An[:, 0, :], cst[0:64, C_M8:C_M8 + 8], P64[:, 0, PAST:NKEY], None, ALU.mult))
                    V.tensor_scalar(An[:, 1, :], cst[0:64, C_M8:C_M8 + 8], P64[:, 1, PAST:NKEY], None, ALU.mult).then_inc(s_anew.sem, 1)

                def sample_probs_in():
                    b = tr_in("spt")
                    link(V.tensor_copy(PTs[:, :, :], b[:, 0:256].rearrange("p (n r) -> p n r", n=4)))
                    V.tensor_copy(PTcs[:, :], b[0:NWIN, 256:320]).then_inc(tb.done, 1)
                    b = tr_in("snew")
                    V.tensor_copy(Pn[:, :, :], b[0:8, 0:128].rearrange("p (r n) -> p r n", r=2)).then_inc(tb.done, 1)

                def log_decays_in():
                    b = tr_in("la01")
                    V.tensor_copy(xla[:, 0:2, :], b[:, :].rearrange("p (g n) -> p g n", g=2)).then_inc(tb.done, 1)
                    b = tr_in("la2")
                    V.tensor_copy(xla[0:NS, 2, :], b[0:NS, 0:256]).then_inc(tb.done, 1)

                def log_decays():
                    dve.wait_ge(la_e.sem, la_e.at(l, 1))
                    V.scalar_tensor_tensor(xla[:, :, :], xla[:, :, :], 0.0, lla, ALU.min, ALU.subtract).then_inc(la_t.sem, 1)

                def sample_key(s):
                    if s >= 2:
                        dve.wait_ge(tb.ready, tb.filled(l, f"SU{s - 2}"))
                    V.tensor_scalar(kz[:, s % 2, :], gltok[0:NS, 2, 0:256], cst[0:NS, C_KD + s:C_KD + s + 1], None, ALU.mult).then_inc(kz_d.sem, 1)

                def state(t, ch):
                    k = 2 * t + ch
                    b = tr_in(f"U{t}{ch}")
                    if k >= 2:
                        dve.wait_ge(ob.ready, ob.filled(l, f"go{(k - 1) // 2}1"))
                    for hp in range(2):
                        for h2 in range(2):
                            new = Sp[64 * h2:64 * h2 + 64, k % 2, hp, :]
                            upd = b[64 * h2:64 * h2 + 64, 256 * hp + 128 * h2:256 * hp + 128 * h2 + 128]
                            if k == 0:
                                ins = V.tensor_copy(new, upd)
                            else:
                                ins = V.scalar_tensor_tensor(new, Sp[64 * h2:64 * h2 + 64, (k - 1) % 2, hp, :],
                                                             EB[64 * h2:64 * h2 + 64, 0, hp, 64 * ch + 63:64 * ch + 64], upd, ALU.mult, ALU.add)
                            if hp + h2 < 2:
                                link(ins)
                            else:
                                ins.then_inc(tb.done, 1)
                    dve.wait_ge(tb.done, tb.emptied(l, f"U{t}{ch}"))
                    V.tensor_copy(st[:, 0, 0:1], Sp[:, k % 2, 0, 0:1]).then_inc(g_state.sem, 1)

                def decays_in(t):
                    b = tr_in(f"aft{t}")
                    V.tensor_copy(kd, b[:, 0:256]).then_inc(tb.done, 1)

                def gla_factors(t):
                    dve.wait_ge(sc.done, sc.emptied(l, f"gB{t}"))
                    q, k = glT[:, 0:2, 128 * t:128 * t + 128], glT[:, 2:4, 128 * t:128 * t + 128]
                    if t == 1:
                        dve.wait_ge(ob.ready, ob.filled(l, "go01"))
                    link(V.scalar_tensor_tensor(qe, q, DK ** -0.5, EB[:, 0, :, :], ALU.mult, ALU.mult))
                    link(V.scalar_tensor_tensor(qm, q, DK ** -0.5, EB[:, 1, :, :], ALU.mult, ALU.mult))
                    link(V.tensor_tensor(km, k, EB[:, 2, :, :], ALU.mult))
                    dve.wait_ge(g_ea.sem, g_ea.at(l, t + 1))
                    V.tensor_tensor(kd, kd, gltok[:, t, 0:256], ALU.mult).then_inc(g_q.sem, 1)

                def gla_scores_in(t):
                    for h2 in range(2):
                        b = tr_in(f"gA{t}{h2}")
                        V.tensor_tensor(gAs[:, h2:4:2, :], b[:, 0:256].rearrange("p (h t) -> p h t", h=2),
                                        cst[:, C_GM:C_GM + 128][:, None, :].to_broadcast([128, 2, 128]), ALU.mult).then_inc(tb.done, 1)

                def sample_state(s):
                    if s == 0:
                        dve.wait_ge(state_in.sem, state_in.at(l, 64))
                        dve.wait_ge(ela_d.sem, ela_d.at(l, 1))
                    b = tr_in(f"SU{s}")
                    for hp in range(2):
                        for h2 in range(2):
                            S = Sst[64 * h2:64 * h2 + 64, s, hp, :]
                            upd = b[64 * h2:64 * h2 + 64, 256 * hp + 128 * h2:256 * hp + 128 * h2 + 128]
                            ins = V.scalar_tensor_tensor(S, S, ela[64 * h2:64 * h2 + 64, hp, s:s + 1], upd, ALU.mult, ALU.add)
                            if hp + h2 < 2:
                                links[0] += 1
                                ins.then_inc(dve_link.sem, 1)
                            else:
                                ins.then_inc(tb.done, 1)
                    dve.wait_ge(tb.done, tb.emptied(l, f"SU{s}"))
                    V.tensor_copy(st[:, 0, 0:1], Sst[:, s, 0, 0:1]).then_inc(s_state.sem, 1)

                def head_norm(i):
                    c0, m = TG[i]
                    dve.wait_ge(ob.done, ob.emptied(l, f"go{i}1" if i < 2 else "gos1"))
                    dve.wait_ge(r_rs.sem, r_rs.at(l, i + 1))
                    o = ogT[:, :, c0:c0 + m]
                    r = rr[:, 0:4 * m].rearrange("p (h t) -> p h t", h=4)
                    link(V.tensor_tensor(o, o, r, ALU.mult))
                    V.scalar_tensor_tensor(o, o, lv[:, V_GN:V_GN + 1], grT[:, :, c0:c0 + m], ALU.mult, ALU.mult).then_inc(og_d.sem, 1)

                for k in range(18):
                    if k == 2:
                        compressed_in(0)
                    if k >= 2:
                        prob_in(k - 2)
                    if k == 10:
                        compressed_in(1)
                    if 1 <= k <= 16:
                        unit_prob(k - 1)
                    if k < 16:
                        unit_max(k)
                    if k == 1:
                        log_decays_in()
                        sample_probs()
                    elif k == 2:
                        sample_probs_in()
                        log_decays()
                    elif k == 3:
                        b = tr_in("elas")
                        V.tensor_copy(ela[:, :, :], b[:, 0:16].rearrange("p (h s) -> p h s", h=2)).then_inc(tb.done, 1)
                        decays_in(0)
                    elif k == 4:
                        gla_factors(0)
                    elif k == 5:
                        gla_scores_in(0)
                    elif k == 6:
                        state(0, 0)
                        state(0, 1)
                    elif k == 9:
                        decays_in(1)
                    elif k == 10:
                        gla_factors(1)
                        V.tensor_scalar(qs[:, :, :], glT[:, 0:2, SEQ:NT], DK ** -0.5, None, ALU.mult).then_inc(qs_d.sem, 1)
                    elif k == 11:
                        gla_scores_in(1)
                        head_norm(0)
                        sample_key(0)
                        sample_key(1)
                    elif k == 12:
                        state(1, 0)
                    elif k == 14:
                        state(1, 1)
                    elif k == 17:
                        head_norm(1)
                    if k in (13, 15, 16, 17):
                        for s in range(2 * max(0, k - 14), 2 * max(0, k - 14) + 2):
                            sample_state(s)
                            if s + 2 < NS:
                                sample_key(s + 2)
                head_norm(2)
                dve.wait_ge(og_d.sem, og_d.at(l, 3))
                V.tensor_copy(st[:, 0, 0:1], ogT[:, 0, 0:1]).then_inc(mixers_done.sem, 1)
                dve.wait_ge(mg_sig.sem, mg_sig.at(l, 16))
                for i in range(8):
                    for a in range(2):
                        dve.wait_ge(acc.done, acc.emptied(l, f"up{2 * i + a}"))
                        m = mgT[:, 8 * a + i, :]
                        link(V.tensor_tensor(m, m, upb[:, a, :], ALU.mult))
                    V.tensor_tensor(mgT[:, i, :], mgT[:, i, :], mgT[:, 8 + i, :], ALU.add).then_inc(up_m.sem, 1)

                def residual(name, res, i):
                    dve.wait_ge(acc.done, acc.emptied(l, f"{name}{i}"))
                    V.scalar_tensor_tensor(hT[:, i, :], hT[:, i, :], ALPHA, yb[:, i % 2, :], ALU.mult, ALU.add).then_inc(res.sem, 1)

                def split_lo(t):
                    dve.wait_ge(w_hi.sem, w_hi.at(l, t - T_M1 + 1))
                    w = wt[t % RING]
                    V.tensor_tensor(wlo[t % RING][:, :, :], w[:, :].rearrange("p (k n) -> p k n", k=KD),
                                    whi[(t - T_M1) % 2][:, :, :], ALU.subtract).then_inc(w_lo.sem, 1)

                def norm(i, vg, res):
                    dve.wait_ge(sc.done, sc.emptied(l, f"ln{i + 1}m"))
                    dve.wait_ge(res.sem, res.at(l, 8))
                    link(V.tensor_tensor(musq, mu, mu, ALU.mult))
                    dve.wait_ge(sc.done, sc.emptied(l, f"ln{i + 1}v"))
                    link(V.tensor_tensor(rs, rs, musq, ALU.subtract))
                    V.tensor_scalar(rs, rs, 0.0, None, ALU.max).then_inc(ln_var.sem, 1)
                    for c in range(KD + 2):
                        if c in (0, 4):
                            link(V.tensor_tensor(hT[:, c:c + 4, :], hT[:, c:c + 4, :], bc(mu, 4), ALU.subtract))
                        if c == 0:
                            dve.wait_ge(ln_rs.sem, ln_rs.at(l, i + 1))
                        if c < KD:
                            V.scalar_tensor_tensor(hT[:, c, :], hT[:, c, :], lv[:, vg + c:vg + c + 1], rs, ALU.mult, ALU.mult).then_inc(ln_sc.sem, 1)
                        if i == 0 and c >= 2:
                            dve.wait_ge(h_hi_d.sem, h_hi_d.at(l, c - 1))
                            V.tensor_tensor(h_lo[:, c - 2, :], hT[:, c - 2, :], h_hi[:, c - 2, :], ALU.subtract).then_inc(h_lo_d.sem, 1)

                for i in range(8):
                    residual("out", res1, i)
                    if i == 5:
                        split_lo(T_M1)
                norm(0, V_L1G, res1)
                split_lo(T_M1 + 1)
                for i in range(32):
                    dve.wait_ge(hid_hi_d.sem, hid_hi_d.at(l, i + 1))
                    link(V.tensor_tensor(yb[:, i % 2, :], yb[:, i % 2, :], yb[:, i % 2, :], ALU.mult))
                    if i == 8:
                        dve.wait_ge(stored, l * (16 * STORES) + 16 * STORES + 16)
                    V.tensor_tensor(hid_lo[:, i, :], yb[:, i % 2, :], hid_hi[:, i, :], ALU.subtract).then_inc(hid_lo_d.sem, 1)
                    if i % 2 == 1:
                        split_lo(T_M1 + i // 2 + 2)
                for t in range(16):
                    if t % 4 == 3:
                        for i in range(t // 2 - 1, t // 2 + 1):
                            residual("m2_", res2, i)
                    if t < 14:
                        split_lo(T_M2 + t + 2)
                norm(1, V_L2G, res2)
                assert links[0] == dve_link.per, links[0]

            for n in range(6):
                g, half = n // 2, n % 2
                m = TG[g][1]
                dve.wait_ge(ini["tr"], 8 + n)
                V.tensor_copy(xin[0:m, g, 512 * half:512 * half + 512], tb.banks[n % 2][0:m, :]).then_inc(ini["trc"], 1)


INS = ["x_prompt", "x_sample", "cache_nsa_kv", "cache_win_kv", "state_gla", "page_table", "ln_in_g", "ln_in_b", "w_in",
       "cmp_k_pe", "cmp_k_w1", "cmp_k_w2", "cmp_v_pe", "cmp_v_w1", "cmp_v_w2", "gla_w_a2", "gla_b_a", "gla_norm_g",
       "w_nsa_up", "w_gla_up", "w_out", "ln1_g", "ln1_b", "mlp_w1", "mlp_w2", "ln2_g", "ln2_b"]
OUTS = [("y_prompt", (1, SEQ, D)), ("y_sample", (NS, 1, D)), ("nsa_kv_prompt", (1, LAYERS, SEQ, 4, GROUPS, HD)),
        ("win_kv_prompt", (1, LAYERS, SEQ, 2, GROUPS, HD)), ("gla_state_prompt", (1, LAYERS, GH, DK, DV)),
        ("nsa_kv_sample", (NS, LAYERS, 1, 4, GROUPS, HD)), ("win_kv_sample", (NS, LAYERS, PAST, 2, GROUPS, HD)),
        ("gla_state_sample", (NS, LAYERS, GH, DK, DV))]


def constants(np):
    c = np.zeros((128, C_N), np.float32)
    i = np.arange(128)
    c[:, C_ID:C_ID + 128] = np.eye(128)
    c[:, C_ONE:C_ONE + 128] = 1.0
    for m in range(128):
        c[m + 32 if m % 64 < 32 else m - 32, C_ROT + m] = -1.0 if m % 64 < 32 else 1.0
    c[:, C_CAUS:C_CAUS + 128] = np.where(i[None, :] <= i[:, None], 0.0, NEG)
    same = i[:, None] // CH == i[None, :] // CH
    u, t = i[:, None], i[None, :]
    mid = t // CH * CH + CH // 2 - 1
    c[:, C_TRI:C_TRI + 128] = same * (u <= t) / TAU
    c[:, C_MID:C_MID + 128] = same * ((u <= t).astype(np.float32) - (u <= mid)) / TAU
    c[:, C_AFT:C_AFT + 128] = same * (u > t) / TAU
    c[:, C_GM:C_GM + 128] = same * (u <= t)
    half = HD // 2
    inv = np.float32(10000.0) ** (-np.arange(half, dtype=np.float32) / np.float32(half))
    pos = np.concatenate([np.arange(SEQ), np.full(NS, PAST)]).astype(np.float32)
    ang = (pos[None, :] * inv[i % half][:, None]).astype(np.float32)
    c[:, C_COS:C_COS + NT] = np.cos(ang)
    c[:, C_SIN:C_SIN + NT] = np.sin(ang)
    for tile in range(2):
        live = (np.arange(NWIN) * CSTR + CLEN - 1)[None, :] <= (tile * 128 + i)[:, None]
        c[:, C_CADD + 15 * tile:C_CADD + 15 * tile + 15] = np.where(live, 0.0, NEG)
        c[:, C_C01 + 15 * tile:C_C01 + 15 * tile + 15] = live
    for r in range(64):
        c[r, C_M8 + (r % 32) // 4] = 1.0
    for s in range(NS):
        c[s, C_KD + s] = 1.0
    c[:, C_EPS] = EPS
    return c


def kernel(**inputs):
    import numpy as np
    import concourse.bacc as bacc
    from concourse.bass_utils import run_bass_kernel_spmd

    nc = bacc.Bacc("TRN2", target_bir_lowering=False, num_devices=1)
    arrays = {f"in_{n}": np.ascontiguousarray(inputs[n]) for n in INS}
    arrays["in_consts"] = constants(np)
    A = {n[3:]: nc.dram_tensor(n, a.shape, mybir.dt.from_np(a.dtype), kind="ExternalInput").ap() for n, a in arrays.items()}
    O = {n: nc.dram_tensor(f"out_{n}", s, F32, kind="ExternalOutput").ap() for n, s in OUTS}
    build(nc, A, O)
    r = run_bass_kernel_spmd(nc, [arrays], core_ids=[0])
    return tuple(r.results[0][f"out_{n}"] for n, _ in OUTS)
```

```python
from contextlib import ExitStack

import concourse.bass as bass
from concourse import mybir

F32 = mybir.dt.float32
F32R = mybir.dt.float32r
I32 = mybir.dt.int32
ALU = mybir.AluOpType
ACT = mybir.ActivationFunctionType
AX = mybir.AxisListType.X

D = 1024
KD = D // 128
SEQ, NS = 256, 8
NT = SEQ + NS
LAYERS = 2
HEADS, GROUPS, HD = 8, 2, 64
SLOTS = 6
SCALE = HD ** -0.5
NWIN = 15
CSTR, CLEN = 16, 32
PAST = 256
NKEY = PAST + 1
GH, DK, DV = 4, 64, 128
CH = 64
RANK = 16
TAU = 16.0
EPS = 1e-5
ALPHA = (2.0 * LAYERS) ** 0.25
NEG = -1e30
GELU_C = 0.7978845608028654
OFF_Q, OFF_KV, OFF_G = 0, 512, 1280
OFF_GQ, OFF_GK, OFF_GV, OFF_LR, OFF_GR, OFF_MG = 1304, 1560, 1816, 2328, 2344, 2856

C_ID, C_ONE, C_ROT, C_CAUS, C_TRI, C_MID, C_AFT, C_GM = (128 * i for i in range(8))
C_COS = 1024
C_SIN = C_COS + NT
C_CADD = C_SIN + NT
C_C01 = C_CADD + 2 * NWIN
C_M8 = C_C01 + 2 * NWIN
C_KD = C_M8 + 8
C_EPS = C_KD + 8
C_N = C_EPS + 1

V_L1G, V_L1B, V_L2G, V_L2B, V_GN, V_PEK, V_PEV, V_N = 0, 8, 16, 24, 32, 33, 49, 65


class Banks:

    def __init__(self, plan, ready, done, banks):
        self.plan, self.ready, self.done, self.banks = plan, ready, done, banks
        self.total = len(plan)
        self.at = {name: i for i, name in enumerate(plan)}
        assert len(self.at) == self.total

    def bank(self, name):
        return self.banks[self.at[name] % 2]

    def filled(self, l, name):
        return l * self.total + (self.at[name] + 1)

    def emptied(self, l, name):
        return l * self.total + (self.at[name] + 3)

    def free(self, l, name):
        return l * self.total + (2 + max(self.at[name] - 1, 0))


class Steps:

    def __init__(self, sem, per_layer):
        self.sem, self.per = sem, per_layer

    def at(self, l, n):
        return l * self.per + n


STORES = 13
LINKS = (299, 35)


def build(nc, A, O):
    RING = 4
    TILES = 61
    T_Q, T_KV, T_GLA, T_GR, T_CMP, T_MG, T_UP, T_OUT, T_M1, T_M2 = 0, 2, 5, 9, 11, 13, 21, 25, 29, 45

    SPLIT_A, SPLIT_B = T_GLA + 2, T_UP + 1
    SPLIT_N = SPLIT_A - 1 + TILES - SPLIT_B

    def split_no(t):
        assert 1 <= t < SPLIT_A or t >= SPLIT_B
        return t - 1 if t < SPLIT_A else t - SPLIT_B + SPLIT_A - 1

    acc_plan = ([f"q{i}" for i in range(4)] + [f"kv{i}" for i in range(6)] + [f"gla{i}" for i in range(4)] + ["small"] + [f"gla{i}" for i in range(4, 8)]
                + [f"gr{i}" for i in range(4)] + [f"mg{i}" for i in range(16)]
                + [f"up{i}" for i in range(16)] + [f"out{i}" for i in range(8)]
                + [f"m1_{i}" for i in range(32)] + [f"m2_{i}" for i in range(8)])
    t_plan = (["vec"] + [f"rope{i}" for i in range(6)] + [f"kvt{i}" for i in range(6)]
              + sum([[f"pairs{s}", f"keys{s}"] for s in range(NS)], []) + [f"glt{i}" for i in range(6)] + ["gate", "kcmp"] + [f"vcmp{i}" for i in range(3)]
              + ["la01", "la2", "pc00", "pc01", "pt0", "spt", "snew", "pt1", "elas", "aft0", "pt2", "pt3", "gA00", "gA01",
                 "pt4", "U00", "U01", "pt5", "SU0", "SU1", "pt6", "SU2", "SU3", "pt7", "aft1", "pt8", "pc10", "pc11", "pt9", "gA10", "gA11", "pt10", "U10",
                 "pt11", "SU4", "SU5", "pt12", "U11", "pt13", "SU6", "SU7", "pt14", "pt15"])
    sc_plan = (["ssc0", "ssc1", "hidk", "hidv", "csc00", "csc01", "csc10", "csc11", "ssc2"] + [f"sc{u}" for u in range(3)] + ["gB0"] + [f"sc{u}" for u in range(3, 9)]
               + ["gB1", "sc9", "rms0"] + [f"sc{u}" for u in range(10, 16)] + ["rms1", "rms2"] + ["ln1m", "ln1v", "ln2m", "ln2v"])
    o_plan = ["o0", "o1", "so", "o2", "go00", "go01", "o3", "o4", "o5", "go10", "go11", "o6", "o7", "gos"]

    with ExitStack() as ctx:
        def sb(name, shape, dt=F32):
            return ctx.enter_context(nc.sbuf_tensor(name, shape, dt))

        def pb(name):
            return ctx.enter_context(nc.psum_tensor(name, [128, 512], F32))

        def sem(name):
            return ctx.enter_context(nc.semaphore(name))

        BIG_N = 40 * NT + 3 * SLOTS * 128 + 3 * 768 + 2 * 1024
        with ExitStack() as shared:
            def part(name, shape):
                return shared.enter_context(nc.sbuf_tensor(name, shape, F32R))

            wlo = [part(f"wlo{i}", [128, KD, 256]) for i in range(RING)]
            whi = [part(f"whi{i}", [128, KD, 256]) for i in range(2)]
            h_parts = part("h_parts", [128, 2, KD, NT])
            big_parts = part("big_parts", [128, BIG_N])
        wt = [sb(f"wt{i}", [128, 2048]) for i in range(RING)]
        Vs = sb("Vs", [128, 2, NS, 2, 128])
        mgT = sb("mgT", [128, 16, NT])
        BIG = sb("BIG", [128, BIG_N])
        assert 64 * NT <= BIG_N
        h_hi, h_lo = h_parts[:, 0], h_parts[:, 1]

        def rows(r0, n, off=0):
            a = off + r0 * NT
            assert a + n * NT <= BIG_N
            return big_parts[:, a:a + n * NT].rearrange("p (c t) -> p c t", c=n)

        hid_hi, hid_lo = rows(0, 32), rows(32, 32)
        x_hi, x_lo = rows(24, 8), rows(32, 8)
        u_off = 40 * NT + 3 * SLOTS * 128
        u_hi, u_lo = rows(0, 8, u_off), rows(8, 8, u_off)
        m_hi, m_lo = rows(4, 8), rows(24, 8)
        cst = sb("cst", [128, C_N])
        ident, ones = cst[:, C_ID:C_ID + 128], cst[:, C_ONE:C_ONE + 128]
        epsc = cst[:, C_EPS:C_EPS + 1]
        ptab = sb("ptab", [1, 16], I32)
        hT = sb("hT", [128, KD, NT])
        wsm = sb("wsm", [128, KD, 56])
        small = sb("small", [32, NT])
        gateT = sb("gateT", [24, NT])
        AR = BIG[:, 0:40 * NT]
        used = [0]

        def ar(n):
            a = AR[:, used[0]:used[0] + n]
            used[0] += n
            return a

        qT = ar(4 * NT).rearrange("p (c t) -> p c t", c=4)
        qR = ar(4 * NT).rearrange("p (c t) -> p c t", c=4)
        kvT = ar(6 * NT).rearrange("p (c t) -> p c t", c=6)
        glT = ar(8 * NT).rearrange("p (c t) -> p c t", c=8)
        cmpT = ar(2 * 2 * 9 * 128).rearrange("p (j g s i) -> p j g s i", j=2, g=2, s=9)
        assert used[0] <= 40 * NT
        gtmp = cmpT.rearrange("p j g s i -> p (j g s i)")
        tused = [0]

        def tmp(n, rows=128):
            a = gtmp[0:rows, tused[0]:tused[0] + n]
            tused[0] += n
            assert tused[0] <= 4608
            return a

        grT = sb("grT", [128, 4, NT])
        sq = mgT[:, 8:16, :]
        gre = mgT[:, 12:16, :]
        kTs = sb("kTs", [128, 2, 2, NKEY])
        u0 = 40 * NT
        kvtok = BIG[:, u0:u0 + 3 * SLOTS * 128].rearrange("p (g n) -> p g n", g=3)
        u0 += 3 * SLOTS * 128
        gltok = BIG[:, u0:u0 + 3 * 768].rearrange("p (g n) -> p g n", g=3)
        u0 += 3 * 768
        stg = BIG[:, u0:u0 + 2048].rearrange("p (s r n) -> p s r n", s=2, r=2)
        stw = sb("stw", [128, 2, 2, 128])
        Sst = sb("Sst", [128, NS, 2, 128])
        Sp = sb("Sp", [128, 2, 2, 128])
        vecr = sb("vecr", [V_N, 128])
        lv = sb("lv", [128, V_N])
        wa2 = sb("wa2", [RANK + 1, 256])
        w2 = sb("w2", [128, 2, 64])
        gates = sb("gates", [128, 3, 24])
        gate64 = sb("gate64", [64, 3])
        tmpA = cmpT.rearrange("p j g s i -> p (j g s i)")[:, 0:NT]
        hb = sb("hb", [128, 2])
        kc = sb("kc", [128, 9 * NWIN])
        cv = sb("cv", [NWIN, (9 + 8) * 128])
        vc = cv[:, 0:9 * 128].rearrange("p (s d) -> p s d", s=9)
        PS = sb("PS", [128, 2, 2, 256])
        pflat = PS[:, :, :, :].rearrange("p u r k -> p (u r k)")
        hx = pflat[:, 0:540].rearrange("p (j n) -> p j n", j=2)
        hy = pflat[:, 540:810]
        PT = sb("PT", [128, 2, 4, 128])
        st = sb("st", [128, 2, 8])
        CS = sb("CS", [128, 2, 8, NWIN])
        cst8 = sb("cst8", [128, 2, 3, 8])
        PTc = cv[:, 9 * 128:17 * 128].rearrange("p (h q) -> p h q", h=8)
        onT = sb("onT", [128, 4, NT])
        ogT = glT[:, 4:8, :]
        Qflat = sb("Qz", [128, 2 * NS * 64 + 64])
        Qz = Qflat[:, 0:2 * NS * 64].rearrange("p (r s x) -> p r s x", r=2, s=NS)
        P64 = sb("P64", [64, 2, NKEY])
        C64 = sb("C64", [64, NWIN])
        s64 = sb("s64", [64, 12])
        PTs = sb("PTs", [128, 4, 64])
        PTcs = sb("PTcs", [NWIN, 64])
        An = sb("An", [64, 2, 8])
        Pn = sb("Pn", [8, 2, 64])
        xla = sb("xla", [128, 3, 256])
        lla = tmp(768).rearrange("p (g n) -> p g n", g=3)
        ela = sb("ela", [128, 2, 8])
        pacc = sb("pacc", [128, 2, 128])
        qsz = sb("qsz", [128, 2, NS, 2])
        EB = tmp(768).rearrange("p (a h n) -> p a h n", a=3, h=2)
        kd = tmp(256)
        qe, qm, km = (tmp(256).rearrange("p (h n) -> p h n", h=2) for _ in range(3))
        gAs = tmp(512).rearrange("p (h n) -> p h n", h=4)
        osq = tmp(512)
        rr = tmp(512)
        kz = tmp(512, NS).rearrange("p (s n) -> p s n", s=2)
        upb = qT[:, 0:2, :]
        yb, mu, rs, musq = onT[:, 0:2, :], onT[:, 2, :], onT[:, 3, :], onT[:, 0, :]
        sumx, sumq = mu, rs
        xin = mgT[:, 0:12, :].rearrange("p a b -> p (a b)")[:, 0:3072].rearrange("p (g f) -> p g f", g=3)

        acc = Banks(acc_plan, sem("acc_ready"), sem("acc_done"), [pb("acc0"), pb("acc1")])
        tb = Banks(t_plan, sem("tr_ready"), sem("tr_done"), [pb("tr0"), pb("tr1")])
        sc = Banks(sc_plan, sem("sc_ready"), sem("sc_done"), [pb("sc0"), pb("sc1")])
        ob = Banks(o_plan, sem("o_ready"), sem("o_done"), [pb("o0"), pb("o1")])

        w_landed = [sem(f"w_landed{i}") for i in range(RING)]
        m2_part = Steps(sem("m2_part"), 12)
        const_in, tables_in = sem("const_in"), sem("tables_in")
        x_in = sem("x_in")
        lnv_in = sem("lnv_in")
        wsm_in = Steps(sem("wsm_in"), 32)
        vec_in = Steps(sem("vec_in"), 16 * 7)
        par_in = Steps(sem("par_in"), 16 * 4)
        cache_in = [Steps(sem(f"cache_in{i}"), 16 * 3 * 4) for i in range(2)]
        mixers_done = Steps(sem("mixers_done"), 1)
        val_in = Steps(sem("val_in"), 16 * NS)
        val_copied = Steps(sem("val_copied"), NS)
        state_in = Steps(sem("state_in"), 64)
        gate_in = Steps(sem("gate_in"), 32)
        stored = sem("stored")
        pe_passed, pool_passed, sp_passed = sem("pe_passed"), sem("pool_passed"), sem("sp_passed")

        ini = {n: sem("in_" + n) for n in ("add", "tr", "trc", "sum", "mu", "cen", "sq", "var", "rs", "h", "zero")}
        dve_link = Steps(sem("dve_link"), 0)
        act_link = Steps(sem("act_link"), 0)
        DVE_LINKS, ACT_LINKS = LINKS
        dve_link.per, act_link.per = DVE_LINKS, ACT_LINKS
        h_ready = Steps(sem("h_ready"), 16)
        h_hi_d, h_lo_d = Steps(sem("h_hi_d"), 8), Steps(sem("h_lo_d"), 8)
        w_hi, w_lo = Steps(sem("w_hi"), 2 * SPLIT_N), Steps(sem("w_lo"), 2 * SPLIT_N)
        x_hi_d, x_lo_d = Steps(sem("x_hi_d"), 2), Steps(sem("x_lo_d"), 2)
        u_hi_d, u_lo_d = Steps(sem("u_hi_d"), 2), Steps(sem("u_lo_d"), 2)
        m_hi_d, m_lo_d = Steps(sem("m_hi_d"), 8), Steps(sem("m_lo_d"), 8)
        hid_hi_d = Steps(sem("hid_hi_d"), 32)
        q_rot = Steps(sem("q_rot"), 6)
        gla_silu = Steps(sem("gla_silu"), 1)
        pairs = Steps(sem("pairs"), 1)
        gre_sig = Steps(sem("gre_sig"), 1)
        gate_exp = Steps(sem("gate_exp"), 1)
        gate_sig = Steps(sem("gate_sig"), 1)
        hid_u = Steps(sem("hid_u"), 2)
        hid_e = Steps(sem("hid_e"), 2)
        hid_g = Steps(sem("hid_g"), 2)
        mg_sig = Steps(sem("mg_sig"), 16)
        c_shift = Steps(sem("c_shift"), 2)
        c_exp = Steps(sem("c_exp"), 2)
        s_cmax = Steps(sem("s_cmax"), 1)
        u_half = Steps(sem("u_half"), 16)
        pv_done = Steps(sem("pv_done"), 8)
        c_prob = Steps(sem("c_prob"), 2)
        u_max = Steps(sem("u_max"), 16)
        u_prob = Steps(sem("u_prob"), 16)
        s_qz = Steps(sem("s_qz"), 1)
        s_keys = Steps(sem("s_keys"), 7)
        s_max = Steps(sem("s_max"), 1)
        s_prob = Steps(sem("s_prob"), 1)
        s_anew = Steps(sem("s_anew"), 1)
        pe_sum = Steps(sem("pe_sum"), 2)
        la_e = Steps(sem("la_e"), 1)
        la_t = Steps(sem("la_t"), 1)
        ela_d = Steps(sem("ela_d"), 1)
        kz_d = Steps(sem("kz_d"), NS)
        qs_d = Steps(sem("qs_d"), 1)
        g_ea = Steps(sem("g_ea"), 2)
        g_q = Steps(sem("g_q"), 2)
        g_state = Steps(sem("g_state"), 4)
        s_state = Steps(sem("s_state"), 8)
        r_sq = Steps(sem("r_sq"), 3)
        r_rs = Steps(sem("r_rs"), 3)
        og_d = Steps(sem("og_d"), 3)
        up_m = Steps(sem("up_m"), 8)
        res1 = Steps(sem("res1"), 8)
        res2 = Steps(sem("res2"), 8)
        hid_lo_d = Steps(sem("hid_lo_d"), 32)
        ln_var = Steps(sem("ln_var"), 2)
        ln_sq = Steps(sem("ln_sq"), 16)
        ln_sc = Steps(sem("ln_sc"), 16)
        ln_rs = Steps(sem("ln_rs"), 2)
        ln_sum = Steps(sem("ln_sum"), 28)

        TG = [(0, 128), (128, 128), (256, NS)]
        updates_at = {6: (0, 1), 7: (2, 3), 12: (4, 5), 14: (6, 7)}
        block = ctx.enter_context(nc.Block())

        def tile_used(l, p):
            if T_CMP <= p < T_CMP + 2:
                return sc.ready, sc.filled(l, ("hidk", "hidv")[p - T_CMP])
            if p >= T_M2:
                cg, kg = (p - T_M2) // 4, (p - T_M2) % 4
                if kg < 3:
                    return m2_part.sem, m2_part.at(l, 3 * cg + kg + 1)
                return acc.ready, acc.filled(l, f"m2_{2 * cg + 1}")
            name = (f"q{2 * (p - T_Q) + 1}" if p < T_KV else f"kv{2 * (p - T_KV) + 1}" if p < T_GLA
                    else f"gla{2 * (p - T_GLA) + 1}" if p < T_GR else f"gr{2 * (p - T_GR) + 1}" if p < T_CMP
                    else f"mg{2 * (p - T_MG) + 1}" if p < T_UP else f"up{4 * (p - T_UP) + 3}" if p < T_OUT
                    else f"out{2 * (p - T_OUT) + 1}" if p < T_M1 else f"m1_{2 * (p - T_M1) + 1}")
            return acc.ready, acc.filled(l, name)

        @block.sync
        def _(sp):
            sp.dma_start(cst[:, 0:C_ROT], A["consts"][:, 0:C_ROT]).then_inc(const_in, 16)
            sp.dma_start(xin[:, 0, :], A["x_prompt"][0, 0:128]).then_inc(x_in, 16)
            sp.dma_start(xin[:, 1, :], A["x_prompt"][0, 128:256]).then_inc(x_in, 16)
            sp.dma_start(xin[0:NS, 2, :], A["x_sample"].rearrange("s t f -> (s t) f")).then_inc(x_in, 16)
            sp.dma_start(ptab[:, :], A["page_table"].rearrange("(a s) n -> a (s n)", a=1)).then_inc(x_in, 16)
            sp.dma_start(cst[:, C_ROT:C_N], A["consts"][:, C_ROT:C_N]).then_inc(tables_in, 16)
            sp.wait_ge(x_in, 64)
            with sp.Fori(0, LAYERS) as l:
                wl = lambda name: A[name][bass.ds(l, 1)].rearrange("a k n -> (a k) n")
                w_in = wl("w_in").rearrange("(k p) n -> p k n", p=128)
                w1 = wl("mlp_w1").rearrange("(k p) n -> p k n", p=128)
                w2m = wl("mlp_w2").rearrange("(kg k p) n -> kg p k n", p=128, k=KD)
                wo = wl("w_out").rearrange("(k p) n -> p k n", p=128)
                wn = wl("w_nsa_up").rearrange("(g c d) n -> g d c n", g=2, c=4)
                wg = wl("w_gla_up").rearrange("(c p) n -> p c n", p=128)

                def slot_free(t):
                    if t < RING:
                        return acc.done, 2 + l * acc.total
                    return tile_used(l, t - RING)

                def load(t, parts):
                    free, v = slot_free(t)
                    v = sp.snap(v)
                    sp.wait_ge(free, v)
                    for i, (dst, src) in enumerate(parts):
                        ins = sp.dma_start(dst, src)
                        ins.then_inc(w_landed[t % RING], 16)

                def t8(t):
                    return wt[t % RING][:, :].rearrange("p (k n) -> p k n", k=KD)

                def cols(t, w, c0):
                    load(t, [(t8(t), w[:, :, c0:c0 + 256])])

                def cached(s):
                    if s >= 2:
                        sp.wait_ge(val_copied.sem, val_copied.at(l, s - 1))
                        sp.sem_inc(sp_passed, 1)
                        sp.wait_ge(tb.done, tb.emptied(l, f"keys{s - 2}"))
                        sp.sem_inc(sp_passed, 1)
                    for pg in range(2):
                        page = sp.value_load(ptab[0:1, 2 * s + pg:2 * s + pg + 1], min_val=0, max_val=A["cache_nsa_kv"].shape[0] - 1)
                        src = A["cache_nsa_kv"][bass.ds(page, 1), bass.ds(l, 1)].rearrange("a b (i r) j g d -> (a b i) r (j g d)", r=2)
                        sp.dma_start(stg[64 * pg:64 * pg + 64, s % 2, :, :], src).then_inc(cache_in[s % 2].sem, 16)
                    win = A["cache_win_kv"][s, bass.ds(l, 1)].rearrange("a (i r) j g d -> (a i) r (j g d)", r=2)
                    sp.dma_start(stw[:, s % 2, :, :], win[:, :, 0:128]).then_inc(cache_in[s % 2].sem, 16)
                    sp.dma_start(Vs[:, 1, s, :, :], win[:, :, 128:256]).then_inc(val_in.sem, 16)

                for i in range(2):
                    dst = wt[(T_Q + i) % RING][:, :].rearrange("p (k c g n) -> p k c g n", k=KD, c=2, g=2)
                    load(T_Q + i, [(dst[:, :, c, g, :], w_in[:, :, OFF_Q + g * 256 + (2 * i + c) * 64:OFF_Q + g * 256 + (2 * i + c) * 64 + 64])
                                   for c in range(2) for g in range(2)])
                for i in range(3):
                    cols(T_KV + i, w_in, OFF_KV + i * 256)

                def cmp_w1(i):
                    dst = wt[(T_CMP + i) % RING][:, :].rearrange("p (k n) -> p k n", k=16)
                    src = wl(("cmp_k_w1", "cmp_v_w1")[i]).rearrange("(k p) n -> p k n", p=128)
                    load(T_CMP + i, [(dst[:, 8 * a:8 * a + 8, :], src[:, 8 * a:8 * a + 8, :]) for a in range(2)])

                for i in range(4):
                    cols(T_GLA + i, w_in, OFF_GQ + i * 256)
                cols(T_GR, w_in, OFF_GR)
                sp.wait_ge(acc.ready, acc.filled(l, "gla3"))
                sp.sem_inc(sp_passed, 1)
                cached(0)
                cached(1)
                cols(T_GR + 1, w_in, OFF_GR + 256)
                cached(2)
                cached(3)
                cmp_w1(0)
                cached(4)
                cached(5)
                cmp_w1(1)
                cached(6)
                cached(7)
                cols(T_MG, w_in, OFF_MG)
                for i in range(1, 8):
                    cols(T_MG + i, w_in, OFF_MG + i * 256)
                for i in range(4):
                    d = t8(T_UP + i)
                    load(T_UP + i, [(d[64 * g:64 * g + 64, 0:4, :], wn[g, :, :, i * 256:i * 256 + 256]) for g in range(2)]
                         + [(d[:, 4:8, :], wg[:, :, i * 256:i * 256 + 256])])
                for i in range(4):
                    cols(T_OUT + i, wo, i * 256)
                for i in range(16):
                    cols(T_M1 + i, w1, i * 256)
                for i in range(16):
                    load(T_M2 + i, [(t8(T_M2 + i), w2m[i % 4, :, :, (i // 4) * 256:(i // 4) * 256 + 256])])

        parts_of = {**{T_Q + i: 4 for i in range(2)}, **{T_CMP + i: 2 for i in range(2)}, **{T_UP + i: 3 for i in range(4)}}
        per_slot = [sum(16 * parts_of.get(t, 1) for t in range(TILES) if t % RING == s) for s in range(RING)]

        def landed(t):
            s = t % RING
            return w_landed[s], per_slot[s], sum(16 * parts_of.get(x, 1) for x in range(t + 1) if x % RING == s)

        @block.gpsimd
        def _(pool):
            pool.memset(vecr[:, :], 0.0).then_inc(ini["zero"], 1)
            pool.wait_ge(ini["zero"], 1)
            pool.dma_start(vecr[0:8, :], A["ln_in_g"].rearrange("(c p) -> c p", p=128)).then_inc(lnv_in, 16)
            pool.dma_start(vecr[8:16, :], A["ln_in_b"].rearrange("(c p) -> c p", p=128)).then_inc(lnv_in, 16)
            pool.memset(small[:, :], 1.0).then_inc(ini["zero"], 1)
            pool.memset(Qz[:, :, :, :], 0.0).then_inc(ini["zero"], 1)
            pool.memset(wsm[:, :, :], 0.0).then_inc(ini["zero"], 1)
            pool.memset(qsz[:, :, :, :], 0.0).then_inc(ini["zero"], 1)
            pool.memset(xla[:, 2, :], 0.0).then_inc(ini["zero"], 1)
            pool.memset(gates[:, 2, :], 0.0).then_inc(ini["zero"], 1)
            pool.dma_start(O["win_kv_sample"][0:1].rearrange("s l t j g d -> (s l) (t j g d)")[:, 0:(PAST - 1) * 256],
                           A["cache_win_kv"][0:1].rearrange("s l t j g d -> (s l) (t j g d)")[:, 256:PAST * 256]).then_inc(stored, 16)
            pool.wait_ge(ini["zero"], 7)
            pool.wait_ge(ini["trc"], 7)
            with pool.Fori(0, LAYERS) as l:
                def row(name, pat, **kw):
                    return A[name][bass.ds(l, 1)].rearrange(pat, **kw)

                wv = A["w_in"][bass.ds(l, 1)].rearrange("a (k p) n -> p (a k) n", p=128)
                pool.wait_ge(mixers_done.sem, mixers_done.at(l, 1))
                pool.sem_inc(pool_passed, 1)
                pool.dma_start(wsm[:, :, 0:RANK], wv[:, :, OFF_LR:OFF_LR + RANK]).then_inc(wsm_in.sem, 16)
                pool.dma_start(wsm[:, :, 32:56], wv[:, :, OFF_G:OFF_G + 24]).then_inc(wsm_in.sem, 16)
                for k, name in ((V_L1G, "ln1_g"), (V_L1B, "ln1_b"), (V_L2G, "ln2_g"), (V_L2B, "ln2_b")):
                    pool.dma_start(vecr[k:k + 8, :], row(name, "a (c p) -> (a c) p", p=128)).then_inc(vec_in.sem, 16)
                pool.dma_start(vecr[V_GN:V_GN + 1, :], row("gla_norm_g", "a p -> a p")).then_inc(vec_in.sem, 16)
                pool.dma_start(vecr[V_PEK:V_PEK + 16, :], row("cmp_k_pe", "a (i b) d -> (a i) (b d)", b=2)).then_inc(vec_in.sem, 16)
                pool.dma_start(vecr[V_PEV:V_PEV + 16, :], row("cmp_v_pe", "a (i b) d -> (a i) (b d)", b=2)).then_inc(vec_in.sem, 16)
                pool.dma_start(wa2[0:RANK, :], row("gla_w_a2", "a r n -> (a r) n")).then_inc(par_in.sem, 16)
                pool.dma_start(wa2[RANK:RANK + 1, :], row("gla_b_a", "a n -> a n")).then_inc(par_in.sem, 16)
                pool.dma_start(w2[:, 0, :], row("cmp_k_w2", "a h n -> (a h) n")).then_inc(par_in.sem, 16)
                pool.dma_start(w2[:, 1, :], row("cmp_v_w2", "a h n -> (a h) n")).then_inc(par_in.sem, 16)
                for h2 in range(2):
                    for hp in range(2):
                        if h2 == 0 and hp == 0:
                            pool.wait_ge(stored, l * (16 * STORES) + 16)
                            pool.sem_inc(pool_passed, 1)
                        ins = pool.dma_start(Sst[64 * h2:64 * h2 + 64, :, hp, :],
                                             A["state_gla"][:, bass.ds(l, 1), 2 * hp + h2].rearrange("s a k v -> k (s a) v"))
                        ins.then_inc(state_in.sem, 16)
                pool.wait_ge(tb.done, tb.emptied(l, "kvt5"))
                pool.sem_inc(pool_passed, 1)
                for g in range(2):
                    pool.dma_start(O["nsa_kv_prompt"][0, bass.ds(l, 1), 128 * g:128 * g + 128].rearrange("a t j g d -> (a t) (j g d)"),
                                   kvtok[:, g, 0:512]).then_inc(stored, 16)
                    pool.dma_start(O["win_kv_prompt"][0, bass.ds(l, 1), 128 * g:128 * g + 128].rearrange("a t j g d -> (a t) (j g d)"),
                                   kvtok[:, g, 512:768]).then_inc(stored, 16)
                pool.dma_start(O["nsa_kv_sample"][:, bass.ds(l, 1), 0].rearrange("s a j g d -> (s a) (j g d)"),
                               kvtok[0:NS, 2, 0:512]).then_inc(stored, 16)
                pool.dma_start(O["win_kv_sample"][:, bass.ds(l, 1), PAST - 1].rearrange("s a j g d -> (s a) (j g d)"),
                               kvtok[0:NS, 2, 512:768]).then_inc(stored, 16)
                pool.dma_start(O["win_kv_sample"][1:NS, bass.ds(l, 1)].rearrange("s l t j g d -> s (l t j g d)")[:, 0:(PAST - 1) * 256],
                               A["cache_win_kv"][1:NS, bass.ds(l, 1)].rearrange("s l t j g d -> s (l t j g d)")[:, 256:PAST * 256]).then_inc(stored, 16)
                pool.wait_ge(gate_sig.sem, gate_sig.at(l, 1))
                pool.sem_inc(pool_passed, 1)
                for g in range(2):
                    pool.dma_start(gate64[32 * g:32 * g + 32, :],
                                   gates[0:NS, 2, 12 * g:12 * g + 12].rearrange("s (c b) -> s c b", c=4)).then_inc(gate_in.sem, 16)
                pool.wait_ge(g_state.sem, g_state.at(l, 4))
                pool.sem_inc(pool_passed, 1)
                for h2 in range(2):
                    pool.dma_start(O["gla_state_prompt"][0, bass.ds(l, 1), h2::2].rearrange("a h k v -> k (a h) v"),
                                   Sp[64 * h2:64 * h2 + 64, 1, :, :]).then_inc(stored, 16)
                pool.wait_ge(s_state.sem, s_state.at(l, 8))
                pool.sem_inc(pool_passed, 1)
                for h2 in range(2):
                    for hp in range(2):
                        pool.dma_start(O["gla_state_sample"][:, bass.ds(l, 1), 2 * hp + h2].rearrange("s a k v -> k (s a) v"),
                                       Sst[64 * h2:64 * h2 + 64, :, hp, :]).then_inc(stored, 16)
                def chunk_sums(i, res):
                    for c in range(1, KD):
                        for n, (dst, src, sem_, v) in enumerate(((sumx, hT, res.sem, res.at(l, c + 1)), (sumq, sq, ln_sq.sem, ln_sq.at(l, 8 * i + c + 1)))):
                            pool.wait_ge(sem_, v)
                            pool.sem_inc(pool_passed, 1)
                            if c > 1:
                                pool.wait_ge(ln_sum.sem, ln_sum.at(l, 14 * i + 2 * c - 3 + n))
                                pool.sem_inc(pool_passed, 1)
                            nc.gpsimd.tensor_tensor(dst, src[:, 0, :] if c == 1 else dst, src[:, c, :], ALU.add).then_inc(ln_sum.sem, 1)

                chunk_sums(0, res1)
                chunk_sums(1, res2)
            pool.wait_ge(ini["trc"], 13)
            pool.dma_start(O["y_prompt"][0].rearrange("(g p) f -> p g f", p=128), xin[:, 0:2, :]).then_inc(stored, 16)
            pool.dma_start(O["y_sample"].rearrange("s t f -> (s t) f"), xin[0:NS, 2, :]).then_inc(stored, 16)
            pool.wait_ge(stored, 16 * (STORES * LAYERS + 3))

        @block.tensor
        def _(pe):
            mm = nc.tensor.matmul
            pe.wait_ge(const_in, 16)
            pe.wait_ge(x_in, 64)

            def tr(out, in_, p0, np_):
                return nc.tensor.transpose(out, in_, cst[p0:p0 + np_, C_ID + p0:C_ID + p0 + np_])

            for n in range(6):
                g, half = n // 2, n % 2
                if n >= 2:
                    pe.wait_ge(ini["trc"], n - 1)
                m = TG[g][1]
                for c in range(4):
                    ins = tr(tb.banks[n % 2][:, 128 * c:128 * c + m], xin[0:m, g, (4 * half + c) * 128:(4 * half + c) * 128 + 128], 0, m)
                ins.then_inc(ini["tr"], 1)
            pe.wait_ge(ini["trc"], 5)
            pe.wait_ge(lnv_in, 32)
            tr(tb.banks[0][:, 0:V_N], vecr[:, :], 0, V_N).then_inc(ini["tr"], 1)
            pe.wait_ge(ini["trc"], 7)
            pe.wait_ge(ini["add"], 3)
            mm(sc.banks[0][:, 0:NT], ones, sq[:, 0, :], start=True, stop=True).then_inc(ini["sum"], 1)
            pe.wait_ge(ini["add"], 6)
            mm(sc.banks[1][:, 0:NT], ones, sq[:, 0, :], start=True, stop=True).then_inc(ini["var"], 1)
            pe.wait_ge(tables_in, 16)

            with pe.Fori(0, LAYERS) as l:
                def wait(sem_, value):
                    pe.wait_ge(sem_, value)
                    pe.sem_inc(pe_passed, 1)

                def take(bk, name):
                    wait(bk.done, bk.free(l, name))
                    return bk.bank(name)

                def chunk(name, w, n, mv, kn=KD, m=128):
                    bank = acc.bank(name)
                    pe.wait_ge(acc.done, acc.free(l, name))
                    for k in range(kn):
                        ins = mm(bank[0:m, 0:NT], w(k, n), mv(k), start=(k == 0), stop=(k == kn - 1))
                    ins.then_inc(acc.ready, 1)

                def tile_in(t):
                    s, per, v = landed(t)
                    pe.wait_ge(s, l * per + v)
                    r = wt[t % RING][:, :].rearrange("p (k n) -> p k n", k=KD)
                    return lambda k, n: r[:, k, n * 128:n * 128 + 128]

                hk = lambda k: hT[:, k, :]
                w = tile_in(T_Q)
                for k in range(KD):
                    pe.wait_ge(h_ready.sem, h_ready.at(l, k + 1))
                    for n in range(2):
                        if k == 0:
                            pe.wait_ge(acc.done, acc.free(l, f"q{n}"))
                        ins = mm(acc.bank(f"q{n}")[:, 0:NT], w(k, n), hk(k), start=(k == 0), stop=(k == KD - 1))
                        if k == KD - 1:
                            ins.then_inc(acc.ready, 1)

                def split_in(t):
                    wait(w_lo.sem, w_lo.at(l, 2 * split_no(t) + 2))
                    hi = whi[split_no(t) % 2]
                    lo = wlo[t % RING]
                    return (lambda k, n: hi[:, k, n * 128:n * 128 + 128]), (lambda k, n: lo[:, k, n * 128:n * 128 + 128])

                def split_chunk(name, w, n, hi, lo, k0=0, kn=KD, first=True, last=True):
                    bank = acc.bank(name)
                    if first:
                        wait(acc.done, acc.free(l, name))
                    for k in range(kn):
                        mm(bank[:, 0:NT], w[0](k0 + k, n), hi(k0 + k), start=(first and k == 0), stop=False)
                        mm(bank[:, 0:NT], w[0](k0 + k, n), lo(k0 + k), start=False, stop=False)
                        ins = mm(bank[:, 0:NT], w[1](k0 + k, n), hi(k0 + k), start=False, stop=(last and k == kn - 1))
                    if last:
                        ins.then_inc(acc.ready, 1)
                    return ins

                def split_pair(names, w, hi, lo, wait_k):
                    banks = [take(acc, name) for name in names]
                    for k in range(KD):
                        wait_k(k)
                        for n in range(2):
                            o = banks[n][:, 0:NT]
                            mm(o, w[0](k, n), hi(k), start=(k == 0), stop=False)
                            mm(o, w[0](k, n), lo(k), start=False, stop=False)
                            ins = mm(o, w[1](k, n), hi(k), start=False, stop=(k == KD - 1))
                            if k == KD - 1:
                                ins.then_inc(acc.ready, 1)

                wait(x_lo_d.sem, x_lo_d.at(l, 2))
                split_tiles = ([(T_Q + 1, ["q2", "q3"])] + [(T_KV + i, [f"kv{2 * i}", f"kv{2 * i + 1}"]) for i in range(3)]
                               + [(T_GLA + i, [f"gla{2 * i}", f"gla{2 * i + 1}"]) for i in range(2)])
                for t, names in split_tiles:
                    w = split_in(t)
                    for n in range(2):
                        split_chunk(names[n], w, n, lambda k: x_hi[:, k, :], lambda k: x_lo[:, k, :])
                wait(wsm_in.sem, wsm_in.at(l, 32))
                chunk("small", lambda k, n: wsm[:, k, :], 0, hk, m=56)

                wait(vec_in.sem, vec_in.at(l, 112))
                b = take(tb, "vec")
                tr(b[:, 0:V_N], vecr[:, :], 0, V_N).then_inc(tb.ready, 1)
                for i in range(6):
                    src, name = (qT[:, i, :], f"q{i}") if i < 4 else (kvT[:, 2 * (i - 3), :], f"kv{2 * (i - 3)}")
                    wait(acc.done, acc.emptied(l, name))
                    b = take(tb, f"rope{i}")
                    mm(b[:, 0:NT], cst[:, C_ROT:C_ROT + 128], src, start=True, stop=True).then_inc(tb.ready, 1)

                wait(q_rot.sem, q_rot.at(l, 6))
                wait(acc.done, acc.emptied(l, "kv5"))
                for i in range(6):
                    c0, n = TG[i // 2]
                    b = take(tb, f"kvt{i}")
                    for j in range(4 if i % 2 == 0 else 2):
                        ins = tr(b[0:n, 128 * j:128 * j + 128], kvT[:, 4 * (i % 2) + j, c0:c0 + n], 0, 128)
                    ins.then_inc(tb.ready, 1)
                wait(s_qz.sem, s_qz.at(l, 1))
                for s in range(NS):
                    wait(cache_in[s % 2].sem, cache_in[s % 2].at(l, 48 * (s // 2 + 1)))
                    b = take(tb, f"pairs{s}")
                    for n in range(4):
                        ins = tr(b[:, 128 * n:128 * n + 128], stg[:, s % 2, n % 2, 128 * (n // 2):128 * (n // 2) + 128], 0, 128)
                    ins.then_inc(tb.ready, 1)
                    b = take(tb, f"keys{s}")
                    for n in range(4):
                        src = stg[:, s % 2, n, 256:384] if n < 2 else stw[:, s % 2, n - 2, :]
                        ins = tr(b[:, 128 * n:128 * n + 128], src, 0, 128)
                    ins.then_inc(tb.ready, 1)
                    if s % 2 == 0:
                        w = tile_in((T_GLA + 2, T_GLA + 3, T_GR, T_GR + 1)[s // 2])
                    chunk(f"gla{4 + s}" if s < 4 else f"gr{s - 4}", w, s % 2, hk)
                    if s == 0:
                        take(sc, "ssc0")
                        take(sc, "ssc1")
                    wait(tb.done, tb.emptied(l, f"keys{s}"))
                    for br in range(2):
                        ins = mm(sc.bank(f"ssc{br}")[0:64, 0:NKEY], Qz[:, 1, s, :], kTs[:, s % 2, br, :], start=(s == 0), stop=(s == NS - 1))
                        if s == NS - 1:
                            ins.then_inc(sc.ready, 1)
                        elif br == 1:
                            ins.then_inc(s_keys.sem, 1)
                wait(acc.done, acc.emptied(l, "gla7"))
                for i in range(6):
                    c0, n = TG[i // 2]
                    b = take(tb, f"glt{i}")
                    for j in range(4 if i % 2 == 0 else 2):
                        ins = tr(b[0:n, 128 * j:128 * j + 128], glT[:, 2 + 4 * (i % 2) + j, c0:c0 + n], 0, 128)
                    ins.then_inc(tb.ready, 1)
                b = take(tb, "gate")
                for g, (c0, n) in enumerate(TG):
                    ins = tr(b[0:n, 24 * g:24 * g + 24], gateT[:, c0:c0 + n], 0, 24)
                ins.then_inc(tb.ready, 1)
                wait(pairs.sem, pairs.at(l, 1))
                for j, name in enumerate(("hidk", "hidv")):
                    s, per, v = landed(T_CMP + j)
                    wait(s, l * per + v)
                    b = take(sc, name)
                    w = wt[(T_CMP + j) % RING]
                    for lp in range(16):
                        wk = w[:, 128 * lp:128 * lp + 128]
                        rows = cmpT[:, j].rearrange("p g s i -> p (g s) i")[:, :, lp:lp + 8 * 14 + 1:8]
                        mm(b[:, 0:270], wk, rows, start=(lp == 0), stop=(lp == 15))
                    wait(pe_sum.sem, pe_sum.at(l, j + 1))
                    mm(b[:, 272:273], pacc[:, j, :], ones[:, 0:1], start=True, stop=True).then_inc(sc.ready, 1)

                def gate_chunk(i):
                    chunk(f"mg{i}", tile_in(T_MG + i // 2), i % 2, hk)

                gate_chunk(0)
                gate_chunk(1)
                wait(par_in.sem, par_in.at(l, 64))
                wait(hid_g.sem, hid_g.at(l, 1))
                b = take(tb, "kcmp")
                for g in range(2):
                    ins = mm(b[64 * g:64 * g + 64, 0:135], w2[:, 0, :], hx[:, 0, 135 * g:135 * g + 135], start=True, stop=True)
                ins.then_inc(tb.ready, 1)
                wait(hid_g.sem, hid_g.at(l, 2))
                for i in range(3):
                    b = take(tb, f"vcmp{i}")
                    for s in range(4 * i, min(4 * i + 4, 9)):
                        for g in range(2):
                            o0 = (s - 4 * i) * 128 + 64 * g
                            ins = mm(b[0:NWIN, o0:o0 + 64], hx[:, 1, 135 * g + 15 * s:135 * g + 15 * s + 15], w2[:, 1, :],
                                     start=True, stop=True)
                    ins.then_inc(tb.ready, 1)

                for t in range(2):
                    wait(tb.done, tb.emptied(l, "kcmp"))
                    for g in range(GROUPS):
                        b = take(sc, f"csc{t}{g}")
                        for c in range(4):
                            ins = mm(b[:, 15 * c:15 * c + 15], qT[64 * g:64 * g + 64, c, 128 * t:128 * t + 128],
                                     kc[64 * g:64 * g + 64, 120:135], start=True, stop=True)
                        ins.then_inc(sc.ready, 1)
                b = take(sc, "ssc2")
                for s in range(NS):
                    ins = mm(b[0:64, 0:NWIN], Qz[:, 0, s, :], kc[:, 15 * s:15 * s + 15], start=(s == 0), stop=(s == NS - 1))
                ins.then_inc(sc.ready, 1)

                def scores(u):
                    t, c, g = u // 8, (u % 8) // 2, u % 2
                    b = take(sc, f"sc{u}")
                    for br in range(2):
                        ins = mm(b[:, 256 * br:256 * br + 128 * (t + 1)], qR[64 * g:64 * g + 64, c, 128 * t:128 * t + 128],
                                 kvT[64 * g:64 * g + 64, 2 + 2 * br, 0:128 * (t + 1)], start=True, stop=True)
                    ins.then_inc(sc.ready, 1)

                def prob_tr(u):
                    t = u // 8
                    wait(u_prob.sem, u_prob.at(l, u + 1))
                    b = take(tb, f"pt{u}")
                    for br in range(2):
                        for kb in range(t + 1):
                            n = br * (t + 1) + kb
                            ins = tr(b[:, 128 * n:128 * n + 128], PS[:, u % 2, br, 128 * kb:128 * kb + 128], 0, 128)
                    ins.then_inc(tb.ready, 1)

                def values(u):
                    t, c, g = u // 8, (u % 8) // 2, u % 2
                    name = f"o{u // 2}"
                    b = take(ob, name) if g == 0 else ob.bank(name)
                    wait(tb.done, tb.emptied(l, f"pt{u}"))
                    o = b[64 * g:64 * g + 64, 0:128]
                    mm(o, vc[:, 8, 64 * g:64 * g + 64], PTc[:, 4 * g + c, :], start=True, stop=False)
                    for br in range(2):
                        for kb in range(t + 1):
                            c0 = (3 + 2 * br) * 128 + 64 * g
                            end = br == 1 and kb == t
                            ins = mm(o, kvtok[:, kb, c0:c0 + 64], PT[:, u % 2, br * (t + 1) + kb, :], start=False, stop=end)
                    ins.then_inc(ob.ready if g == 1 else pv_done.sem, 1)

                def compressed_tr(t):
                    wait(c_prob.sem, c_prob.at(l, t + 1))
                    for a in range(2):
                        b = take(tb, f"pc{t}{a}")
                        for i in range(4):
                            ins = tr(b[0:NWIN, 128 * i:128 * i + 128], CS[:, t, 4 * a + i, :], 0, 128)
                        ins.then_inc(tb.ready, 1)

                def sample_probs():
                    wait(s_prob.sem, s_prob.at(l, 1))
                    b = take(tb, "spt")
                    for n in range(4):
                        tr(b[:, 64 * n:64 * n + 64], P64[:, n // 2, 128 * (n % 2):128 * (n % 2) + 128], 0, 64)
                    tr(b[0:NWIN, 256:320], C64[:, :], 0, 64).then_inc(tb.ready, 1)
                    b = take(tb, "snew")
                    wait(s_anew.sem, s_anew.at(l, 1))
                    for br in range(2):
                        ins = mm(b[0:8, 64 * br:64 * br + 64], An[:, br, :], cst[0:64, C_ID:C_ID + 64], start=True, stop=True)
                    ins.then_inc(tb.ready, 1)

                def sample_values():
                    wait(val_in.sem, val_in.at(l, 16 * NS))
                    wait(val_copied.sem, val_copied.at(l, NS))
                    wait(tb.done, tb.emptied(l, "snew"))
                    b = take(ob, "so")
                    for br in range(2):
                        c0 = (3 + 2 * br) * 128
                        mm(b[:, 0:64], kvtok[0:8, 2, c0:c0 + 128], Pn[:, br, :], start=(br == 0), stop=False, skip_group_check=True)
                    for s in range(NS):
                        o = b[:, 0:64].rearrange("p (g s c) -> p g s c", g=2, s=NS)[:, :, s, :]
                        for n in range(4):
                            mv = PTs[:, n, :].rearrange("p (g s c) -> p g s c", g=2, s=NS)[:, :, s, :]
                            mm(o, Vs[:, n // 2, s, n % 2, :], mv, start=False, stop=False, skip_group_check=True)
                        mv = PTcs[:, :].rearrange("p (g s c) -> p g s c", g=2, s=NS)[:, :, s, :]
                        ins = mm(o, vc[:, s, :], mv, start=False, stop=(s == NS - 1), skip_group_check=True)
                    ins.then_inc(ob.ready, 1)

                def log_decays():
                    b = take(tb, "la01")
                    wait(acc.done, acc.emptied(l, "small"))
                    for g in range(2):
                        ins = mm(b[:, 256 * g:256 * g + 256], small[0:RANK + 1, 128 * g:128 * g + 128], wa2[:, :], start=True, stop=True)
                    ins.then_inc(tb.ready, 1)
                    b = take(tb, "la2")
                    mm(b[0:NS, 0:256], small[0:RANK + 1, SEQ:NT], wa2[:, :], start=True, stop=True).then_inc(tb.ready, 1)

                def sample_decays():
                    wait(la_t.sem, la_t.at(l, 1))
                    b = take(tb, "elas")
                    for hp in range(2):
                        ins = tr(b[:, 8 * hp:8 * hp + 8], xla[0:NS, 2, 128 * hp:128 * hp + 128], 0, NS)
                    ins.then_inc(tb.ready, 1)

                def head_squares(i):
                    wait(r_sq.sem, r_sq.at(l, i + 1))
                    n = 512 if i < 2 else 32
                    b = take(sc, f"rms{i}")
                    mm(b[:, 0:n], ones, osq[:, 0:n], start=True, stop=True).then_inc(sc.ready, 1)

                def decays(t):
                    b = take(sc, f"gB{t}")
                    for hp in range(2):
                        ins = mm(b[:, 256 * hp:256 * hp + 256], xla[:, t, 128 * hp:128 * hp + 128], cst[:, C_TRI:C_TRI + 256], start=True, stop=True)
                    ins.then_inc(sc.ready, 1)
                    b = take(tb, f"aft{t}")
                    mm(b[:, 0:256], cst[:, C_AFT:C_AFT + 128], xla[:, t, :], start=True, stop=True).then_inc(tb.ready, 1)

                def gla_scores(t):
                    wait(g_q.sem, g_q.at(l, t + 1))
                    for h2 in range(2):
                        b = take(tb, f"gA{t}{h2}")
                        for hp in range(2):
                            ins = mm(b[:, 128 * hp:128 * hp + 128], km[64 * h2:64 * h2 + 64, hp, :], qm[64 * h2:64 * h2 + 64, hp, :], start=True, stop=True)
                        ins.then_inc(tb.ready, 1)

                def gla_update(t, ch):
                    b = take(tb, f"U{t}{ch}")
                    for hp in range(2):
                        ins = mm(b[:, 256 * hp:256 * hp + 256], kd[64 * ch:64 * ch + 64, 128 * hp:128 * hp + 128],
                                 gltok[64 * ch:64 * ch + 64, t, 256 + 256 * hp:512 + 256 * hp], start=True, stop=True)
                    ins.then_inc(tb.ready, 1)

                def gla_values(t):
                    bs = [take(ob, f"go{t}{h2}") for h2 in range(2)]
                    wait(tb.done, tb.emptied(l, f"gA{t}1"))
                    for h2 in range(2):
                        for hp in range(2):
                            h = 2 * hp + h2
                            mm(bs[h2][:, 128 * hp:128 * hp + 128], gltok[:, t, 256 + 128 * h:384 + 128 * h], gAs[:, h, :],
                               start=(hp == 0), stop=False, skip_group_check=True)
                    for ch in range(2):
                        k = 2 * t + ch
                        if k == 0:
                            continue
                        wait(g_state.sem, g_state.at(l, k))
                        for h2 in range(2):
                            for hp in range(2):
                                c0 = 128 * hp + 64 * ch
                                ins = mm(bs[h2][:, c0:c0 + 64], Sp[64 * h2:64 * h2 + 64, (k - 1) % 2, hp, :],
                                         qe[64 * h2:64 * h2 + 64, hp, 64 * ch:64 * ch + 64],
                                         start=False, stop=(ch == 1 and hp == 1), skip_group_check=True)
                            if ch == 1:
                                ins.then_inc(ob.ready, 1)

                def sample_update(s):
                    wait(kz_d.sem, kz_d.at(l, s + 1))
                    b = take(tb, f"SU{s}")
                    for hp in range(2):
                        ins = mm(b[:, 256 * hp:256 * hp + 256], kz[:, s % 2, 128 * hp:128 * hp + 128], gltok[0:NS, 2, 256 + 256 * hp:512 + 256 * hp], start=True, stop=True)
                    ins.then_inc(tb.ready, 1)

                def sample_output(s):
                    if s == 0:
                        wait(qs_d.sem, qs_d.at(l, 1))
                        take(ob, "gos")
                        wait(s_state.sem, s_state.at(l, NS))
                    for hp in range(2):
                        c0 = 2 * (NS * hp + s)
                        ins = mm(ob.bank("gos")[:, c0:c0 + 2], Sst[:, s, hp, :], qsz[:, hp, s, :], start=True, stop=True)
                    if s == NS - 1:
                        ins.then_inc(ob.ready, 1)

                for k in range(18):
                    if k < 16:
                        scores(k)
                    if k < 14:
                        gate_chunk(k + 2)
                    if k == 1:
                        compressed_tr(0)
                    if 1 <= k <= 16:
                        prob_tr(k - 1)
                    if k >= 2:
                        values(k - 2)
                    if k == 9:
                        compressed_tr(1)
                    if k == 0:
                        log_decays()
                    elif k == 1:
                        sample_probs()
                    elif k == 2:
                        sample_decays()
                        decays(0)
                    elif k == 4:
                        gla_scores(0)
                    elif k == 5:
                        sample_values()
                        gla_update(0, 0)
                        gla_update(0, 1)
                    elif k == 7:
                        gla_values(0)
                    elif k == 8:
                        decays(1)
                    elif k == 9:
                        head_squares(0)
                    elif k == 10:
                        gla_scores(1)
                    elif k == 11:
                        gla_update(1, 0)
                    elif k == 13:
                        gla_values(1)
                        gla_update(1, 1)
                    elif k == 15:
                        head_squares(1)
                    if k in updates_at:
                        for s in updates_at[k]:
                            sample_update(s)
                    if k >= 16:
                        for s in range(4 * (k - 16), 4 * (k - 16) + 4):
                            sample_output(s)
                head_squares(2)

                wait(ob.done, ob.emptied(l, "so"))
                wait(og_d.sem, og_d.at(l, 3))
                w = tile_in(T_UP)
                for n in range(2):
                    chunk(f"up{2 * n}", w, n, lambda k: onT[:, k, :], kn=4)
                    chunk(f"up{2 * n + 1}", lambda k, n: w(4 + k, n), n, lambda k: ogT[:, k, :], kn=4)
                wait(u_lo_d.sem, u_lo_d.at(l, 2))
                for i in range(1, 4):
                    w = split_in(T_UP + i)
                    for n in range(2):
                        for a in range(2):
                            split_chunk(f"up{4 * i + 2 * n + a}", w, n, lambda k: u_hi[:, k, :], lambda k: u_lo[:, k, :], k0=4 * a, kn=4)

                def norm_sums(i):
                    for n, (name, src) in enumerate((("m", sumx), ("v", sumq))):
                        b = take(sc, f"ln{i + 1}{name}")
                        wait(ln_sum.sem, ln_sum.at(l, 14 * i + 13 + n))
                        mm(b[:, 0:NT], ones, src, start=True, stop=True).then_inc(sc.ready, 1)

                for i in range(4):
                    w = split_in(T_OUT + i)
                    hi, lo = (lambda k: m_hi[:, k, :]), (lambda k: m_lo[:, k, :])
                    if i == 0:
                        split_pair(["out0", "out1"], w, hi, lo, lambda k: wait(m_lo_d.sem, m_lo_d.at(l, k + 1)))
                        continue
                    for n in range(2):
                        split_chunk(f"out{2 * i + n}", w, n, hi, lo)
                norm_sums(0)

                for i in range(16):
                    w = split_in(T_M1 + i)
                    hi, lo = (lambda k: h_hi[:, k, :]), (lambda k: h_lo[:, k, :])
                    if i == 0:
                        split_pair(["m1_0", "m1_1"], w, hi, lo, lambda k: wait(h_lo_d.sem, h_lo_d.at(l, k + 1)))
                        continue
                    for n in range(2):
                        split_chunk(f"m1_{2 * i + n}", w, n, hi, lo)
                for cg in range(4):
                    for kg in range(4):
                        w = split_in(T_M2 + 4 * cg + kg)
                        if cg == 0:
                            wait(hid_lo_d.sem, hid_lo_d.at(l, 8 * kg + 8))
                        for n in range(2):
                            ins = split_chunk(f"m2_{2 * cg + n}", w, n, lambda k: hid_hi[:, 8 * kg + k, :], lambda k: hid_lo[:, 8 * kg + k, :],
                                              first=(kg == 0), last=(kg == 3))
                        if kg < 3:
                            ins.then_inc(m2_part.sem, 1)
                norm_sums(1)

            pe.wait_ge(h_ready.sem, LAYERS * 16 + 8)
            for n in range(6):
                g, half = n // 2, n % 2
                c0, m = TG[g]
                if n >= 2:
                    pe.wait_ge(ini["trc"], 6 + n)
                for c in range(4):
                    ins = tr(tb.banks[n % 2][0:m, 128 * c:128 * c + 128], hT[:, 4 * half + c, c0:c0 + m], 0, 128)
                ins.then_inc(ini["tr"], 1)

        @block.scalar
        def _(act):
            A_ = nc.scalar.activation
            act.preload_act_table_set("natural_log_exp_and_others")
            act.sem_inc(acc.done, 2)
            act.sem_inc(sc.done, 2)
            act.sem_inc(ob.done, 2)
            act.wait_ge(ini["sum"], 1)
            A_(mu, sc.banks[0][:, 0:NT], ACT.Copy, scale=1.0 / D).then_inc(ini["mu"], 1)
            act.wait_ge(ini["cen"], 1)
            A_(sq[:, 0:4, :], hT[:, 0:4, :], ACT.Square).then_inc(ini["sq"], 1)
            act.wait_ge(ini["cen"], 2)
            A_(sq[:, 4:8, :], hT[:, 4:8, :], ACT.Square).then_inc(ini["sq"], 1)
            act.wait_ge(tables_in, 16)
            act.wait_ge(ini["var"], 1)
            A_(rs, sc.banks[1][:, 0:NT], ACT.Ln, scale=1.0 / D, bias=epsc).then_inc(ini["rs"], 1)
            act.wait_ge(ini["rs"], 1)
            A_(rs, rs, ACT.Exp, scale=-0.5).then_inc(ini["rs"], 1)
            for c in range(KD):
                act.wait_ge(ini["cen"], c + 3)
                A_(hT[:, c, :], hT[:, c, :], ACT.Identity, bias=lv[:, 8 + c:9 + c]).then_inc(h_ready.sem, 1)

            with act.Fori(0, LAYERS) as l:
                links = [0]

                def link(ins):
                    links[0] += 1
                    ins.then_inc(act_link.sem, 1)
                    act.wait_ge(act_link.sem, act_link.at(l, links[0]))

                def evac(name, dst, func=ACT.Copy, m=128, **kw):
                    act.wait_ge(acc.ready, acc.filled(l, name))
                    A_(dst, acc.bank(name)[0:m, 0:NT], func, **kw).then_inc(acc.done, 1)

                def split_hi(t, halves=(0, 1)):
                    if 0 in halves:
                        s, per, v = landed(t)
                        if split_no(t) >= 2 and t not in (SPLIT_B, SPLIT_B + 1):
                            act.wait_ge(*tile_used(l, t - 2))
                        act.wait_ge(s, l * per + v)
                    for a in halves:
                        A_(whi[split_no(t) % 2][:, 4 * a:4 * a + 4, :],
                           wt[t % RING][:, 1024 * a:1024 * a + 1024].rearrange("p (k n) -> p k n", k=4), ACT.Copy).then_inc(w_hi.sem, 1)

                act.wait_ge(h_ready.sem, h_ready.at(l, 8))
                for a in range(2):
                    A_(x_hi[:, 4 * a:4 * a + 4, :], hT[:, 4 * a:4 * a + 4, :], ACT.Copy).then_inc(x_hi_d.sem, 1)
                split_hi(1)
                split_hi(2)
                chunks = ([(f"q{i}", qT[:, i, :]) for i in range(4)] + [(f"kv{i}", kvT[:, i, :]) for i in range(6)]
                          + [(f"gla{i}", glT[:, i, :]) for i in range(4)])
                for i, (name, dst) in enumerate(chunks):
                    evac(name, dst)
                    if i % 2 == 1 and 3 <= i // 2 + 2 < SPLIT_A:
                        split_hi(i // 2 + 2)
                act.wait_ge(ini["zero"], 7)
                act.wait_ge(acc.ready, acc.filled(l, "small"))
                link(A_(small[0:RANK, :], acc.bank("small")[0:RANK, 0:NT], ACT.Copy))
                A_(gateT[:, :], acc.bank("small")[32:56, 0:NT], ACT.Copy).then_inc(acc.done, 1)
                for s in range(NS):
                    act.wait_ge(cache_in[s % 2].sem, cache_in[s % 2].at(l, 48 * (s // 2 + 1)))
                    A_(Vs[:, 0, s, :, :], stg[:, s % 2, :, 384:512], ACT.Copy).then_inc(val_copied.sem, 1)
                    if s < 4:
                        evac(f"gla{4 + s}", glT[:, 4 + s, :])
                    else:
                        i = s - 4
                        act.wait_ge(acc.ready, acc.filled(l, f"gr{i}"))
                        link(A_(gre[:, i, :], acc.bank(f"gr{i}")[:, 0:NT], ACT.Exp, scale=-1.0))
                        A_(grT[:, i, :], acc.bank(f"gr{i}")[:, 0:NT], ACT.Copy).then_inc(acc.done, 1)
                act.wait_ge(s_max.sem, s_max.at(l, 1))
                for br in range(2):
                    A_(P64[:, br, :], sc.bank(f"ssc{br}")[0:64, 0:NKEY], ACT.Exp, scale=SCALE, bias=s64[:, 3 + br:4 + br],
                       accum_out=s64[:, 6 + br:7 + br]).then_inc(sc.done, 1)
                act.wait_ge(acc.done, acc.emptied(l, "gr3"))
                link(A_(gre, gre, ACT.Ln, bias=1.0))
                A_(gre, gre, ACT.Exp, scale=-1.0).then_inc(gre_sig.sem, 1)
                act.wait_ge(tb.done, tb.emptied(l, "gate"))
                A_(gates[:, :, :], gates[:, :, :], ACT.Exp, scale=-1.0).then_inc(gate_exp.sem, 1)
                for j, name in enumerate(("hidk", "hidv")):
                    act.wait_ge(sc.ready, sc.filled(l, name))
                    b = sc.bank(name)
                    link(A_(hb[:, j:j + 1], b[:, 272:273], ACT.Copy))
                    A_(hx[:, j, :], b[:, 0:270], ACT.Identity, bias=hb[:, j:j + 1]).then_inc(sc.done, 1)
                    act.wait_ge(hid_u.sem, hid_u.at(l, j + 1))
                    A_(hy, hy, ACT.Exp, scale=-2.0 * GELU_C).then_inc(hid_e.sem, 1)

                def gate_sigmoid(i):
                    m = mgT[:, i, :]
                    evac(f"mg{i}", m, ACT.Exp, scale=-1.0)
                    act.wait_ge(acc.done, acc.emptied(l, f"mg{i}"))
                    link(A_(m, m, ACT.Ln, bias=1.0))
                    A_(m, m, ACT.Exp, scale=-1.0).then_inc(mg_sig.sem, 1)

                gate_sigmoid(0)
                gate_sigmoid(1)
                for t in range(2):
                    for g in range(GROUPS):
                        act.wait_ge(sc.ready, sc.filled(l, f"csc{t}{g}"))
                        A_(CS[:, t, 4 * g:4 * g + 4, :], sc.bank(f"csc{t}{g}")[:, 0:60].rearrange("p (h k) -> p h k", h=4), ACT.Copy).then_inc(sc.done, 1)
                for t in range(2):
                    act.wait_ge(c_shift.sem, c_shift.at(l, t + 1))
                    A_(CS[:, t, :, :], CS[:, t, :, :], ACT.Exp, scale=SCALE).then_inc(c_exp.sem, 1)
                act.wait_ge(s_cmax.sem, s_cmax.at(l, 1))
                A_(C64[:, :], sc.bank("ssc2")[0:64, 0:NWIN], ACT.Exp, scale=SCALE, bias=s64[:, 5:6],
                   accum_out=s64[:, 8:9]).then_inc(sc.done, 1)
                def unit_exp(u):
                    n = 128 * (u // 8 + 1)
                    act.wait_ge(u_max.sem, u_max.at(l, u + 1))
                    if u >= 2:
                        act.wait_ge(tb.ready, tb.filled(l, f"pt{u - 2}"))
                    b = sc.bank(f"sc{u}")
                    A_(PS[:, u % 2, 0, 0:n], b[:, 0:n], ACT.Exp, scale=SCALE, bias=st[:, u % 2, 2:3],
                       accum_out=st[:, u % 2, 4:5]).then_inc(u_half.sem, 1)
                    A_(PS[:, u % 2, 1, 0:n], b[:, 256:256 + n], ACT.Exp, scale=SCALE, bias=st[:, u % 2, 3:4],
                       accum_out=st[:, u % 2, 5:6]).then_inc(sc.done, 1)

                def sample_values():
                    act.wait_ge(ob.ready, ob.filled(l, "so"))
                    for g in range(2):
                        ins = A_(onT[64 * g:64 * g + 64, :, SEQ:NT].rearrange("p c s -> p s c"),
                                 ob.bank("so")[64 * g:64 * g + 64, 32 * g:32 * g + 32].rearrange("p (s c) -> p s c", s=NS), ACT.Copy)
                        if g == 0:
                            link(ins)
                        else:
                            ins.then_inc(ob.done, 1)

                def log_decays():
                    act.wait_ge(tb.done, tb.emptied(l, "la2"))
                    link(A_(lla[:, :, :], xla[:, :, :], ACT.Abs))
                    link(A_(lla[:, :, :], lla[:, :, :], ACT.Exp, scale=-1.0))
                    A_(lla[:, :, :], lla[:, :, :], ACT.Ln, bias=1.0).then_inc(la_e.sem, 1)

                def decays(t):
                    if t == 1:
                        act.wait_ge(g_q.sem, g_q.at(l, 1))
                        act.wait_ge(g_state.sem, g_state.at(l, 2))
                    act.wait_ge(sc.ready, sc.filled(l, f"gB{t}"))
                    B = sc.bank(f"gB{t}")[:, :].rearrange("p (h m n) -> p h m n", h=2, m=2)
                    link(A_(EB[:, 0, :, :], B[:, :, 0, :], ACT.Exp))
                    link(A_(EB[:, 1, :, :], B[:, :, 1, :], ACT.Exp))
                    A_(EB[:, 2, :, :], B[:, :, 1, :], ACT.Exp, scale=-1.0).then_inc(sc.done, 1)

                def decays_after(t):
                    act.wait_ge(tb.done, tb.emptied(l, f"aft{t}"))
                    A_(kd, kd, ACT.Exp).then_inc(g_ea.sem, 1)

                def rms_squares(i):
                    n = 512 if i < 2 else 32
                    c0, m = TG[i]
                    if i > 0:
                        act.wait_ge(sc.ready, sc.filled(l, f"rms{i - 1}"))
                    if i == 2:
                        act.wait_ge(ob.ready, ob.filled(l, "gos"))
                        o = ob.bank("gos")[:, 0:32].rearrange("p (h s g) -> p h g s", h=2, g=2)
                        A_(osq[:, 0:n].rearrange("p (h g s) -> p h g s", h=2, g=2), o, ACT.Square).then_inc(r_sq.sem, 1)
                        A_(ogT[:, :, c0:c0 + m].rearrange("p (h g) s -> p h g s", h=2), o, ACT.Copy).then_inc(ob.done, 1)
                        return
                    for h2 in range(2):
                        name = f"go{i}{h2}"
                        act.wait_ge(ob.ready, ob.filled(l, name))
                        o = ob.bank(name)[:, 0:n // 2].rearrange("p (h t) -> p h t", h=2)
                        ins = A_(osq[:, 0:n].rearrange("p (h t) -> p h t", h=4)[:, h2:4:2, :], o, ACT.Square)
                        if h2 == 0:
                            link(ins)
                        else:
                            ins.then_inc(r_sq.sem, 1)
                        A_(ogT[:, h2:4:2, c0:c0 + m], o, ACT.Copy).then_inc(ob.done, 1)

                def rms_scale(i):
                    n = 512 if i < 2 else 32
                    act.wait_ge(sc.ready, sc.filled(l, f"rms{i}"))
                    if i > 0:
                        act.wait_ge(og_d.sem, og_d.at(l, i))
                    A_(rr[:, 0:n], sc.bank(f"rms{i}")[:, 0:n], ACT.Ln, scale=1.0 / DV, bias=epsc).then_inc(sc.done, 1)
                    act.wait_ge(sc.done, sc.emptied(l, f"rms{i}"))
                    A_(rr[:, 0:n], rr[:, 0:n], ACT.Exp, scale=-0.5).then_inc(r_rs.sem, 1)

                for k in range(18):
                    if k < 16:
                        unit_exp(k)
                    if k >= 3 and k % 2 == 1:
                        n = (k - 3) // 2
                        act.wait_ge(ob.ready, ob.filled(l, f"o{n}"))
                        A_(onT[:, n % 4, 128 * (n // 4):128 * (n // 4) + 128], ob.bank(f"o{n}")[:, 0:128], ACT.Copy).then_inc(ob.done, 1)
                    if k < 14:
                        if k == 10:
                            act.wait_ge(gla_silu.sem, gla_silu.at(l, 1))
                        gate_sigmoid(k + 2)
                    if k == 1:
                        log_decays()
                    elif k == 2:
                        decays(0)
                    elif k == 3:
                        act.wait_ge(tb.done, tb.emptied(l, "elas"))
                        A_(ela[:, :, :], ela[:, :, :], ACT.Exp, scale=1.0 / TAU).then_inc(ela_d.sem, 1)
                        decays_after(0)
                    elif k == 5:
                        sample_values()
                    elif k == 7:
                        rms_squares(0)
                    elif k == 8:
                        decays(1)
                    elif k == 9:
                        decays_after(1)
                        rms_scale(0)
                    elif k == 13:
                        rms_squares(1)
                    elif k == 15:
                        rms_scale(1)
                    elif k == 17:
                        act.wait_ge(ob.done, ob.emptied(l, "o7"))
                        A_(u_hi[:, 0:4, :], onT[:, :, :], ACT.Copy).then_inc(u_hi_d.sem, 1)
                        split_hi(T_UP + 1)
                        rms_squares(2)
                rms_scale(2)
                act.wait_ge(og_d.sem, og_d.at(l, 3))
                A_(u_hi[:, 4:8, :], ogT, ACT.Copy).then_inc(u_hi_d.sem, 1)
                def merged_hi(i):
                    act.wait_ge(up_m.sem, up_m.at(l, i + 1))
                    A_(m_hi[:, i, :], mgT[:, i, :], ACT.Copy).then_inc(m_hi_d.sem, 1)

                for i in range(16):
                    if i >= 2:
                        act.wait_ge(up_m.sem, up_m.at(l, i // 2))
                    evac(f"up{i}", upb[:, i % 2, :])
                    if i % 2 == 1 and i >= 3:
                        merged_hi(i // 2 - 1)
                    if i >= 3 and i % 2 == 1:
                        split_hi(T_UP + (i - 3) // 4 + 2, ((i - 3) // 2 % 2,))
                merged_hi(7)
                split_hi(T_UP + 5, (1,))
                def square(i, res, c):
                    act.wait_ge(res.sem, res.at(l, c + 1))
                    A_(sq[:, c, :], hT[:, c, :], ACT.Square).then_inc(ln_sq.sem, 1)

                def norm(i, vb):
                    act.wait_ge(sc.ready, sc.filled(l, f"ln{i + 1}m"))
                    A_(mu, sc.bank(f"ln{i + 1}m")[:, 0:NT], ACT.Copy, scale=1.0 / D).then_inc(sc.done, 1)
                    act.wait_ge(sc.ready, sc.filled(l, f"ln{i + 1}v"))
                    A_(rs, sc.bank(f"ln{i + 1}v")[:, 0:NT], ACT.Copy, scale=1.0 / D).then_inc(sc.done, 1)
                    act.wait_ge(ln_var.sem, ln_var.at(l, i + 1))
                    link(A_(rs, rs, ACT.Ln, bias=epsc))
                    A_(rs, rs, ACT.Exp, scale=-0.5).then_inc(ln_rs.sem, 1)
                    for c in range(KD):
                        act.wait_ge(ln_sc.sem, ln_sc.at(l, 8 * i + c + 1))
                        A_(hT[:, c, :], hT[:, c, :], ACT.Identity, bias=lv[:, vb + c:vb + c + 1]).then_inc(h_ready.sem, 1)
                        if i == 0:
                            act.wait_ge(h_ready.sem, h_ready.at(l, 9 + c))
                            A_(h_hi[:, c, :], hT[:, c, :], ACT.Copy).then_inc(h_hi_d.sem, 1)

                for i in range(8):
                    if i >= 2:
                        act.wait_ge(res1.sem, res1.at(l, i - 1))
                    evac(f"out{i}", yb[:, i % 2, :])
                    if i >= 1:
                        square(0, res1, i - 1)
                    if i % 2 == 1 and i < 7:
                        split_hi(T_OUT + i // 2 + 2)
                square(0, res1, 7)
                split_hi(T_M1 + 1)
                norm(0, V_L1B)
                for i in range(32):
                    if i >= 2:
                        act.wait_ge(hid_lo_d.sem, hid_lo_d.at(l, i - 1))
                    evac(f"m1_{i}", yb[:, i % 2, :], ACT.Relu)
                    act.wait_ge(acc.done, acc.emptied(l, f"m1_{i}"))
                    A_(hid_hi[:, i, :], yb[:, i % 2, :], ACT.Square).then_inc(hid_hi_d.sem, 1)
                    if i % 2 == 1:
                        split_hi(T_M1 + i // 2 + 2)
                act.wait_ge(hid_lo_d.sem, hid_lo_d.at(l, 32))
                for t in range(16):
                    if t % 4 == 3:
                        for i in range(t // 2 - 1, t // 2 + 1):
                            if i >= 2:
                                act.wait_ge(res2.sem, res2.at(l, i - 1))
                            evac(f"m2_{i}", yb[:, i % 2, :])
                        square(1, res2, t // 2 - 1)
                        square(1, res2, t // 2)
                    if t < 14:
                        split_hi(T_M2 + t + 2)
                norm(1, V_L2B)
                assert links[0] == act_link.per, links[0]

        @block.vector
        def _(dve):
            V = nc.vector
            dve.sem_inc(tb.done, 2)
            dve.sem_inc(mixers_done.sem, 1)
            for n in range(6):
                g, half = n // 2, n % 2
                c0, m = TG[g]
                dve.wait_ge(ini["tr"], n + 1)
                V.tensor_copy(hT[:, 4 * half:4 * half + 4, c0:c0 + m],
                              tb.banks[n % 2][:, :].rearrange("p (c t) -> p c t", c=4)[:, :, 0:m]).then_inc(ini["trc"], 1)
            dve.wait_ge(ini["tr"], 7)
            V.tensor_copy(lv[:, :], tb.banks[0][:, 0:V_N]).then_inc(ini["trc"], 1)

            def bc(a, n):
                return a[:, None, :].to_broadcast([128, n, NT])

            def add_chunks(a, n0):
                for n, half in enumerate((4, 2, 1)):
                    src = a if n == 0 else sq
                    V.tensor_tensor(sq[:, 0:half, :], src[:, 0:half, :], src[:, half:2 * half, :], ALU.add).then_inc(ini["add"], 1)
                    dve.wait_ge(ini["add"], n0 + n + 1)

            dve.wait_ge(ini["trc"], 7)
            add_chunks(hT, 0)
            dve.wait_ge(ini["mu"], 1)
            for c in (0, 4):
                V.tensor_tensor(hT[:, c:c + 4, :], hT[:, c:c + 4, :], bc(mu, 4), ALU.subtract).then_inc(ini["cen"], 1)
            dve.wait_ge(ini["sq"], 2)
            add_chunks(sq, 3)
            dve.wait_ge(ini["cen"], 2)
            dve.wait_ge(ini["rs"], 2)
            for c in range(KD):
                V.scalar_tensor_tensor(hT[:, c, :], hT[:, c, :], lv[:, c:c + 1], rs, ALU.mult, ALU.mult).then_inc(ini["cen"], 1)

            with dve.Fori(0, LAYERS) as l:
                links = [0]

                def link(ins):
                    links[0] += 1
                    ins.then_inc(dve_link.sem, 1)
                    dve.wait_ge(dve_link.sem, dve_link.at(l, links[0]))

                def tr_in(name):
                    dve.wait_ge(tb.ready, tb.filled(l, name))
                    return tb.bank(name)

                def split_lo(t, halves=(0, 1)):
                    for a in halves:
                        dve.wait_ge(w_hi.sem, w_hi.at(l, 2 * split_no(t) + a + 1))
                        V.tensor_tensor(wlo[t % RING][:, 4 * a:4 * a + 4, :], wt[t % RING][:, 1024 * a:1024 * a + 1024].rearrange("p (k n) -> p k n", k=4),
                                        whi[split_no(t) % 2][:, 4 * a:4 * a + 4, :], ALU.subtract).then_inc(w_lo.sem, 1)

                for a in range(2):
                    dve.wait_ge(x_hi_d.sem, x_hi_d.at(l, a + 1))
                    V.tensor_tensor(x_lo[:, 4 * a:4 * a + 4, :], hT[:, 4 * a:4 * a + 4, :], x_hi[:, 4 * a:4 * a + 4, :], ALU.subtract).then_inc(x_lo_d.sem, 1)
                for t in range(1, SPLIT_A):
                    split_lo(t)
                b = tr_in("vec")
                dve.wait_ge(h_ready.sem, h_ready.at(l, 8))
                V.tensor_copy(lv[:, :], b[:, 0:V_N]).then_inc(tb.done, 1)
                cos, sin = cst[:, C_COS:C_COS + NT], cst[:, C_SIN:C_SIN + NT]
                for i in range(6):
                    b = tr_in(f"rope{i}")
                    src, dst = (qT[:, i, :], qR[:, i, :]) if i < 4 else (kvT[:, 2 * (i - 3), :],) * 2
                    link(V.tensor_tensor(tmpA[:, :], b[:, 0:NT], sin, ALU.mult))
                    V.tensor_tensor(dst, src, cos, ALU.mult).then_inc(tb.done, 1)
                    dve.wait_ge(tb.done, tb.emptied(l, f"rope{i}"))
                    V.tensor_tensor(dst, dst, tmpA[:, :], ALU.add).then_inc(q_rot.sem, 1)
                    dve.wait_ge(q_rot.sem, q_rot.at(l, i + 1))
                dve.wait_ge(ini["zero"], 7)
                for r, q in enumerate((qT, qR)):
                    for g in range(2):
                        c0 = r * NS * 64 + 32 * g
                        dst = Qflat[64 * g:64 * g + 64, c0:c0 + NS * 68].rearrange("p (s x) -> p s x", s=NS)[:, :, 0:4]
                        ins = V.tensor_copy(dst, q[64 * g:64 * g + 64, :, SEQ:NT].rearrange("p c s -> p s c"))
                        if (r, g) == (1, 1):
                            ins.then_inc(s_qz.sem, 1)
                        else:
                            links[0] += 1
                            ins.then_inc(dve_link.sem, 1)
                dve.wait_ge(stored, l * (16 * STORES) + 16)
                def token_major(kind, dst):
                    for i in range(6):
                        b = tr_in(f"{kind}{i}")
                        g, a = i // 2, i % 2
                        m, n = TG[g][1], (256 if a else 512)
                        V.tensor_copy(dst[0:m, g, 512 * a:512 * a + n], b[0:m, 0:n]).then_inc(tb.done, 1)

                token_major("kvt", kvtok)
                for j in range(2):
                    for g in range(2):
                        for r in range(2):
                            ins = V.tensor_copy(cmpT[64 * r:64 * r + 64, j, g, NS, :], kvT[64 * g:64 * g + 64, j, r:SEQ:2])
                            if (j, g, r) == (1, 1, 1):
                                ins.then_inc(pairs.sem, 1)
                            else:
                                links[0] += 1
                                ins.then_inc(dve_link.sem, 1)
                def pe_product(j, half):
                    if half == 0:
                        slot, per, v = landed(T_CMP + j)
                        dve.wait_ge(slot, l * per + v)
                    w = wt[(T_CMP + j) % RING]
                    for lp in range(8 * half, 8 * half + 8):
                        wk, pe_ = w[:, 128 * lp:128 * lp + 128], lv[:, V_PEK + 16 * j + lp:V_PEK + 16 * j + lp + 1]
                        if lp == 0:
                            link(V.tensor_scalar(pacc[:, j, :], wk, pe_, None, ALU.mult))
                        elif lp < 15:
                            link(V.scalar_tensor_tensor(pacc[:, j, :], wk, pe_, pacc[:, j, :], ALU.mult, ALU.add))
                        else:
                            V.scalar_tensor_tensor(pacc[:, j, :], wk, pe_, pacc[:, j, :], ALU.mult, ALU.add).then_inc(pe_sum.sem, 1)

                for s in range(NS):
                    b = tr_in(f"pairs{s}")
                    for g in range(2):
                        for r in range(2):
                            ins = V.tensor_copy(cmpT[64 * r:64 * r + 64, :, g, s, :],
                                                b[64 * g:64 * g + 64, :].rearrange("p (j r i) -> p j r i", j=2, r=2)[:, :, r, :])
                            if g + r < 2:
                                links[0] += 1
                                ins.then_inc(dve_link.sem, 1)
                            else:
                                ins.then_inc(tb.done, 1)
                    b = tr_in(f"keys{s}")
                    if s >= 2:
                        dve.wait_ge(s_keys.sem, s_keys.at(l, s - 1))
                    link(V.tensor_copy(kTs[:, s % 2, :, PAST:NKEY], kvT[:, 2:6:2, SEQ + s:SEQ + s + 1]))
                    V.tensor_copy(kTs[:, s % 2, :, 0:PAST], b[:, :].rearrange("p (r k) -> p r k", r=2)).then_inc(tb.done, 1)
                    if s >= 5:
                        pe_product((s - 5) // 2, (s - 5) % 2)
                for br in range(2):
                    dve.wait_ge(sc.ready, sc.filled(l, f"ssc{br}"))
                    link(V.tensor_reduce(s64[:, br:br + 1], sc.bank(f"ssc{br}")[0:64, 0:NKEY], AX, ALU.max))
                V.tensor_scalar(s64[:, 3:5], s64[:, 0:2], -SCALE, None, ALU.mult).then_inc(s_max.sem, 1)
                token_major("glt", gltok)
                pe_product(1, 1)
                b = tr_in("gate")
                for g, (c0, m) in enumerate(TG):
                    ins = V.tensor_copy(gates[0:m, g, :], b[0:m, 24 * g:24 * g + 24])
                    if g < 2:
                        link(ins)
                    else:
                        ins.then_inc(tb.done, 1)
                dve.wait_ge(gate_exp.sem, gate_exp.at(l, 1))
                link(V.tensor_scalar(gates[:, :, :], gates[:, :, :], 1.0, None, ALU.add))
                V.reciprocal(gates[:, :, :], gates[:, :, :]).then_inc(gate_sig.sem, 1)
                dve.wait_ge(acc.done, acc.emptied(l, "gr3"))
                dve.wait_ge(gre_sig.sem, gre_sig.at(l, 1))
                V.tensor_tensor(grT[:, :, :], grT[:, :, :], gre, ALU.mult).then_inc(gla_silu.sem, 1)
                for j in range(2):
                    dve.wait_ge(sc.done, sc.emptied(l, ("hidk", "hidv")[j]))
                    x = hx[:, j, :]
                    if j == 1:
                        dve.wait_ge(hid_g.sem, hid_g.at(l, 1))
                    link(V.tensor_tensor(hy, x, x, ALU.mult))
                    link(V.tensor_scalar(hy, hy, 0.044715, 1.0, ALU.mult, ALU.add))
                    link(V.tensor_tensor(hy, hy, x, ALU.mult))
                    V.tensor_scalar(hy, hy, -50.0, None, ALU.max).then_inc(hid_u.sem, 1)
                    dve.wait_ge(hid_e.sem, hid_e.at(l, j + 1))
                    link(V.tensor_scalar(hy, hy, 1.0, None, ALU.add))
                    link(V.reciprocal(hy, hy))
                    V.tensor_tensor(x, x, hy, ALU.mult).then_inc(hid_g.sem, 1)
                b = tr_in("kcmp")
                V.tensor_copy(kc[:, :], b[:, 0:135]).then_inc(tb.done, 1)
                for i in range(3):
                    b = tr_in(f"vcmp{i}")
                    n = min(4, 9 - 4 * i)
                    V.tensor_copy(vc[:, 4 * i:4 * i + n, :], b[0:NWIN, 0:128 * n].rearrange("p (s d) -> p s d", d=128)).then_inc(tb.done, 1)
                def heads(a, w):
                    return a[:, :, None].to_broadcast([128, 8, w])

                for t in range(2):
                    S = CS[:, t, :, :]
                    add = cst[:, C_CADD + 15 * t:C_CADD + 15 * t + 15][:, None, :].to_broadcast([128, 4, NWIN])
                    for g in range(GROUPS):
                        dve.wait_ge(sc.done, sc.emptied(l, f"csc{t}{g}"))
                        ins = V.tensor_tensor(S[:, 4 * g:4 * g + 4, :], S[:, 4 * g:4 * g + 4, :], add, ALU.add)
                        links[0] += 1
                        ins.then_inc(dve_link.sem, 1)
                    dve.wait_ge(dve_link.sem, dve_link.at(l, links[0]))
                    link(V.tensor_reduce(cst8[:, t, 0, :], S, AX, ALU.max))
                    V.tensor_tensor(S, S, heads(cst8[:, t, 0, :], NWIN), ALU.subtract).then_inc(c_shift.sem, 1)
                for t in range(2):
                    S = CS[:, t, :, :]
                    dve.wait_ge(c_exp.sem, c_exp.at(l, t + 1))
                    live = cst[:, C_C01 + 15 * t:C_C01 + 15 * t + 15][:, None, :].to_broadcast([128, 8, NWIN])
                    link(V.tensor_tensor(S, S, live, ALU.mult))
                    link(V.tensor_reduce(cst8[:, t, 1, :], S, AX, ALU.add))
                    link(V.tensor_scalar(cst8[:, t, 1, :], cst8[:, t, 1, :], 1e-30, None, ALU.max))
                    link(V.reciprocal(cst8[:, t, 1, :], cst8[:, t, 1, :]))
                    link(V.tensor_tensor(cst8[:, t, 2, :], cst8[:, t, 1, :], gates[:, t, 0:24:3], ALU.mult))
                    V.tensor_tensor(S, S, heads(cst8[:, t, 2, :], NWIN), ALU.mult).then_inc(c_prob.sem, 1)
                dve.wait_ge(sc.ready, sc.filled(l, "ssc2"))
                link(V.tensor_reduce(s64[:, 2:3], sc.bank("ssc2")[0:64, 0:NWIN], AX, ALU.max))
                V.tensor_scalar(s64[:, 5:6], s64[:, 2:3], -SCALE, None, ALU.mult).then_inc(s_cmax.sem, 1)

                def unit_max(u):
                    t = u // 8
                    dve.wait_ge(sc.ready, sc.filled(l, f"sc{u}"))
                    b = sc.bank(f"sc{u}")[:, :].rearrange("p (r k) -> p r k", r=2)
                    diag = b[:, :, 128 * t:128 * t + 128]
                    mask = cst[:, C_CAUS:C_CAUS + 128][:, None, :].to_broadcast([128, 2, 128])
                    link(V.tensor_tensor(diag, diag, mask, ALU.add))
                    link(V.tensor_reduce(st[:, u % 2, 0:2], b[:, :, 0:128 * (t + 1)], AX, ALU.max))
                    V.tensor_scalar(st[:, u % 2, 2:4], st[:, u % 2, 0:2], -SCALE, None, ALU.mult).then_inc(u_max.sem, 1)

                def unit_prob(u):
                    t, c, g = u // 8, (u % 8) // 2, u % 2
                    n, h = 128 * (t + 1), 4 * g + c
                    dve.wait_ge(u_half.sem, u_half.at(l, u + 1))
                    dve.wait_ge(sc.done, sc.emptied(l, f"sc{u}"))
                    link(V.reciprocal(st[:, u % 2, 4:6], st[:, u % 2, 4:6]))
                    link(V.tensor_tensor(st[:, u % 2, 6:8], st[:, u % 2, 4:6], gates[:, t, 3 * h + 1:3 * h + 3], ALU.mult))
                    link(V.tensor_scalar(PS[:, u % 2, 0, 0:n], PS[:, u % 2, 0, 0:n], st[:, u % 2, 6:7], None, ALU.mult))
                    V.tensor_scalar(PS[:, u % 2, 1, 0:n], PS[:, u % 2, 1, 0:n], st[:, u % 2, 7:8], None, ALU.mult).then_inc(u_prob.sem, 1)

                def compressed_in(t):
                    if t == 1:
                        dve.wait_ge(ob.ready, ob.filled(l, "o3"))
                    for a in range(2):
                        b = tr_in(f"pc{t}{a}")
                        V.tensor_copy(PTc[:, 4 * a:4 * a + 4, :], b[0:NWIN, :].rearrange("p (h q) -> p h q", h=4)).then_inc(tb.done, 1)

                def prob_in(u):
                    b = tr_in(f"pt{u}")
                    n = 256 * (u // 8 + 1)
                    if u >= 2 and u % 2 == 0:
                        dve.wait_ge(pv_done.sem, pv_done.at(l, u // 2))
                    elif u >= 3:
                        dve.wait_ge(ob.ready, ob.filled(l, f"o{(u - 2) // 2}"))
                    V.tensor_copy(PT[:, u % 2, 0:n // 128, :], b[:, 0:n].rearrange("p (a q) -> p a q", q=128)).then_inc(tb.done, 1)

                def sample_probs():
                    dve.wait_ge(sc.done, sc.emptied(l, "ssc2"))
                    dve.wait_ge(gate_in.sem, gate_in.at(l, 32))
                    link(V.reciprocal(s64[:, 6:9], s64[:, 6:9]))
                    link(V.tensor_tensor(s64[:, 9:10], s64[:, 8:9], gate64[:, 0:1], ALU.mult))
                    link(V.tensor_tensor(s64[:, 10:12], s64[:, 6:8], gate64[:, 1:3], ALU.mult))
                    link(V.tensor_scalar(C64[:, :], C64[:, :], s64[:, 9:10], None, ALU.mult))
                    link(V.tensor_scalar(P64[:, 0, :], P64[:, 0, :], s64[:, 10:11], None, ALU.mult))
                    V.tensor_scalar(P64[:, 1, :], P64[:, 1, :], s64[:, 11:12], None, ALU.mult).then_inc(s_prob.sem, 1)
                    dve.wait_ge(s_prob.sem, s_prob.at(l, 1))
                    link(V.tensor_scalar(An[:, 0, :], cst[0:64, C_M8:C_M8 + 8], P64[:, 0, PAST:NKEY], None, ALU.mult))
                    V.tensor_scalar(An[:, 1, :], cst[0:64, C_M8:C_M8 + 8], P64[:, 1, PAST:NKEY], None, ALU.mult).then_inc(s_anew.sem, 1)

                def sample_probs_in():
                    b = tr_in("spt")
                    link(V.tensor_copy(PTs[:, :, :], b[:, 0:256].rearrange("p (n r) -> p n r", n=4)))
                    V.tensor_copy(PTcs[:, :], b[0:NWIN, 256:320]).then_inc(tb.done, 1)
                    b = tr_in("snew")
                    V.tensor_copy(Pn[:, :, :], b[0:8, 0:128].rearrange("p (r n) -> p r n", r=2)).then_inc(tb.done, 1)

                def log_decays_in():
                    b = tr_in("la01")
                    V.tensor_copy(xla[:, 0:2, :], b[:, :].rearrange("p (g n) -> p g n", g=2)).then_inc(tb.done, 1)
                    b = tr_in("la2")
                    V.tensor_copy(xla[0:NS, 2, :], b[0:NS, 0:256]).then_inc(tb.done, 1)

                def log_decays():
                    dve.wait_ge(la_e.sem, la_e.at(l, 1))
                    V.scalar_tensor_tensor(xla[:, :, :], xla[:, :, :], 0.0, lla, ALU.min, ALU.subtract).then_inc(la_t.sem, 1)

                def sample_key(s):
                    if s >= 2:
                        dve.wait_ge(tb.ready, tb.filled(l, f"SU{s - 2}"))
                    V.tensor_scalar(kz[:, s % 2, :], gltok[0:NS, 2, 0:256], cst[0:NS, C_KD + s:C_KD + s + 1], None, ALU.mult).then_inc(kz_d.sem, 1)

                def state(t, ch):
                    k = 2 * t + ch
                    b = tr_in(f"U{t}{ch}")
                    if k >= 2:
                        dve.wait_ge(ob.ready, ob.filled(l, f"go{(k - 1) // 2}1"))
                    for hp in range(2):
                        for h2 in range(2):
                            new = Sp[64 * h2:64 * h2 + 64, k % 2, hp, :]
                            upd = b[64 * h2:64 * h2 + 64, 256 * hp + 128 * h2:256 * hp + 128 * h2 + 128]
                            if k == 0:
                                ins = V.tensor_copy(new, upd)
                            else:
                                ins = V.scalar_tensor_tensor(new, Sp[64 * h2:64 * h2 + 64, (k - 1) % 2, hp, :],
                                                             EB[64 * h2:64 * h2 + 64, 0, hp, 64 * ch + 63:64 * ch + 64], upd, ALU.mult, ALU.add)
                            if hp + h2 < 2:
                                link(ins)
                            else:
                                ins.then_inc(tb.done, 1)
                    dve.wait_ge(tb.done, tb.emptied(l, f"U{t}{ch}"))
                    V.tensor_copy(st[:, 0, 0:1], Sp[:, k % 2, 0, 0:1]).then_inc(g_state.sem, 1)

                def decays_in(t):
                    b = tr_in(f"aft{t}")
                    V.tensor_copy(kd, b[:, 0:256]).then_inc(tb.done, 1)

                def gla_factors(t):
                    dve.wait_ge(sc.done, sc.emptied(l, f"gB{t}"))
                    q, k = glT[:, 0:2, 128 * t:128 * t + 128], glT[:, 2:4, 128 * t:128 * t + 128]
                    if t == 1:
                        dve.wait_ge(ob.ready, ob.filled(l, "go01"))
                    link(V.scalar_tensor_tensor(qe, q, DK ** -0.5, EB[:, 0, :, :], ALU.mult, ALU.mult))
                    link(V.scalar_tensor_tensor(qm, q, DK ** -0.5, EB[:, 1, :, :], ALU.mult, ALU.mult))
                    link(V.tensor_tensor(km, k, EB[:, 2, :, :], ALU.mult))
                    dve.wait_ge(g_ea.sem, g_ea.at(l, t + 1))
                    V.tensor_tensor(kd, kd, gltok[:, t, 0:256], ALU.mult).then_inc(g_q.sem, 1)

                def gla_scores_in(t):
                    for h2 in range(2):
                        b = tr_in(f"gA{t}{h2}")
                        V.tensor_tensor(gAs[:, h2:4:2, :], b[:, 0:256].rearrange("p (h t) -> p h t", h=2),
                                        cst[:, C_GM:C_GM + 128][:, None, :].to_broadcast([128, 2, 128]), ALU.mult).then_inc(tb.done, 1)

                def sample_state(s):
                    if s == 0:
                        dve.wait_ge(state_in.sem, state_in.at(l, 64))
                        dve.wait_ge(ela_d.sem, ela_d.at(l, 1))
                    b = tr_in(f"SU{s}")
                    for hp in range(2):
                        for h2 in range(2):
                            S = Sst[64 * h2:64 * h2 + 64, s, hp, :]
                            upd = b[64 * h2:64 * h2 + 64, 256 * hp + 128 * h2:256 * hp + 128 * h2 + 128]
                            ins = V.scalar_tensor_tensor(S, S, ela[64 * h2:64 * h2 + 64, hp, s:s + 1], upd, ALU.mult, ALU.add)
                            if hp + h2 < 2:
                                links[0] += 1
                                ins.then_inc(dve_link.sem, 1)
                            else:
                                ins.then_inc(tb.done, 1)
                    dve.wait_ge(tb.done, tb.emptied(l, f"SU{s}"))
                    V.tensor_copy(st[:, 0, 0:1], Sst[:, s, 0, 0:1]).then_inc(s_state.sem, 1)

                def head_norm(i):
                    c0, m = TG[i]
                    dve.wait_ge(ob.done, ob.emptied(l, f"go{i}1" if i < 2 else "gos"))
                    dve.wait_ge(r_rs.sem, r_rs.at(l, i + 1))
                    o = ogT[:, :, c0:c0 + m]
                    r = rr[:, 0:4 * m].rearrange("p (h t) -> p h t", h=4)
                    link(V.tensor_tensor(o, o, r, ALU.mult))
                    V.scalar_tensor_tensor(o, o, lv[:, V_GN:V_GN + 1], grT[:, :, c0:c0 + m], ALU.mult, ALU.mult).then_inc(og_d.sem, 1)

                def for_up_lo(a):
                    dve.wait_ge(u_hi_d.sem, u_hi_d.at(l, a + 1))
                    V.tensor_tensor(u_lo[:, 4 * a:4 * a + 4, :], (onT, ogT)[a][:, :, :], u_hi[:, 4 * a:4 * a + 4, :], ALU.subtract).then_inc(u_lo_d.sem, 1)

                for k in range(18):
                    if k == 2:
                        compressed_in(0)
                    if k >= 2:
                        prob_in(k - 2)
                    if k == 10:
                        compressed_in(1)
                    if 1 <= k <= 16:
                        unit_prob(k - 1)
                    if k < 16:
                        unit_max(k)
                    if k == 1:
                        log_decays_in()
                        sample_probs()
                    elif k == 2:
                        sample_probs_in()
                        log_decays()
                    elif k == 3:
                        b = tr_in("elas")
                        V.tensor_copy(ela[:, :, :], b[:, 0:16].rearrange("p (h s) -> p h s", h=2)).then_inc(tb.done, 1)
                        decays_in(0)
                    elif k == 4:
                        gla_factors(0)
                    elif k == 5:
                        gla_scores_in(0)
                        sample_key(0)
                        sample_key(1)
                    elif k == 6:
                        state(0, 0)
                        state(0, 1)
                    elif k == 9:
                        decays_in(1)
                    elif k == 10:
                        gla_factors(1)
                        for h2 in range(2):
                            q = glT[64 * h2:64 * h2 + 64, 0:2, SEQ:NT]
                            ins = V.tensor_scalar(qsz[64 * h2:64 * h2 + 64, :, :, h2], q, DK ** -0.5, None, ALU.mult)
                            if h2 == 0:
                                link(ins)
                            else:
                                ins.then_inc(qs_d.sem, 1)
                    elif k == 11:
                        gla_scores_in(1)
                        head_norm(0)
                    elif k == 12:
                        state(1, 0)
                    elif k == 14:
                        state(1, 1)
                    elif k == 16:
                        head_norm(1)
                    if k - 1 in updates_at:
                        for s in updates_at[k - 1]:
                            sample_state(s)
                            if s + 2 < NS:
                                sample_key(s + 2)
                split_lo(T_UP + 1)
                for_up_lo(0)
                head_norm(2)
                dve.wait_ge(og_d.sem, og_d.at(l, 3))
                V.tensor_copy(st[:, 0, 0:1], ogT[:, 0, 0:1]).then_inc(mixers_done.sem, 1)
                dve.wait_ge(mg_sig.sem, mg_sig.at(l, 16))
                def merged_lo(i):
                    dve.wait_ge(m_hi_d.sem, m_hi_d.at(l, i + 1))
                    V.tensor_tensor(m_lo[:, i, :], mgT[:, i, :], m_hi[:, i, :], ALU.subtract).then_inc(m_lo_d.sem, 1)

                for_up_lo(1)
                for i in range(8):
                    for a in range(2):
                        dve.wait_ge(acc.done, acc.emptied(l, f"up{2 * i + a}"))
                        m = mgT[:, 8 * a + i, :]
                        link(V.tensor_tensor(m, m, upb[:, a, :], ALU.mult))
                    V.tensor_tensor(mgT[:, i, :], mgT[:, i, :], mgT[:, 8 + i, :], ALU.add).then_inc(up_m.sem, 1)
                    if i >= 1:
                        merged_lo(i - 1)
                    if i >= 1:
                        split_lo(T_UP + (i - 1) // 2 + 2, ((i - 1) % 2,))
                merged_lo(7)
                split_lo(T_UP + 5, (1,))

                def residual(name, res, i):
                    dve.wait_ge(acc.done, acc.emptied(l, f"{name}{i}"))
                    V.scalar_tensor_tensor(hT[:, i, :], hT[:, i, :], ALPHA, yb[:, i % 2, :], ALU.mult, ALU.add).then_inc(res.sem, 1)

                def norm(i, vg, res):
                    dve.wait_ge(sc.done, sc.emptied(l, f"ln{i + 1}m"))
                    dve.wait_ge(res.sem, res.at(l, 8))
                    link(V.tensor_tensor(musq, mu, mu, ALU.mult))
                    dve.wait_ge(sc.done, sc.emptied(l, f"ln{i + 1}v"))
                    link(V.tensor_tensor(rs, rs, musq, ALU.subtract))
                    V.tensor_scalar(rs, rs, 0.0, None, ALU.max).then_inc(ln_var.sem, 1)
                    for c in range(KD + 2):
                        if c in (0, 4):
                            link(V.tensor_tensor(hT[:, c:c + 4, :], hT[:, c:c + 4, :], bc(mu, 4), ALU.subtract))
                        if c == 0:
                            dve.wait_ge(ln_rs.sem, ln_rs.at(l, i + 1))
                        if c < KD:
                            V.scalar_tensor_tensor(hT[:, c, :], hT[:, c, :], lv[:, vg + c:vg + c + 1], rs, ALU.mult, ALU.mult).then_inc(ln_sc.sem, 1)
                        if i == 0 and c >= 2:
                            dve.wait_ge(h_hi_d.sem, h_hi_d.at(l, c - 1))
                            V.tensor_tensor(h_lo[:, c - 2, :], hT[:, c - 2, :], h_hi[:, c - 2, :], ALU.subtract).then_inc(h_lo_d.sem, 1)

                for i in range(8):
                    residual("out", res1, i)
                    if i % 2 == 1 and i < 7:
                        split_lo(T_OUT + i // 2 + 2)
                split_lo(T_M1 + 1)
                norm(0, V_L1G, res1)
                for i in range(32):
                    dve.wait_ge(hid_hi_d.sem, hid_hi_d.at(l, i + 1))
                    link(V.tensor_tensor(yb[:, i % 2, :], yb[:, i % 2, :], yb[:, i % 2, :], ALU.mult))
                    if i == 8:
                        dve.wait_ge(stored, l * (16 * STORES) + 16 * STORES + 16)
                    V.tensor_tensor(hid_lo[:, i, :], yb[:, i % 2, :], hid_hi[:, i, :], ALU.subtract).then_inc(hid_lo_d.sem, 1)
                    if i % 2 == 1:
                        split_lo(T_M1 + i // 2 + 2)
                for t in range(16):
                    if t % 4 == 3:
                        for i in range(t // 2 - 1, t // 2 + 1):
                            residual("m2_", res2, i)
                    if t < 14:
                        split_lo(T_M2 + t + 2)
                norm(1, V_L2G, res2)
                assert links[0] == dve_link.per, links[0]

            for n in range(6):
                g, half = n // 2, n % 2
                m = TG[g][1]
                dve.wait_ge(ini["tr"], 8 + n)
                V.tensor_copy(xin[0:m, g, 512 * half:512 * half + 512], tb.banks[n % 2][0:m, :]).then_inc(ini["trc"], 1)


INS = ["x_prompt", "x_sample", "cache_nsa_kv", "cache_win_kv", "state_gla", "page_table", "ln_in_g", "ln_in_b", "w_in",
       "cmp_k_pe", "cmp_k_w1", "cmp_k_w2", "cmp_v_pe", "cmp_v_w1", "cmp_v_w2", "gla_w_a2", "gla_b_a", "gla_norm_g",
       "w_nsa_up", "w_gla_up", "w_out", "ln1_g", "ln1_b", "mlp_w1", "mlp_w2", "ln2_g", "ln2_b"]
OUTS = [("y_prompt", (1, SEQ, D)), ("y_sample", (NS, 1, D)), ("nsa_kv_prompt", (1, LAYERS, SEQ, 4, GROUPS, HD)),
        ("win_kv_prompt", (1, LAYERS, SEQ, 2, GROUPS, HD)), ("gla_state_prompt", (1, LAYERS, GH, DK, DV)),
        ("nsa_kv_sample", (NS, LAYERS, 1, 4, GROUPS, HD)), ("win_kv_sample", (NS, LAYERS, PAST, 2, GROUPS, HD)),
        ("gla_state_sample", (NS, LAYERS, GH, DK, DV))]


def constants(np):
    c = np.zeros((128, C_N), np.float32)
    i = np.arange(128)
    c[:, C_ID:C_ID + 128] = np.eye(128)
    c[:, C_ONE:C_ONE + 128] = 1.0
    for m in range(128):
        c[m + 32 if m % 64 < 32 else m - 32, C_ROT + m] = -1.0 if m % 64 < 32 else 1.0
    c[:, C_CAUS:C_CAUS + 128] = np.where(i[None, :] <= i[:, None], 0.0, NEG)
    same = i[:, None] // CH == i[None, :] // CH
    u, t = i[:, None], i[None, :]
    mid = t // CH * CH + CH // 2 - 1
    c[:, C_TRI:C_TRI + 128] = same * (u <= t) / TAU
    c[:, C_MID:C_MID + 128] = same * ((u <= t).astype(np.float32) - (u <= mid)) / TAU
    c[:, C_AFT:C_AFT + 128] = same * (u > t) / TAU
    c[:, C_GM:C_GM + 128] = same * (u <= t)
    half = HD // 2
    inv = np.float32(10000.0) ** (-np.arange(half, dtype=np.float32) / np.float32(half))
    pos = np.concatenate([np.arange(SEQ), np.full(NS, PAST)]).astype(np.float32)
    ang = (pos[None, :] * inv[i % half][:, None]).astype(np.float32)
    c[:, C_COS:C_COS + NT] = np.cos(ang)
    c[:, C_SIN:C_SIN + NT] = np.sin(ang)
    for tile in range(2):
        live = (np.arange(NWIN) * CSTR + CLEN - 1)[None, :] <= (tile * 128 + i)[:, None]
        c[:, C_CADD + 15 * tile:C_CADD + 15 * tile + 15] = np.where(live, 0.0, NEG)
        c[:, C_C01 + 15 * tile:C_C01 + 15 * tile + 15] = live
    for r in range(64):
        c[r, C_M8 + (r % 32) // 4] = 1.0
    for s in range(NS):
        c[s, C_KD + s] = 1.0
    c[:, C_EPS] = EPS
    return c


def kernel(**inputs):
    import numpy as np
    import concourse.bacc as bacc
    from concourse.bass_utils import run_bass_kernel_spmd

    nc = bacc.Bacc("TRN2", target_bir_lowering=False, num_devices=1)
    arrays = {f"in_{n}": np.ascontiguousarray(inputs[n]) for n in INS}
    arrays["in_consts"] = constants(np)
    A = {n[3:]: nc.dram_tensor(n, a.shape, mybir.dt.from_np(a.dtype), kind="ExternalInput").ap() for n, a in arrays.items()}
    O = {n: nc.dram_tensor(f"out_{n}", s, F32, kind="ExternalOutput").ap() for n, s in OUTS}
    build(nc, A, O)
    r = run_bass_kernel_spmd(nc, [arrays], core_ids=[0])
    return tuple(r.results[0][f"out_{n}"] for n, _ in OUTS)
```
